# Optimizing a Trainium2 kernel written in Bass

```python
import jax, jax.numpy as jnp
from jax import lax
import numpy as np

D_MODEL = 1024
BATCH = 1
SEQ = 256
DEPTH = 1

HEAD_DIM = 64
GRID_W = 64
NA_HEADS = 8
NA_KH_MAX = 8
NA_KW = 16
NA_QCB = NA_KW
NA_SPAN = 2 * NA_KW
SW_HEADS = 8
SW_KV_HEADS = 2
SW_WINDOW = 128
SW_BLOCK = 128
T5_BUCKETS = 32
T5_MAX_DIST = 128
FFN_HIDDEN = -(-8 * D_MODEL // (3 * 256)) * 256

A_W = NA_HEADS * HEAD_DIM
B_QW = SW_HEADS * HEAD_DIM
B_KVW = SW_KV_HEADS * HEAD_DIM
IN_WIDTHS = [A_W, A_W, A_W, B_QW, B_KVW, B_KVW, D_MODEL, D_MODEL]
IN_WIDTH = sum(IN_WIDTHS)
IN_SPLITS = list(np.cumsum(IN_WIDTHS)[:-1])
RMS_EPS = 1e-6
NEG_INF = -1e30


def rms_norm(x, g):
    xf = x.astype(jnp.float32)
    y = xf * lax.rsqrt(jnp.mean(xf * xf, axis=-1, keepdims=True) + RMS_EPS)
    return y.astype(x.dtype) * g

def t5_bucket(rel):
    half = T5_BUCKETS // 2
    max_exact = half // 2
    ret = (rel > 0).astype(np.int32) * half
    n = np.abs(rel)
    large = max_exact + (np.log(np.maximum(n, 1) / max_exact)
                         / np.log(T5_MAX_DIST / max_exact) * (half - max_exact)).astype(np.int32)
    large = np.minimum(large, half - 1)
    return ret + np.where(n < max_exact, n, large)

def neighbourhood_attention(q, k, v, rpb):
    B, T, H, D = q.shape
    rows = T // GRID_W
    kh = min(NA_KH_MAX, rows)
    ncb = GRID_W // NA_QCB
    r = np.arange(rows)
    row_start = np.clip(r - kh // 2, 0, rows - kh)
    key_rows = row_start[:, None] + np.arange(kh)[None, :]
    j = np.arange(ncb)
    span_start = np.clip(j * NA_QCB - NA_KW // 2, 0, GRID_W - NA_SPAN)
    key_cols = span_start[:, None] + np.arange(NA_SPAN)[None, :]
    q_cols = j[:, None] * NA_QCB + np.arange(NA_QCB)[None, :]
    win_start = np.clip(q_cols - NA_KW // 2, 0, GRID_W - NA_KW)
    kc = key_cols[:, None, :]
    in_win = (kc >= win_start[..., None]) & (kc < win_start[..., None] + NA_KW)

    idx = (key_rows[:, None, :, None] * GRID_W + key_cols[None, :, None, :]).reshape(rows, ncb, kh * NA_SPAN)
    kg = jnp.take(k, idx, axis=1)
    vg = jnp.take(v, idx, axis=1)
    qb = q.reshape(B, rows, ncb, NA_QCB, H, D)
    s = jnp.einsum('brjqhd,brjkhd->brjhqk', qb, kg,
                   preferred_element_type=jnp.float32) * (HEAD_DIM ** -0.5)

    dr = key_rows - r[:, None] + (NA_KH_MAX - 1)
    dc = np.clip(kc - q_cols[..., None], -(NA_KW - 1), NA_KW - 1) + (NA_KW - 1)
    bias = rpb[dr[:, None, None, :, None], dc[None, :, :, None, :]]
    bias = jnp.transpose(bias, (0, 1, 5, 2, 3, 4)).astype(jnp.float32)
    bias = jnp.where(in_win[None, :, None, :, None, :], bias, NEG_INF)
    bias = bias.reshape(rows, ncb, H, NA_QCB, kh * NA_SPAN)
    p = jax.nn.softmax(s + bias[None], axis=-1)
    o = jnp.einsum('brjhqk,brjkhd->brjqhd', p.astype(v.dtype), vg)
    return o.reshape(B, T, H, D)

def sliding_window_attention(q, k, v, sink, t5_table):
    B, T, H, D = q.shape
    kvh = k.shape[2]
    g = H // kvh
    nb = T // SW_BLOCK
    pad = ((0, 0), (SW_BLOCK, SW_BLOCK), (0, 0), (0, 0))
    kp = jnp.pad(k, pad).reshape(B, nb + 2, SW_BLOCK, kvh, D)
    vp = jnp.pad(v, pad).reshape(B, nb + 2, SW_BLOCK, kvh, D)
    kw = jnp.concatenate([kp[:, :-2], kp[:, 1:-1], kp[:, 2:]], axis=2)
    vw = jnp.concatenate([vp[:, :-2], vp[:, 1:-1], vp[:, 2:]], axis=2)
    qb = q.reshape(B, nb, SW_BLOCK, kvh, g, D)
    s = jnp.einsum('bnqkgd,bnskd->bnkgqs', qb, kw,
                   preferred_element_type=jnp.float32) * (HEAD_DIM ** -0.5)

    rel = np.arange(3 * SW_BLOCK)[None, :] - SW_BLOCK - np.arange(SW_BLOCK)[:, None]
    bias = t5_table[t5_bucket(rel)]
    bias = jnp.transpose(bias, (2, 0, 1)).reshape(kvh, g, SW_BLOCK, 3 * SW_BLOCK).astype(jnp.float32)
    key_pos = np.arange(nb)[:, None] * SW_BLOCK + np.arange(3 * SW_BLOCK)[None, :] - SW_BLOCK
    valid = (np.abs(rel) <= SW_WINDOW)[None] & ((key_pos >= 0) & (key_pos < T))[:, None, :]
    s = jnp.where(valid[None, :, None, None], s + bias[None, None], NEG_INF)

    sk = sink.astype(jnp.float32).reshape(1, 1, kvh, g, 1, 1)
    m = jnp.maximum(jnp.max(s, axis=-1, keepdims=True), sk)
    e = jnp.exp(s - m)
    p = e / (jnp.sum(e, axis=-1, keepdims=True) + jnp.exp(sk - m))
    o = jnp.einsum('bnkgqs,bnskd->bnqkgd', p.astype(v.dtype), vw)
    return o.reshape(B, T, H, D)

def first_inputs(seed: int = 0) -> dict:
    key = jax.random.key(seed)
    ks = jax.random.split(key, 18)
    f32 = jnp.float32

    def w(k, shape, fan_in):
        return jax.random.normal(k, shape, f32) * fan_in ** -0.5

    def gain(k, shape):
        return 1.0 + 0.05 * jax.random.normal(k, shape, f32)

    return {
        "x": jax.random.normal(ks[0], (BATCH, SEQ, D_MODEL), f32),
        "norm_mix": gain(ks[1], (DEPTH, D_MODEL)),
        "w_in": w(ks[2], (DEPTH, D_MODEL, IN_WIDTH), D_MODEL),
        "q_norm_a": gain(ks[3], (DEPTH, HEAD_DIM)),
        "k_norm_a": gain(ks[4], (DEPTH, HEAD_DIM)),
        "rpb_a": 0.1 * jax.random.normal(ks[5], (DEPTH, 2 * NA_KH_MAX - 1, 2 * NA_KW - 1, NA_HEADS), f32),
        "q_norm_b": gain(ks[6], (DEPTH, HEAD_DIM)),
        "k_norm_b": gain(ks[7], (DEPTH, HEAD_DIM)),
        "sink_b": 1.0 + 0.5 * jax.random.normal(ks[8], (DEPTH, SW_HEADS), f32),
        "t5_table": 0.1 * jax.random.normal(ks[9], (T5_BUCKETS, SW_HEADS), f32),
        "w_branch_a": w(ks[10], (DEPTH, A_W, D_MODEL), A_W),
        "w_branch_b": w(ks[11], (DEPTH, B_QW, D_MODEL), B_QW),
        "w_out": w(ks[12], (DEPTH, D_MODEL, D_MODEL), D_MODEL),
        "norm_ffn": gain(ks[13], (DEPTH, D_MODEL)),
        "w_gate": w(ks[14], (DEPTH, D_MODEL, FFN_HIDDEN), D_MODEL),
        "w_up": w(ks[15], (DEPTH, D_MODEL, FFN_HIDDEN), D_MODEL),
        "w_down": w(ks[16], (DEPTH, FFN_HIDDEN, D_MODEL), FFN_HIDDEN),
    }

def first_block(x, norm_mix, w_in, q_norm_a, k_norm_a, rpb_a, q_norm_b, k_norm_b, sink_b,
              t5_table, w_branch_a, w_branch_b, w_out, norm_ffn, w_gate, w_up, w_down):
    B, T, _ = x.shape
    for l in range(DEPTH):
        h = rms_norm(x, norm_mix[l])
        proj = jnp.einsum('btd,de->bte', h, w_in[l])
        q_a, k_a, v_a, q_b, k_b, v_b, g_a, g_b = jnp.split(proj, IN_SPLITS, axis=-1)

        q_a = rms_norm(q_a.reshape(B, T, NA_HEADS, HEAD_DIM), q_norm_a[l])
        k_a = rms_norm(k_a.reshape(B, T, NA_HEADS, HEAD_DIM), k_norm_a[l])
        v_a = v_a.reshape(B, T, NA_HEADS, HEAD_DIM)
        o_a = neighbourhood_attention(q_a, k_a, v_a, rpb_a[l]).reshape(B, T, A_W)

        q_b = rms_norm(q_b.reshape(B, T, SW_HEADS, HEAD_DIM), q_norm_b[l])
        k_b = rms_norm(k_b.reshape(B, T, SW_KV_HEADS, HEAD_DIM), k_norm_b[l])
        v_b = v_b.reshape(B, T, SW_KV_HEADS, HEAD_DIM)
        o_b = sliding_window_attention(q_b, k_b, v_b, sink_b[l], t5_table).reshape(B, T, B_QW)

        y = (jax.nn.sigmoid(g_a) * jnp.einsum('bte,ed->btd', o_a, w_branch_a[l])
             + jax.nn.sigmoid(g_b) * jnp.einsum('bte,ed->btd', o_b, w_branch_b[l]))
        x = x + jnp.einsum('btd,de->bte', y, w_out[l])

        h = rms_norm(x, norm_ffn[l])
        u = jax.nn.silu(jnp.einsum('btd,df->btf', h, w_gate[l])) * jnp.einsum('btd,df->btf', h, w_up[l])
        x = x + jnp.einsum('btf,fd->btd', u, w_down[l])
    return x


CHUNK = 64
MIX_WIDTH = D_MODEL
RET_WIDTH = MIX_WIDTH // 2
RWKV_WIDTH = MIX_WIDTH - RET_WIDTH
RET_HEADS = 4
RET_HEAD_DIM = RET_WIDTH // RET_HEADS
RWKV_HEAD_DIM = 64
RWKV_HEADS = RWKV_WIDTH // RWKV_HEAD_DIM
DECAY_LORA = 64
AAA_LORA = 64
GATE_LORA = 128
RWKV_COLS = 3 * RWKV_WIDTH + DECAY_LORA + AAA_LORA + GATE_LORA
IN_COLS = 4 * RET_WIDTH + RWKV_COLS
N_GROUPS = 4
EXPERTS_PER_GROUP = 8
N_EXPERTS = N_GROUPS * EXPERTS_PER_GROUP
TOP_K = 2
D_EXPERT = 512
MOE_BLOCK = 128
ROPE_BASE = 10000.0
NORM_EPS = 1e-6
RET_GN_EPS = 1e-5
RWKV_GN_EPS = 64e-5


def rms_norm_2(x, gain):
    xf = x.astype(jnp.float32)
    y = xf * lax.rsqrt(jnp.mean(xf * xf, axis=-1, keepdims=True) + NORM_EPS)
    return (y * gain.astype(jnp.float32)).astype(x.dtype)

def head_norm(y, gain, eps):
    mu = jnp.mean(y, axis=-1, keepdims=True)
    yc = y - mu
    var = jnp.mean(yc * yc, axis=-1, keepdims=True)
    return yc * lax.rsqrt(var + eps) * gain.astype(jnp.float32)

def rotary(x):
    S, d = x.shape[1], x.shape[-1]
    half = d // 2
    inv = ROPE_BASE ** (-jnp.arange(half, dtype=jnp.float32) / half)
    ang = jnp.arange(S, dtype=jnp.float32)[:, None] * inv[None, :]
    cos = jnp.cos(ang)[None, :, None, :]
    sin = jnp.sin(ang)[None, :, None, :]
    x1, x2 = x[..., :half], x[..., half:]
    return jnp.concatenate([x1 * cos - x2 * sin, x1 * sin + x2 * cos], axis=-1)

def retention(q, k, v):
    B, S, H, d = q.shape
    NC = S // CHUNK
    log_g = jnp.log(1.0 - jnp.exp2(-5.0 - jnp.arange(H, dtype=jnp.float32)))
    idx = jnp.arange(CHUNK, dtype=jnp.float32)
    intra_decay = jnp.exp(log_g[:, None, None] * jnp.abs(idx[:, None] - idx[None, :]))
    k_decay = jnp.exp(log_g[:, None] * (CHUNK - 1.0 - idx)[None, :])
    q_decay = jnp.exp(log_g[:, None] * (idx + 1.0)[None, :])
    chunk_decay = jnp.exp(log_g * CHUNK)
    qc = q.reshape(B, NC, CHUNK, H, d)
    kc = k.reshape(B, NC, CHUNK, H, d) * (d ** -0.5)
    vc = v.reshape(B, NC, CHUNK, H, d)
    scores = jnp.einsum('bnchd,bnmhd->bnhcm', qc, kc) * intra_decay[None, None]
    intra = jnp.einsum('bnhcm,bnmhe->bnche', scores, vc)
    kv = jnp.einsum('bnmhd,hm,bnmhe->bnhde', kc, k_decay, vc)

    def step(state, kv_n):
        return state * chunk_decay[None, :, None, None] + kv_n, state

    _, prev = lax.scan(step, jnp.zeros((B, H, d, d), jnp.float32), jnp.moveaxis(kv, 1, 0))
    prev = jnp.moveaxis(prev, 0, 1)
    cross = jnp.einsum('bnchd,hc,bnhde->bnche', qc, q_decay, prev)
    return (intra + cross).reshape(B, S, H, d)

def token_shift_lerp(feat, mu):
    prev = jnp.concatenate([jnp.zeros_like(feat[:, :1]), feat[:, :-1]], axis=1)
    return feat + (prev - feat) * mu

def rwkv7_time_mix(feats, mu, w0, w_up, a0, a_up, g_up, k_k, k_a, r_k, gn_gain):
    B, S, _ = feats.shape
    H, N, W = RWKV_HEADS, RWKV_HEAD_DIM, RWKV_WIDTH
    f = token_shift_lerp(feats.astype(jnp.float32), mu.astype(jnp.float32))
    r = f[..., 0:W]
    k = f[..., W:2 * W]
    v = f[..., 2 * W:3 * W]
    o = 3 * W
    w_lo = f[..., o:o + DECAY_LORA]
    a_lo = f[..., o + DECAY_LORA:o + DECAY_LORA + AAA_LORA]
    g_lo = f[..., o + DECAY_LORA + AAA_LORA:]
    w = -jax.nn.softplus(-(w0 + jnp.tanh(w_lo) @ w_up)) - 0.5
    decay = jnp.exp(-jnp.exp(w))
    a = jax.nn.sigmoid(a0 + a_lo @ a_up)
    g = jax.nn.sigmoid(g_lo) @ g_up
    kk = (k * k_k).reshape(B, S, H, N)
    kk = kk / jnp.maximum(jnp.sqrt(jnp.sum(kk * kk, axis=-1, keepdims=True)), 1e-12)
    k = k * (1.0 + (a - 1.0) * k_a)
    rh = r.reshape(B, S, H, N)
    kh = k.reshape(B, S, H, N)
    vh = v.reshape(B, S, H, N)
    ah = a.reshape(B, S, H, N)
    dh = decay.reshape(B, S, H, N)
    a_vec = -kk
    b_vec = kk * ah

    def step(state, inp):
        r_t, k_t, v_t, w_t, a_t, b_t = inp
        sa = jnp.einsum('bhvk,bhk->bhv', state, a_t)
        state = state * w_t[:, :, None, :] + sa[..., None] * b_t[:, :, None, :] + v_t[..., None] * k_t[:, :, None, :]
        return state, jnp.einsum('bhvk,bhk->bhv', state, r_t)

    xs = tuple(jnp.moveaxis(t, 1, 0) for t in (rh, kh, vh, dh, a_vec, b_vec))
    _, y = lax.scan(step, jnp.zeros((B, H, N, N), jnp.float32), xs)
    y = jnp.moveaxis(y, 0, 1)
    y = head_norm(y, gn_gain.reshape(H, N), RWKV_GN_EPS)
    bonus = jnp.sum(rh * kh * r_k[None, None].astype(jnp.float32), axis=-1, keepdims=True) * vh
    return (y + bonus).reshape(B, S, W) * g

def hier_moe(xn, w_route_group, b_route_group, w_route_expert, b_route_expert, w_gate, w_up, w_down):
    B, S, D = xn.shape
    T = B * S
    xt = xn.reshape(T, D)
    group_logits = (xt @ w_route_group).astype(jnp.float32) + b_route_group.astype(jnp.float32)
    group_prob = jax.nn.softmax(group_logits, axis=-1)
    g_idx = jnp.argmax(group_logits, axis=-1).astype(jnp.int32)
    g_p = jnp.take_along_axis(group_prob, g_idx[:, None], axis=1)
    exp_logits = ((xt @ w_route_expert).astype(jnp.float32) + b_route_expert.astype(jnp.float32)).reshape(T, N_GROUPS, EXPERTS_PER_GROUP)
    in_group = jnp.take_along_axis(exp_logits, g_idx[:, None, None], axis=1)[:, 0]
    top_v, top_i = lax.top_k(in_group, TOP_K)
    top_w = jax.nn.softmax(top_v, axis=-1) * g_p
    expert_id = (g_idx[:, None] * EXPERTS_PER_GROUP + top_i.astype(jnp.int32)).reshape(-1)
    token_id = jnp.repeat(jnp.arange(T, dtype=jnp.int32), TOP_K)
    weight = top_w.reshape(-1)
    A = T * TOP_K
    order = jnp.argsort(expert_id)
    se, st, sw = expert_id[order], token_id[order], weight[order]
    counts = jax.ops.segment_sum(jnp.ones((A,), jnp.int32), expert_id, num_segments=N_EXPERTS)
    starts = jnp.cumsum(counts) - counts
    padded = (counts + MOE_BLOCK - 1) // MOE_BLOCK * MOE_BLOCK
    pad_ends = jnp.cumsum(padded)
    pad_starts = pad_ends - padded
    dest = pad_starts[se] + jnp.arange(A, dtype=jnp.int32) - starts[se]
    P = ((A + MOE_BLOCK - 1) // MOE_BLOCK + N_EXPERTS) * MOE_BLOCK
    NB = P // MOE_BLOCK
    slot_tok = jnp.full((P,), T, jnp.int32).at[dest].set(st)
    slot_w = jnp.zeros((P,), jnp.float32).at[dest].set(sw)
    block_expert = jnp.clip(jnp.searchsorted(pad_ends, jnp.arange(NB, dtype=jnp.int32) * MOE_BLOCK, side='right'), 0, N_EXPERTS - 1)
    x_pad = jnp.concatenate([xt, jnp.zeros((1, D), xt.dtype)], axis=0)
    xb = x_pad[slot_tok].reshape(NB, MOE_BLOCK, D)

    def expert_block(args):
        xblk, e = args
        hdn = jax.nn.silu(xblk @ w_gate[e]) * (xblk @ w_up[e])
        return hdn @ w_down[e]

    yb = lax.map(expert_block, (xb, block_expert)).reshape(P, D)
    y = jax.ops.segment_sum(yb.astype(jnp.float32) * slot_w[:, None], slot_tok, num_segments=T + 1)[:T]
    return y.reshape(B, S, D).astype(xn.dtype)

def second_inputs(seed: int = 0) -> dict:
    key = jax.random.key(seed)
    ks = jax.random.split(key, 24)
    L, D = DEPTH, D_MODEL
    nrm = lambda k, shape, s: jax.random.normal(k, shape, jnp.float32) * s
    return {
        'x': nrm(ks[0], (BATCH, SEQ, D), 1.0),
        'norm1_gain': 1.0 + nrm(ks[1], (L, D), 0.02),
        'w_in': nrm(ks[2], (L, D, IN_COLS), D ** -0.5),
        'ret_gn_gain': 1.0 + nrm(ks[3], (L, RET_WIDTH), 0.02),
        'rwkv_mu': jax.random.uniform(ks[4], (L, RWKV_COLS), jnp.float32),
        'rwkv_w0': nrm(ks[5], (L, RWKV_WIDTH), 0.5) + 0.5,
        'rwkv_w_up': nrm(ks[6], (L, DECAY_LORA, RWKV_WIDTH), 0.5 * DECAY_LORA ** -0.5),
        'rwkv_a0': nrm(ks[7], (L, RWKV_WIDTH), 0.5),
        'rwkv_a_up': nrm(ks[8], (L, AAA_LORA, RWKV_WIDTH), 0.5 * AAA_LORA ** -0.5),
        'rwkv_g_up': nrm(ks[9], (L, GATE_LORA, RWKV_WIDTH), GATE_LORA ** -0.5),
        'rwkv_k_k': 0.85 + nrm(ks[10], (L, RWKV_WIDTH), 0.05),
        'rwkv_k_a': 1.0 + nrm(ks[11], (L, RWKV_WIDTH), 0.05),
        'rwkv_r_k': nrm(ks[12], (L, RWKV_HEADS, RWKV_HEAD_DIM), 0.1),
        'rwkv_gn_gain': 1.0 + nrm(ks[13], (L, RWKV_WIDTH), 0.02),
        'w_out': nrm(ks[14], (L, MIX_WIDTH, D), MIX_WIDTH ** -0.5),
        'norm2_gain': 1.0 + nrm(ks[15], (L, D), 0.02),
        'w_route_group': nrm(ks[16], (L, D, N_GROUPS), D ** -0.5),
        'b_route_group': nrm(ks[17], (L, N_GROUPS), 0.01),
        'w_route_expert': nrm(ks[18], (L, D, N_EXPERTS), D ** -0.5),
        'b_route_expert': nrm(ks[19], (L, N_EXPERTS), 0.01),
        'w_gate': nrm(ks[20], (L, N_EXPERTS, D, D_EXPERT), D ** -0.5),
        'w_up': nrm(ks[21], (L, N_EXPERTS, D, D_EXPERT), D ** -0.5),
        'w_down': nrm(ks[22], (L, N_EXPERTS, D_EXPERT, D), D_EXPERT ** -0.5),
        'final_norm_gain': 1.0 + nrm(ks[23], (D,), 0.02),
    }

def second_block(x, norm1_gain, w_in, ret_gn_gain, rwkv_mu, rwkv_w0, rwkv_w_up, rwkv_a0, rwkv_a_up, rwkv_g_up, rwkv_k_k, rwkv_k_a, rwkv_r_k, rwkv_gn_gain, w_out, norm2_gain, w_route_group, b_route_group, w_route_expert, b_route_expert, w_gate, w_up, w_down, final_norm_gain):
    B, S, _ = x.shape
    h = x
    for l in range(DEPTH):
        xn = rms_norm_2(h, norm1_gain[l])
        proj = xn @ w_in[l]
        rp = proj[..., :4 * RET_WIDTH].astype(jnp.float32)
        q = rotary(rp[..., 0:RET_WIDTH].reshape(B, S, RET_HEADS, RET_HEAD_DIM))
        k = rotary(rp[..., RET_WIDTH:2 * RET_WIDTH].reshape(B, S, RET_HEADS, RET_HEAD_DIM))
        v = rp[..., 2 * RET_WIDTH:3 * RET_WIDTH].reshape(B, S, RET_HEADS, RET_HEAD_DIM)
        ret = head_norm(retention(q, k, v), ret_gn_gain[l].reshape(RET_HEADS, RET_HEAD_DIM), RET_GN_EPS)
        ret = jax.nn.silu(rp[..., 3 * RET_WIDTH:]) * ret.reshape(B, S, RET_WIDTH)
        rw = rwkv7_time_mix(proj[..., 4 * RET_WIDTH:], rwkv_mu[l], rwkv_w0[l], rwkv_w_up[l], rwkv_a0[l], rwkv_a_up[l], rwkv_g_up[l], rwkv_k_k[l], rwkv_k_a[l], rwkv_r_k[l], rwkv_gn_gain[l])
        mixed = jnp.concatenate([ret, rw], axis=-1).astype(x.dtype)
        h = h + mixed @ w_out[l]
        h = h + hier_moe(rms_norm_2(h, norm2_gain[l]), w_route_group[l], b_route_group[l], w_route_expert[l], b_route_expert[l], w_gate[l], w_up[l], w_down[l])
    return rms_norm_2(h, final_norm_gain)


def setup_inputs(seed=0):
    out = dict(first_inputs(seed))
    for name, value in second_inputs(seed + 1).items():
        if name != "x":
            out[name + "_2"] = value
    return out


def reference(
    x, norm_mix, w_in, q_norm_a, k_norm_a, rpb_a, q_norm_b, k_norm_b, sink_b, t5_table,
    w_branch_a, w_branch_b, w_out, norm_ffn, w_gate, w_up, w_down, norm1_gain_2, w_in_2,
    ret_gn_gain_2, rwkv_mu_2, rwkv_w0_2, rwkv_w_up_2, rwkv_a0_2, rwkv_a_up_2, rwkv_g_up_2,
    rwkv_k_k_2, rwkv_k_a_2, rwkv_r_k_2, rwkv_gn_gain_2, w_out_2, norm2_gain_2, w_route_group_2,
    b_route_group_2, w_route_expert_2, b_route_expert_2, w_gate_2, w_up_2, w_down_2,
    final_norm_gain_2,
):
    x = first_block(
        x, norm_mix, w_in, q_norm_a, k_norm_a, rpb_a, q_norm_b, k_norm_b, sink_b, t5_table,
        w_branch_a, w_branch_b, w_out, norm_ffn, w_gate, w_up, w_down,
    )
    return second_block(
        x, norm1_gain_2, w_in_2, ret_gn_gain_2, rwkv_mu_2, rwkv_w0_2, rwkv_w_up_2, rwkv_a0_2,
        rwkv_a_up_2, rwkv_g_up_2, rwkv_k_k_2, rwkv_k_a_2, rwkv_r_k_2, rwkv_gn_gain_2, w_out_2,
        norm2_gain_2, w_route_group_2, b_route_group_2, w_route_expert_2, b_route_expert_2,
        w_gate_2, w_up_2, w_down_2, final_norm_gain_2,
    )


_drawn_inputs = setup_inputs


def setup_inputs(seed=0):
    import zlib

    import numpy as np

    out = dict(_drawn_inputs(seed))
    spreads = {}
    factors = {'q_norm_a': 3.502,
     'k_norm_a': 3.23,
     'q_norm_b': 4.144,
     'k_norm_b': 4.974,
     'sink_b': 6.514,
     't5_table': 3.097,
     'ret_gn_gain_2': 3.738,
     'rwkv_k_k_2': 3.939,
     'rwkv_gn_gain_2': 7.001,
     'norm2_gain_2': 2.877,
     'b_route_group_2': 8.0,
     'b_route_expert_2': 3.577,
     'final_norm_gain_2': 2.852}
    for name, (base, spread) in spreads.items():
        noise = np.random.default_rng([zlib.crc32(name.encode()), seed]).standard_normal(out[name].shape)
        drawn = base * np.exp(spread * noise) if base else spread * noise
        out[name] = __import__('jax').numpy.asarray(drawn.astype(out[name].dtype))
    for name, factor in factors.items():
        out[name] = (out[name] * factor).astype(out[name].dtype)
    return out
```

```python
from contextlib import ExitStack

import numpy as np

import concourse.bass as bass
from concourse import mybir

F32 = mybir.dt.float32
I32 = mybir.dt.int32
ALU = mybir.AluOpType
ACT = mybir.ActivationFunctionType
AX = mybir.AxisListType.X

P = 128
T = 256
NT = T // P
D = 1024
DK = D // P
HD = 64
GRID_W = 64
EPS = 1e-6
NEG = -1e30

A_W = 512
NQKV = 3 * A_W + 512 + 256
FFN = 2816
FFK = FFN // P
REL = 2 * T - 1
EXT = T + P
KW = 16
RET_H, RET_D = 4, 128
RW_H = 8
CH = 64
NCH = T // CH
DECAY = float(np.exp(-0.5))
FTC = 14
E = 32
EG = 4
CAP = 32
NG = E // EG
DE = 512
ROUNDS = T // CAP
QK_SUMS = ((192, 32), (224, 20))

SLOT = 4096
NSLOT = 3
QUAD = 2 * SLOT
NQ = 4
B0 = NSLOT * SLOT


def layout(*fields, base=0):
    at, out = base, {}
    for name, size in fields:
        out[name] = (at, at + size)
        at += size
    out["end"] = at
    return out


L1 = layout(("nat", NT * NQKV), ("sig", NT * 2048), ("biasA", 8 * 6 * 64), ("biasB", 8 * EXT),
            ("qaT", 1024), ("kaT", 1024), ("qbT", 1024), ("kbT", 512), ("prob", 2048), ("probT", 2048),
            ("kdup", 512), base=B0)
LM = layout(("M", 14 * 1024), ("fT", FTC * 257), ("RT", 2048), ("N", 4096), base=B0)
LE = layout(("xg", 1024), ("G", 256), ("Gw", 256), ("GT", 256), ("sg", 512), ("h", 512), ("hT", 512),
            ("d", 1024), base=NQ * QUAD)
ARENA = max(L1["end"], LM["end"], LE["end"])

CST = layout(("ident", 128), ("reset", T), ("winm", 64), ("wina", 64), ("slot", CAP), ("desc4", 4), ("desc32", 32),
             ("mAdT", 128), ("mAd", 128), ("m16T", 128), ("m32T", 128), ("mlt", 128), ("mle", 128),
             ("same", 128), ("sel", 2), ("before", 128), ("ones", 128), ("cos", 128), ("sin", 128),
             ("dec", 1536))
COLS = layout(("norm0", 8), ("norm1", 8), ("norm2", 8), ("norm3", 8), ("qa", 1), ("ka", 1), ("qb", 1), ("kb", 1),
              ("mu", FTC), ("w0", 4), ("a0", 4), ("k_k", 4), ("k_a", 4), ("r_k", 4))
ROWS = layout(("sink", 8), ("brt", 36), ("ret_gn", 512), ("rw_gn", 512))


def constants():
    c = np.zeros((P, CST["end"]), np.float32)

    def put(name, a):
        lo, hi = CST[name]
        c[:, lo:hi] = np.asarray(a, np.float32).reshape(P, hi - lo)

    p, i = np.arange(P)[:, None], np.arange(P)[None, :]
    put("ident", p == i)
    put("reset", np.broadcast_to(np.arange(T) % CH != 0, (P, T)))
    col, key = p % GRID_W, np.arange(GRID_W)[None, :]
    start = np.clip(col - KW // 2, 0, GRID_W - KW)
    win = (key >= start) & (key < start + KW)
    put("winm", win)
    put("wina", np.where(win, 0.0, NEG))
    put("slot", np.broadcast_to(np.arange(CAP), (P, CAP)))
    put("desc4", np.broadcast_to(np.arange(4, 0, -1), (P, 4)))
    put("desc32", np.broadcast_to(np.arange(32, 0, -1), (P, 32)))
    put("mAdT", (p < i) & (p // 16 == i // 16))
    put("mAd", (i < p) & (p // 16 == i // 16))
    put("m16T", (p < i) & (p // 32 == i // 32) & (p // 16 != i // 16))
    put("m32T", (p < i) & (p // 64 == i // 64) & (p // 32 != i // 32))
    put("mlt", (p < i) & (p // 64 == i // 64))
    put("mle", (p <= i) & (p // 64 == i // 64))
    put("same", p // 64 == i // 64)
    put("sel", p // 64 == np.arange(2)[None, :])
    put("before", p < i)
    put("ones", np.ones((P, P)))
    half = RET_D // 2
    inv = np.float32(10000.0) ** (-np.arange(half, dtype=np.float32) / np.float32(half))
    ang = np.arange(T, dtype=np.float32)[:, None] * inv[None, :]
    tile = lambda a: a.reshape(NT, P, -1).transpose(1, 0, 2)
    put("cos", tile(np.cos(ang)))
    put("sin", tile(np.sin(ang)))
    logg = np.log(1.0 - np.exp2(-5.0 - np.arange(RET_H)))
    t = np.arange(T)
    seen = (t[:, None] // CH) <= (t[None, :] // CH)
    dec = np.exp(logg[:, None, None] * np.abs(t[None, :, None] - t[None, None, :])) * seen * RET_D ** -0.5
    first = dec[:, :P, :].transpose(1, 0, 2).reshape(P, -1)
    second = dec[:, P:, P:].transpose(1, 0, 2).reshape(P, -1)
    put("dec", np.concatenate([first, second], 1))
    return c


def t5_one_hot():
    rel = np.arange(-(T - 1), T)
    half, exact = 16, 8
    n = np.abs(rel)
    large = exact + (np.log(np.maximum(n, 1) / exact) / np.log(128 / exact) * (half - exact)).astype(np.int32)
    bucket = (rel > 0) * half + np.where(n < exact, n, np.minimum(large, half - 1))
    m = np.zeros((33, REL), np.float32)
    m[bucket, np.arange(REL)] = 1.0
    m[32] = np.where(n <= 128, 0.0, NEG)
    return m


def plan_fills():
    f = []

    def add(who, *key):
        f.append((key, who))

    def norm(n):
        for t in range(NT):
            for b in range(2):
                add("dve", "nt", n, t, b)

    norm(0)
    add("act", "t5")
    for u in range(5):
        for t in range(NT):
            add("act", "p1", u, t)
    for s in ("qa", "ka", "qb", "kb"):
        for t in range(NT):
            add("act", "qkT", s, t)
    for i in range(9):
        if i < 8:
            add("dve", "S", i, 0)
            add("dve", "S", i, 1)
            add("act", "p1", 5 + i // 2, i % 2)
        if i >= 1:
            add("act", "PT", i - 1, 0)
            add("dve", "PT", i - 1, 1)
            add("dve", "PV", i - 1)
    for br in range(2):
        for t in range(NT):
            add("act", "oT", br, t)
    for br in range(2):
        for t in range(NT):
            for n in range(2):
                add("dve", "br", br, t, n)
    for t in range(NT):
        for b in range(2):
            add("act", "yT", t, b)
    for n in range(2):
        for t in range(NT):
            add("dve", "wo", n, t)
    norm(1)
    for u in range(FFK // 2):
        add("act", "gate", u)
        add("dve", "up", u)
    for t in range(NT):
        for n in range(2):
            add("dve", "down", t, n)
    norm(2)
    for c in RW_ORDER:
        add("act", "rw", c)
    for t in range(NT):
        add("act", "p2", 0, t)
    for k in ("z", "za"):
        for b in range(2):
            add("act", k, b)
    for t in range(NT):
        add("act", "p2", 1, t)
    for b in range(2):
        add("act", "ss", b)
    for u in (2, 3):
        for t in range(NT):
            add("act", "p2", u, t)
    for s in ("q", "k"):
        for t in range(NT):
            add("act", "rT", s, t)
    for j in range(3):
        add("dve", "rs", j)
    for t in range(NT):
        add("dve", "ro", t)
    for w in ("A", "B", "K", "V"):
        for t in range(NT):
            add("act", "natl", w, t)
    add("dve", "bonus")
    for m in ("AT", "A"):
        for t in range(NT):
            for par in range(2):
                add("dve", "mat", m, t, par)
    for n, (name, who) in enumerate(INVERSE):
        for t in range(NT):
            for par in range(2):
                add(who, "inv", name, t, par)
        for extra in INV_EXTRA.get(name, ()):
            for t in range(NT):
                for par in range(2):
                    add("dve", "mat", extra, t, par)
        if name == "Z2":
            for t in range(NT):
                add("act", "Q", t)
            for t in range(NT):
                add("act", "gn", t)
    for t in range(NT):
        add("act", "WT", t)
    for c in range(NCH):
        add("dve", "U", c, 0)
        add("act", "U", c, 1)
        if c < NCH - 1:
            add("dve", "St", c)
        if c % 2:
            for par in range(2):
                add("act", "Y", c // 2, par)
    for t in range(NT):
        for b in range(2):
            add("act", "mT", t, b)
    for n in range(2):
        for t in range(NT):
            add("dve", "wo2", n, t)
    norm(3)
    for t in range(NT):
        add("dve", "logit", t)
    for t in range(NT):
        add("dve", "rank", t)
    add("dve", "count")
    return f


RW_ORDER = (6, 2, 3, 0, 1, 4, 5)
INVERSE = (("P2", "act"), ("P2T", "dve"), ("X1", "dve"), ("P4", "act"), ("P4T", "dve"), ("X2", "dve"),
           ("P8T", "act"), ("X3", "dve"), ("T16T", "act"), ("Z1", "act"), ("X4", "dve"), ("T32T", "act"),
           ("Z2", "act"), ("X5", "dve"), ("TT", "act"))
INV_EXTRA = {"X3": ("Aak",), "T32T": ("Arb",), "TT": ("Ark",)}


def build(nc, A, out):
    fills = plan_fills()
    index = {key: n for n, (key, _) in enumerate(fills)}
    turn, seen = {}, {"act": 0, "dve": 0}
    for key, who in fills:
        turn[key] = seen[who]
        seen[who] += 1
    who_of = dict(fills)

    with ExitStack() as ctx:
        def sb(name, shape, dt=F32):
            return ctx.enter_context(nc.sbuf_tensor(name, shape, dt))

        def sem(name):
            return ctx.enter_context(nc.semaphore(name))

        arena = sb("arena", [P, ARENA])
        x = sb("x", [P, NT, D])
        xn = sb("xn", [P, NT, D])
        featT = sb("featT", [P, DK, T])
        cst = sb("cst", [P, CST["end"]])
        cols = sb("cols", [P, COLS["end"]])
        rows = sb("rows", [P, ROWS["end"]])
        lora = sb("lora", [P, 512])
        gup = sb("gup", [P, 512])
        wr = sb("wr", [P, DK, 36])
        t5b = sb("t5b", [33, 8])
        st = sb("st", [P, 512])
        rt = sb("rt", [P, 1024])
        cnt = sb("cnt", [P, 2], I32)
        psum = ctx.enter_context(nc.psum_tensor("psum", [P, 8, 512], F32))

        def area(lay, name, *shape):
            lo, hi = lay[name]
            v = arena[:, lo:hi]
            if len(shape) == 2:
                v = v.rearrange("p (a b) -> p a b", a=shape[0])
            elif len(shape) == 3:
                v = v.rearrange("p (a b c) -> p a b c", a=shape[0], b=shape[1])
            elif len(shape) == 4:
                v = v.rearrange("p (a b c d) -> p a b c d", a=shape[0], b=shape[1], c=shape[2])
            return v

        def piece(lo, *shape):
            n = int(np.prod(shape))
            return area({"v": (lo, lo + n)}, "v", *shape)

        def con(name):
            lo, hi = CST[name]
            return cst[:, lo:hi]

        def colp(name, k=None):
            lo, hi = COLS[name]
            return cols[:, lo:hi] if k is None else cols[:, lo + k:lo + k + 1]

        def row(name):
            lo, hi = ROWS[name]
            return rows[:, lo:hi]

        ident = con("ident")
        nat = area(L1, "nat", NT, NQKV)
        sig = area(L1, "sig", NT, 2048)
        biasA = area(L1, "biasA", 8, 6, 64)
        biasB = area(L1, "biasB", 8, EXT)
        qaT, kaT, qbT = (area(L1, n, 4, T) for n in ("qaT", "kaT", "qbT"))
        kbT = area(L1, "kbT", 2, T)
        kdup = area(L1, "kdup", NT, 2, P)
        negmax, esink, sums = (st[:, 64 + 32 * n:96 + 32 * n] for n in range(3))
        bonus = st[:, 160:176]
        eps_col = st[:, 176:179]
        tanh_w = sb("tanh_w", [64, T])
        sig_g = sb("sig_g", [P, T])
        prob = area(L1, "prob", 2, 2, 2, T)
        probT = area(L1, "probT", 4, 2, 2, P)
        onehot = arena[0:33, L1["probT"][0]:L1["probT"][0] + REL]
        tb_sb = arena[0:8, L1["probT"][0] + 512:L1["probT"][0] + 512 + REL]
        hT = piece(B0, FFK, T)
        silu_t = piece(L1["biasA"][0], 2, 512)
        M0 = LM["M"][0]
        mslot = lambda n: piece(M0 + 1024 * n, 4, T)
        fT = area(LM, "fT", FTC, 257)
        f_r, f_k, f_v = (fT[:, 4 * n:4 * n + 4, 1:257] for n in range(3))
        At, Bt = (piece(LM["RT"][0] + 1024 * n, 4, T) for n in range(2))
        natl = {w: piece(LM["N"][0] + 1024 * n, NT, 512) for n, w in enumerate("ABKV")}
        dtmp, kk, kk2, sw, sa, Ls, Le = (mslot(n) for n in range(7))
        Einv, Ein, Eex, kp, rk, BhT, KhT = sw, Ls, Le, kk2, dtmp, sa, kk2
        retn = piece(M0 + 7 * 1024, NT, 2048)
        rqT, rkT = (piece(M0 + n * 1024, 4, T) for n in (11, 12))
        rsc = (featT[:, 0:4, :], featT[:, 4:6, :].rearrange("p a b -> p (a b)").rearrange("p (h q) -> p h q", h=4))
        mats = [piece(M0 + 2048 * n, NT, 8, P) for n in range(7)]
        AdT, Ad, o16T, o32T, X, P2, P2T = mats
        P4T, P4, P8T, TT, Z = AdT, Ad, P2, P2T, Ad
        AakT, ArbT, ArkT = AdT, P2, Ad
        Qn = piece(M0 + 2048 * 2, NT, 512)
        WT = piece(M0 + 2048 * 2 + 1024, 4, T)
        Un = piece(M0 + 2048 * 3, NT, 2, 256)
        gnat = piece(M0 + 2048 * 3 + 1024, NT, 512)
        ynat = piece(M0 + 2048 * 4, NT, 512)
        ytmp = piece(M0 + 2048 * 4 + 1024, NT, 512)
        S = piece(LM["RT"][0], NCH, 4, 64)
        PC = sb("PC", [P, 4, NCH])
        quad = [piece(QUAD * n, EG, 4, 512) for n in range(NQ)]
        xg = area(LE, "xg", DK, P)
        G, Gw = (area(LE, n, NT, EG, CAP) for n in ("G", "Gw"))
        GT = area(LE, "GT", NT, P)
        sg, hh = (arena[:, LE[n][0]:LE[n][1]] for n in ("sg", "h"))
        hhT = area(LE, "hT", 4, P)
        dd = area(LE, "d", 2, 512)
        rank = rt[:, 0:64].rearrange("p (t e) -> p t e", t=NT)
        comb = rt[:, 64:128].rearrange("p (t e) -> p t e", t=NT)
        rank4, comb4 = rt[:, 576:584], rt[:, 584:592]
        selr = rt[:, 128:192].rearrange("p (t e) -> p t e", t=NT)

        x_in = sem("x_in")
        params_in = sem("params_in")
        rpb_copied = sem("rpb_copied")
        biasA_in = sem("biasA_in")
        t5_in = sem("t5_in")
        t5_stored = sem("t5_stored")
        biasB_in = sem("biasB_in")
        gain_in = sem("gain_in")
        slot_in = [sem(f"slot_in{n}") for n in range(NSLOT)]
        down_units_read = sem("down_units_read")
        filled = sem("psum_filled")
        emptied = {w: sem(f"psum_emptied_{w}") for w in ("act", "dve")}
        dve_step = sem("dve_step")
        act_step = sem("act_step")
        rms_ready = sem("rms_ready")
        var_ready = sem("var_ready")
        root_ready = sem("root_ready")
        eps_ready = sem("eps_ready")
        xn_ready = sem("xn_ready")
        resid_ready = sem("resid_ready")
        qk_ready = sem("qk_ready")
        max_ready = sem("max_ready")
        exp_ready = sem("exp_ready")
        o_ready = sem("o_ready")
        y_ready = sem("y_ready")
        lerp_ready = sem("lerp_ready")
        lora_act = sem("lora_act")
        kk_ready = sem("kk_ready")
        kk2_ready = sem("kk2_ready")
        scan_ready = sem("scan_ready")
        decay_ready = sem("decay_ready")
        rot_ready = sem("rot_ready")
        rw_ready = sem("rw_ready")
        x0_ready = sem("x0_ready")
        mixed_ready = sem("mixed_ready")
        route_ready = sem("route_ready")
        count_ready = sem("count_ready")
        quad_in = [sem(f"quad_in{n}") for n in range(NQ)]
        quads_read = sem("quads_read")
        onehot_ready = sem("onehot_ready")
        gathered = sem("gathered")
        xg_ready = sem("xg_ready")
        silu_ready = sem("silu_ready")
        h_ready = sem("h_ready")
        gt_filled = sem("gt_filled")
        gt_ready = sem("gt_ready")
        hT_filled = sem("hT_filled")
        hT_ready = sem("hT_ready")
        d0_ready = sem("d0_ready")
        d1_ready = sem("d1_ready")
        scattered = sem("scattered")
        moe_done = sem("moe_done")
        shifted = sem("shifted")
        sum_done = sem("sum_done")
        out_ready = sem("out_ready")
        out_done = sem("out_done")

        rpb = A["rpb"]
        RPB = rpb.shape[1]
        rpb_copies = nc.dram_tensor("rpb_copies", (8, GRID_W, RPB), F32, kind="Internal").ap()
        t5_copies = nc.dram_tensor("t5_copies", (8, P, REL), F32, kind="Internal").ap()

        def kxn(w, lo, n):
            return w[:, lo:lo + n].rearrange("(k p) n -> p k n", p=P)

        units, uname = [], {}

        def unit(name, *parts):
            uname[name] = len(units)
            units.append(parts)

        w_in, w_in2 = A["w_in"], A["w_in_2"]
        for u in range(9):
            lo = 512 * u if u < 4 else (2048 if u == 4 else NQKV + 512 * (u - 5))
            n = 256 if u == 4 else 512
            unit(("p1", u), (0, DK, n, kxn(w_in, lo, n)))
        unit(("br", 0), (0, 4, D, kxn(A["w_branch_a"], 0, D)))
        unit(("br", 1), (0, 4, D, kxn(A["w_branch_b"], 0, D)))
        for n in range(2):
            unit(("wo", n), (0, DK, 512, kxn(A["w_out"], 512 * n, 512)))
        for u in range(FFK // 2):
            unit(("ffn", u), (0, DK, 256, kxn(A["w_gate"], 256 * u, 256)),
                 (2048, DK, 256, kxn(A["w_up"], 256 * u, 256)))
        for u in range(-(-FFK // 4)):
            kn = min(4, FFK - 4 * u)
            unit(("down", u), (0, kn, D, A["w_down"][512 * u:512 * u + kn * P, :].rearrange("(k p) n -> p k n", p=P)))
        unit(("rw", 3), (0, DK, 256, kxn(w_in2, 2048 + 1536, 256)))
        for u in (1, 0, 2):
            unit(("rw", u), (0, DK, 512, kxn(w_in2, 2048 + 512 * u, 512)))
        for u in range(4):
            unit(("p2", u), (0, DK, 512, kxn(w_in2, 512 * u, 512)))
        for n in range(2):
            unit(("wo2", n), (0, DK, 512, kxn(A["w_out_2"], 512 * n, 512)))
        loads_so_far, unit_level = [0] * NSLOT, []
        for n, parts in enumerate(units):
            loads_so_far[n % NSLOT] += 16 * len(parts)
            unit_level.append(loads_so_far[n % NSLOT])
        last_fill = {}
        for u in range(9):
            last_fill[("p1", u)] = ("p1", u, 1)
        for br in range(2):
            last_fill[("br", br)] = ("br", br, 1, 1)
        for n in range(2):
            last_fill[("wo", n)] = ("wo", n, 1)
            last_fill[("wo2", n)] = ("wo2", n, 1)
        for u in range(FFK // 2):
            last_fill[("ffn", u)] = ("up", u)
        last_fill[("rw", 3)] = ("rw", 6)
        for u in range(3):
            last_fill[("rw", u)] = ("rw", 2 * u + 1)
        for u in range(4):
            last_fill[("p2", u)] = ("p2", u, 1)
        last_fill[("down", 5)] = ("down", 1, 1)
        names = list(uname)

        def wview(name, part=0):
            n = uname[name]
            off, k, w, _ = units[n][part]
            return piece((n % NSLOT) * SLOT + off, k, w)

        def wait_filled(eng, *key):
            eng.wait_ge(filled, index[key] + 1)

        def wait_emptied(eng, *key):
            eng.wait_ge(emptied[who_of[key]], turn[key] + 1)

        def bank(*key):
            return psum[:, index[key] % 8, :]

        class Steps:

            def __init__(self, eng, s):
                self.eng, self.sem, self.n, self.drains = eng, s, 0, 0

            def link(self, ins):
                ins.then_inc(self.sem, 1)
                self.n += 1
                self.eng.wait_ge(self.sem, self.n)

            def empty(self, who, ins, *key):
                assert who_of[key] == who and turn[key] == self.drains, (key, turn[key], self.drains)
                self.drains += 1
                ins.then_inc(emptied[who], 1)
                self.eng.wait_ge(emptied[who], self.drains)

        PARAMS_IN = 16 * 6
        block = ctx.enter_context(nc.Block())

        moe_w = {"gate": A["w_gate_2"], "up": A["w_up_2"], "down": A["w_down_2"]}
        QUADS_PER_GROUP = 6
        ALLQ = NG * QUADS_PER_GROUP

        def quad_slot(q):
            return (2, 3, 1, 0)[q % NQ]

        @block.sync
        def _(sp):
            nc.sync.dma_start(x[:], A["x"].rearrange("(t p) d -> p t d", p=P)).then_inc(x_in, 16)
            for n, parts in enumerate(units):
                if n >= NSLOT:
                    old = names[n - NSLOT]
                    if old in last_fill:
                        wait_filled(sp, *last_fill[old])
                    else:
                        sp.wait_ge(down_units_read, old[1] + 1)
                for off, k, w, src in parts:
                    nc.sync.dma_start(piece((n % NSLOT) * SLOT + off, k, w), src).then_inc(slot_in[n % NSLOT], 16)

            def load_quad(pair, q):
                gp, q6 = q // QUADS_PER_GROUP, q % QUADS_PER_GROUP
                kind, half = ("gate", "up", "down")[q6 // 2], q6 % 2
                for j in range(EG):
                    e = pair * (2 * EG) + (gp * EG + j)
                    if isinstance(e, int):
                        w = moe_w[kind][e]
                    else:
                        w = moe_w[kind][bass.ds(e, 1)].rearrange("a k n -> (a k) n")
                    w = w[:, 512 * half:512 * half + 512] if kind == "down" else w[512 * half:512 * half + 512, :]
                    nc.sync.dma_start(quad[quad_slot(q)][:, j], w.rearrange("(k p) n -> p k n", p=P))\
                        .then_inc(quad_in[quad_slot(q)], 16)

            def moe_stream(r, first):
                for q in range(NQ):
                    if first and q == 0:
                        sp.wait_ge(mixed_ready, 2 * NT)
                    if first and q >= 2:
                        wait_filled(sp, "wo2", q - 2, 1)
                    if not first and q == 0:
                        sp.wait_ge(quads_read, r * ALLQ)
                    load_quad(0, q)
                with sp.Fori(0, NG // 2 - 1) as pair:
                    for q in range(NQ, 12 + NQ):
                        sp.wait_ge(quads_read, r * ALLQ + pair * 12 + (q - NQ + 1))
                        load_quad(pair + q // 12, q % 12)
                for q in range(NQ, 12):
                    sp.wait_ge(quads_read, r * ALLQ + (ALLQ - 12 + q - NQ + 1))
                    load_quad(NG // 2 - 1, q)

            moe_stream(0, True)
            sp.wait_ge(count_ready, 1)
            most = sp.value_load(cnt[0:1, 0:1], min_val=0, max_val=T)
            with sp.Fori(1, ROUNDS) as r:
                with sp.If(most > r * CAP):
                    moe_stream(r, False)
            for t in range(NT):
                sp.wait_ge(out_ready, t + 1)
                nc.sync.dma_start(out[t * P:(t + 1) * P, :], xn[:, t, :]).then_inc(out_done, 16)
            sp.wait_ge(out_done, 16 * NT)

        @block.gpsimd
        def _(pool):
            pool.wait_ge(rpb_copied, 16)
            for h in range(8):
                for half in range(2):
                    src = bass.AP(tensor=rpb_copies.tensor, offset=h * GRID_W * RPB + (5 - half) * 31 + 15,
                                  ap=[[RPB - 1, GRID_W], [31, 6], [1, GRID_W]])
                    nc.gpsimd.dma_start(biasA[64 * half:64 * half + 64, h], src).then_inc(biasA_in, 16)
            wait_emptied(pool, "t5")
            nc.gpsimd.dma_start(t5_copies, tb_sb.unsqueeze(1).to_broadcast([8, P, REL])).then_inc(t5_stored, 16)
            pool.wait_ge(t5_stored, 16)
            src = bass.AP(tensor=t5_copies.tensor, offset=P - 1, ap=[[REL - 1, P], [P * REL, 8], [1, EXT]])
            nc.gpsimd.dma_start(biasB, src).then_inc(biasB_in, 16)
            wait_filled(pool, "logit", NT - 1)
            nc.gpsimd.dma_start(featT[:, 0:4, :].rearrange("p a b -> p (a b)"),
                                A["final_gain"].to_broadcast([P, D])).then_inc(gain_in, 16)

        @block.tensor
        def _(pe):
            at = [0]

            def begin(*key):
                n = index[key]
                assert n == at[0], (key, n, at[0])
                at[0] += 1
                if n >= 8:
                    wait_emptied(pe, *fills[n - 8][0])
                return psum[:, n % 8, :]

            def end(ins):
                ins.then_inc(filled, 1)

            def have(name):
                n = uname[name]
                pe.wait_ge(slot_in[n % NSLOT], unit_level[n])

            mm, tr = nc.tensor.matmul, nc.tensor.transpose

            def transposes(key, sources, ready):
                b = begin(*key).rearrange("p (k q) -> p k q", q=P)
                ready()
                for k, s in enumerate(sources):
                    ins = tr(b[:, k, :], s, ident)
                end(ins)

            def norm_T(n):
                for t in range(NT):
                    for h in range(2):
                        transposes(("nt", n, t, h), [xn[:, t, (4 * h + k) * P:(4 * h + k + 1) * P] for k in range(4)],
                                   lambda: pe.wait_ge(xn_ready, NT * n + t + 1))

            def project(key, w, t, width):
                b = begin(*key)
                for k in range(DK):
                    ins = mm(b[:, 0:width], featT[:, k, t * P:(t + 1) * P], w[:, k, :], start=k == 0, stop=k == DK - 1)
                end(ins)

            pe.wait_ge(params_in, PARAMS_IN)
            norm_T(0)
            b = begin("t5")
            pe.wait_ge(t5_in, 32)
            end(mm(b[0:8, 0:REL], t5b[:], onehot, start=True, stop=True))
            wait_emptied(pe, "nt", 0, 1, 1)
            for u in range(5):
                have(("p1", u))
                for t in range(NT):
                    project(("p1", u, t), wview(("p1", u)), t, 256 if u == 4 else 512)
            offs = {"qa": 0, "ka": 512, "qb": 1536}
            for s, name in enumerate(("qa", "ka", "qb", "kb")):
                for t in range(NT):
                    if name == "kb":
                        src = [kdup[:, t, kv, :] for kv in range(2)]
                    else:
                        src = [nat[:, t, offs[name] + P * k:offs[name] + P * (k + 1)] for k in range(4)]
                    transposes(("qkT", name, t), src, lambda: pe.wait_ge(qk_ready, 2 * s + t + 1))

            def scores(i):
                br, t, g = i // 4, i // 2 % 2, i % 2
                banks = [begin("S", i, par).rearrange("p (a k) -> p a k", a=2) for par in range(2)]
                for name in ("qa", "ka") if br == 0 else ("qb", "kb"):
                    wait_emptied(pe, "qkT", name, 1)
                for pair in range(2):
                    for par in range(2):
                        rows_ = slice(64 * par, 64 * par + 64)
                        q = (qbT if br else qaT)[rows_, 2 * g + pair, t * P:(t + 1) * P]
                        k = kbT[rows_, g, :] if br else kaT[rows_, 2 * g + pair, :]
                        ins = mm(banks[par][:, pair, :], q, k, start=True, stop=True)
                        if pair == 1:
                            end(ins)

            def weighted(i):
                br, t, g = i // 4, i // 2 % 2, i % 2
                for par in range(2):
                    b = begin("PT", i, par).rearrange("p (a k q) -> p a k q", a=2, k=2)
                    pe.wait_ge(exp_ready, 2 * i + par + 1)
                    for pair in range(2):
                        for kt in range(NT):
                            ins = tr(b[:, pair, kt, :], prob[:, i % 2, par, pair, kt * P:(kt + 1) * P], ident)
                    end(ins)
                b = begin("PV", i)
                for par in range(2):
                    wait_emptied(pe, "PT", i, par)
                for h in range(4):
                    for kt in range(NT):
                        v0 = 2176 + 64 * g if br else 1024 + 64 * (4 * g + h)
                        ins = mm(b[:, 64 * h:64 * h + 64], probT[:, 2 * (i % 2) + h % 2, h // 2, kt, :],
                                 nat[:, kt, v0:v0 + 64], start=kt == 0, stop=kt == NT - 1)
                end(ins)

            for i in range(9):
                if i < 8:
                    scores(i)
                    u, t = 5 + i // 2, i % 2
                    have(("p1", u))
                    project(("p1", u, t), wview(("p1", u)), t, 512)
                if i >= 1:
                    weighted(i - 1)
            for br in range(2):
                for t in range(NT):
                    transposes(("oT", br, t), [xn[:, t, 512 * br + P * k:512 * br + P * (k + 1)] for k in range(4)],
                               lambda: wait_emptied(pe, "PV", 4 * br + 2 * t + 1))
            for br in range(2):
                have(("br", br))
                w = wview(("br", br))
                for t in range(NT):
                    for n in range(2):
                        b = begin("br", br, t, n)
                        wait_emptied(pe, "oT", br, t)
                        for k in range(4):
                            ins = mm(b, featT[:, 4 * br + k, t * P:(t + 1) * P], w[:, k, 512 * n:512 * n + 512],
                                     start=k == 0, stop=k == 3)
                        end(ins)
            for t in range(NT):
                for h in range(2):
                    transposes(("yT", t, h), [sig[:, t, (4 * h + k) * P:(4 * h + k + 1) * P] for k in range(4)],
                               lambda: pe.wait_ge(y_ready, 2 * t + h + 1))
            wait_emptied(pe, "yT", 1, 1)
            for n in range(2):
                have(("wo", n))
                for t in range(NT):
                    project(("wo", n, t), wview(("wo", n)), t, 512)
            norm_T(1)
            wait_emptied(pe, "nt", 1, 1, 1)
            for u in range(FFK // 2):
                have(("ffn", u))
                for part, name in enumerate(("gate", "up")):
                    w = wview(("ffn", u), part)
                    b = begin(name, u).rearrange("p (f t) -> p f t", f=2)
                    for f in range(2):
                        for k in range(DK):
                            ins = mm(b[:, f, :], w[:, k, P * f:P * f + P], featT[:, k, :], start=k == 0, stop=k == DK - 1)
                    end(ins)
            banks = {(t, n): begin("down", t, n) for t in range(NT) for n in range(2)}
            for u in range(-(-FFK // 4)):
                have(("down", u))
                w = wview(("down", u))
                kn = units[uname[("down", u)]][0][1]
                for k in range(4 * u, 4 * u + kn):
                    wait_emptied(pe, "up", k // 2)
                    for t in range(NT):
                        for n in range(2):
                            ins = mm(banks[t, n], hT[:, k, t * P:(t + 1) * P], w[:, k - 4 * u, 512 * n:512 * n + 512],
                                     start=k == 0, stop=k == FFK - 1, skip_group_check=True)
                            if k == FFK - 1:
                                end(ins)
                if u < FFK // 4:
                    ins.then_inc(down_units_read, 1)

            norm_T(2)
            wait_emptied(pe, "nt", 2, 1, 1)
            for c in RW_ORDER:
                u = c // 2
                have(("rw", u))
                w = wview(("rw", u))
                b = begin("rw", c).rearrange("p (f t) -> p f t", f=2)
                for f in range(2):
                    lo = P * f if c == 6 else P * (2 * (c % 2) + f)
                    for k in range(DK):
                        ins = mm(b[:, f, :], w[:, k, lo:lo + P], featT[:, k, :], start=k == 0, stop=k == DK - 1)
                end(ins)

            def ret_project(u):
                have(("p2", u))
                for t in range(NT):
                    project(("p2", u, t), wview(("p2", u)), t, 512)

            ret_project(0)
            for name, lo, level in (("z", 0, 1), ("za", 64, 0)):
                for h in range(2):
                    b = begin(name, h).rearrange("p (f t) -> p f t", f=2)
                    if level:
                        pe.wait_ge(lora_act, 1)
                    else:
                        pe.wait_ge(lerp_ready, 1)
                    src = tanh_w[:] if level else fT[64:128, 12, 1:257]
                    for f in range(2):
                        c = 2 * h + f
                        ins = mm(b[:, f, :], lora[lo:lo + 64, P * c:P * c + P], src, start=True, stop=True)
                    end(ins)
            ret_project(1)
            for h in range(2):
                b = begin("ss", h)
                pe.wait_ge(kk2_ready, 1)
                end(mm(b, con("same"), kk2[:, 2 * h:2 * h + 2, :].rearrange("p a b -> p (a b)"), start=True, stop=True))
            ret_project(2)
            ret_project(3)
            for s, name in enumerate(("q", "k")):
                for t in range(NT):
                    transposes(("rT", name, t), [retn[:, t, 512 * s + P * k:512 * s + P * (k + 1)] for k in range(4)],
                               lambda: pe.wait_ge(rot_ready, t + 1))
            for j in range(3):
                b = begin("rs", j)
                for name in ("q", "k"):
                    wait_emptied(pe, "rT", name, 1)
                if j < 2:
                    for a in range(2):
                        ins = mm(b[:, T * a:T * a + T], rkT[:, 2 * j + a, 0:P], rqT[:, 2 * j + a, :], start=True, stop=True)
                else:
                    for a in range(4):
                        ins = mm(b[:, P * a:P * a + P], rkT[:, a, P:T], rqT[:, a, P:T], start=True, stop=True)
                end(ins)
            for t in range(NT):
                b = begin("ro", t)
                wait_emptied(pe, "rs", 2 * t if t else 1)
                for a in range(4):
                    for kt in range(t + 1):
                        lhs = rsc[0][:, a, t * P:(t + 1) * P] if kt == 0 else rsc[1][:, a, :]
                        ins = mm(b[:, P * a:P * a + P], lhs, retn[:, kt, 1024 + P * a:1024 + P * (a + 1)],
                                 start=kt == 0, stop=kt == t)
                end(ins)
            src = {"A": At, "B": BhT, "K": KhT, "V": f_v}
            for w in "ABKV":
                for t in range(NT):
                    transposes(("natl", w, t), [src[w][:, k, t * P:(t + 1) * P] for k in range(4)],
                               lambda: pe.wait_ge(rw_ready, 1))
            b = begin("bonus")
            for t in range(NT):
                for k in range(4):
                    ins = mm(b[:, 8 * t + 2 * k:8 * t + 2 * k + 2], rk[:, k, t * P:(t + 1) * P], con("sel"),
                             start=True, stop=True)
            end(ins)

            sides = {"AT": (Bt, At), "A": (At, Bt), "Aak": (f_k, At), "Arb": (Bt, f_r), "Ark": (f_k, f_r)}

            def mat(name):
                lhs, rhs = sides[name]
                for t in range(NT):
                    for par in range(2):
                        b = begin("mat", name, t, par).rearrange("p (i q) -> p i q", i=4)
                        for i in range(4):
                            r = slice(64 * par, 64 * par + 64)
                            ins = mm(b[:, i, :], lhs[r, i, t * P:(t + 1) * P], rhs[r, i, t * P:(t + 1) * P],
                                     start=True, stop=True)
                        end(ins)

            mat("AT")
            mat("A")
            steps = {
                "P2": (AdT, Ad, ("mat A",)), "P2T": (Ad, AdT, ()),
                "X1": (P2T, X, ("P2T", "X0")), "P4": (P2T, P2, ("P2",)), "P4T": (P2, P2T, ()),
                "X2": (P4T, X, ("P4T", "X1")), "P8T": (P4, P4T, ("P4",)), "X3": (P8T, X, ("P8T", "X2")),
                "T16T": (X, None, ("X3",)), "Z1": (o16T, X, ()), "X4": (TT, Z, ("Z1", "T16T")),
                "T32T": (X, None, ("X4",)), "Z2": (o32T, X, ()), "X5": (TT, Z, ("Z2", "T32T")),
                "TT": (X, None, ("X5",)),
            }
            for name, _ in INVERSE:
                lhs, rhs, needs = steps[name]
                for t in range(NT):
                    for par in range(2):
                        b = begin("inv", name, t, par).rearrange("p (i q) -> p i q", i=4)
                        for need in needs:
                            if need == "mat A":
                                wait_emptied(pe, "mat", "A", t, par)
                            elif need == "X0":
                                pe.wait_ge(x0_ready, 2 * t + par + 1)
                            else:
                                wait_emptied(pe, "inv", need, t, par)
                        for i in range(4):
                            h = 4 * par + i
                            if rhs is None:
                                ins = tr(b[:, i, :], lhs[:, t, h, :], ident)
                            else:
                                ins = mm(b[:, i, :], lhs[:, t, h, :], rhs[:, t, h, :], start=True, stop=True)
                        end(ins)
                for extra in INV_EXTRA.get(name, ()):
                    mat(extra)
                if name == "Z2":
                    for t in range(NT):
                        b = begin("Q", t)
                        for par in range(2):
                            wait_emptied(pe, "mat", "Aak", t, par)
                        wait_emptied(pe, "natl", "V", t)
                        for h in range(8):
                            ins = mm(b[:, 64 * h:64 * h + 64], AakT[:, t, 4 * (h % 2) + h // 2, :],
                                     natl["V"][:, t, 64 * h:64 * h + 64], start=True, stop=True)
                        end(ins)
                    for t in range(NT):
                        b = begin("gn", t)
                        pe.wait_ge(lora_act, 2)
                        end(mm(b, sig_g[:, t * P:(t + 1) * P], gup[:], start=True, stop=True))
            for t in range(NT):
                b = begin("WT", t).rearrange("p (i q) -> p i q", i=4)
                for par in range(2):
                    wait_emptied(pe, "inv", "TT", t, par)
                for h in range(8):
                    ins = mm(b[64 * (h % 2):64 * (h % 2) + 64, h // 2, :], natl["A"][:, t, 64 * h:64 * h + 64],
                             TT[:, t, 4 * (h % 2) + h // 2, :], start=True, stop=True, skip_group_check=True)
                end(ins)
            for c in range(NCH):
                t, ro = c // 2, 64 * (c % 2)
                tok = slice(CH * c, CH * c + CH)
                for par in range(2):
                    b = begin("U", c, par)
                    wait_emptied(pe, "Q", t)
                    wait_emptied(pe, "WT", t)
                    if c > 0:
                        wait_emptied(pe, "St", c - 1)
                    for i in range(4):
                        h = 2 * i + par
                        o = b[ro:ro + 64, 64 * i:64 * i + 64]
                        ins = mm(o, TT[:, t, 4 * par + i, ro:ro + 64], Qn[:, t, 64 * h:64 * h + 64],
                                 start=True, stop=c == 0)
                        if c > 0:
                            r = slice(64 * par, 64 * par + 64)
                            ins = mm(o, WT[r, i, tok], S[r, c, i, :], start=False, stop=True)
                    end(ins)
                if c < NCH - 1:
                    b = begin("St", c).rearrange("p (i v) -> p i v", v=64)
                    for par in range(2):
                        wait_emptied(pe, "U", c, par)
                    r = slice(ro, ro + 64)
                    for h in range(8):
                        par, i = h % 2, h // 2
                        o = b[64 * par:64 * par + 64, i, :]
                        mm(o, natl["B"][r, t, 64 * h:64 * h + 64], Un[r, t, par, 64 * i:64 * i + 64],
                           start=True, stop=False, skip_group_check=True)
                        ins = mm(o, natl["K"][r, t, 64 * h:64 * h + 64], natl["V"][r, t, 64 * h:64 * h + 64],
                                 start=False, stop=True, skip_group_check=True)
                    end(ins)
                if c % 2:
                    for par in range(2):
                        b = begin("Y", t, par)
                        for p2 in range(2):
                            wait_emptied(pe, "U", c, p2)
                            wait_emptied(pe, "mat", "Ark", t, p2)
                        for i in range(4):
                            h = 2 * i + par
                            mm(b[:, 64 * i:64 * i + 64], ArbT[:, t, 4 * par + i, :], Un[:, t, par, 64 * i:64 * i + 64],
                               start=True, stop=False, skip_group_check=True)
                            ins = mm(b[:, 64 * i:64 * i + 64], ArkT[:, t, 4 * par + i, :], natl["V"][:, t, 64 * h:64 * h + 64],
                                     start=False, stop=False, skip_group_check=True)
                            r = slice(64 * par, 64 * par + 64)
                            for cc in (c - 1, c):
                                if cc > 0:
                                    ins = mm(b[64 * (cc % 2):64 * (cc % 2) + 64, 64 * i:64 * i + 64],
                                             f_r[r, i, CH * cc:CH * cc + CH], S[r, cc, i, :],
                                             start=False, stop=cc == c, skip_group_check=True)
                        end(ins)
            for t in range(NT):
                for h in range(2):
                    transposes(("mT", t, h), [xn[:, t, (4 * h + k) * P:(4 * h + k + 1) * P] for k in range(4)],
                               lambda: pe.wait_ge(mixed_ready, t + 1 + NT * h))
            wait_emptied(pe, "mT", 1, 1)
            for n in range(2):
                have(("wo2", n))
                for t in range(NT):
                    project(("wo2", n, t), wview(("wo2", n)), t, 512)
            norm_T(3)
            for t in range(NT):
                b = begin("logit", t)
                wait_emptied(pe, "nt", 3, t, 1)
                for k in range(DK):
                    ins = mm(b[:, 0:36], featT[:, k, t * P:(t + 1) * P], wr[:, k, :], start=k == 0, stop=k == DK - 1)
                end(ins)
            for t in range(NT):
                b = begin("rank", t)
                pe.wait_ge(route_ready, 1)
                if t:
                    mm(b[:, 0:E], con("ones"), selr[:, 0, :], start=True, stop=False)
                end(mm(b[:, 0:E], con("before"), selr[:, t, :], start=t == 0, stop=True))
            b = begin("count")
            for t in range(NT):
                ins = mm(b[:, 0:E], con("ones"), selr[:, t, :], start=t == 0, stop=t == NT - 1)
            end(ins)

            wait_emptied(pe, "count")
            ybank = {(t, n): psum[:, 2 * t + n, :] for t in range(NT) for n in range(2)}
            pe.wait_ge(gt_ready, 1)
            for t in range(NT):
                for n in range(2):
                    ins = mm(ybank[t, n], GT[:, t, :], dd[:, n, :], start=True, stop=False, skip_group_check=True)
            ins.then_inc(scattered, 1)

            def moe_group(r, pair, gp):
                n = r * NG + pair * 2 + gp
                base = r * ALLQ + pair * 12 + gp * 6

                def quad_ready(q):
                    pe.wait_ge(quad_in[quad_slot(q)], r * (12 * 64) + pair * (3 * 64) + (q // NQ + 1) * 64)
                    return quad[quad_slot(q)]

                pe.wait_ge(onehot_ready, n + 1)
                for kb in range(2):
                    b = psum[:, 6 + kb, :].rearrange("p (k s) -> p k s", k=4)
                    for k in range(4):
                        for t in range(NT):
                            ins = mm(b[:, k, :], xn[:, t, (4 * kb + k) * P:(4 * kb + k + 1) * P],
                                     G[:, t].rearrange("p e s -> p (e s)"), start=t == 0, stop=t == NT - 1)
                    ins.then_inc(gathered, 1)
                pe.wait_ge(xg_ready, 2 * n + 2)
                for m in range(2):
                    for half in range(2):
                        w = quad_ready(6 * gp + 2 * m + half)
                        for k in range(4):
                            for j in range(EG):
                                ins = mm(psum[32 * j:32 * j + 32, 4 + m, :], xg[:, 4 * half + k, 32 * j:32 * j + 32],
                                         w[:, j, k, :], start=half == 0 and k == 0, stop=half == 1 and k == 3,
                                         skip_group_check=True)
                        ins.then_inc(quads_read, 1)
                b = psum[:, 6, 0:2 * P].rearrange("p (t q) -> p t q", t=NT)
                for t in range(NT):
                    ins = tr(b[:, t, :], Gw[:, t].rearrange("p e s -> p (e s)"), ident)
                ins.then_inc(gt_filled, 1)
                pe.wait_ge(h_ready, n + 1)
                b = psum[:, 7, :].rearrange("p (k s) -> p k s", k=4)
                for k in range(4):
                    ins = tr(b[:, k, :], hh[:, k * P:(k + 1) * P], ident)
                ins.then_inc(hT_filled, 1)
                pe.wait_ge(hT_ready, n + 1)
                for half in range(2):
                    w = quad_ready(6 * gp + 4 + half)
                    for k in range(4):
                        for j in range(EG):
                            ins = mm(psum[32 * j:32 * j + 32, 4 + half, :], hhT[:, k, 32 * j:32 * j + 32], w[:, j, k, :],
                                     start=k == 0, stop=k == 3, skip_group_check=True)
                    ins.then_inc(quads_read, 1)
                pe.wait_ge(gt_ready, n + 2)
                pe.wait_ge(d0_ready, n + 1)
                pe.wait_ge(d1_ready, n + 1)
                for t in range(NT):
                    for k in range(2):
                        ins = mm(ybank[t, k], GT[:, t, :], dd[:, k, :], start=False, stop=False, skip_group_check=True)
                ins.then_inc(scattered, 1)

            def moe_round(r):
                with pe.Fori(0, NG // 2) as pair:
                    for gp in range(2):
                        moe_group(r, pair, gp)

            moe_round(0)
            pe.wait_ge(count_ready, 1)
            most = pe.value_load(cnt[0:1, 0:1], min_val=0, max_val=T)
            with pe.Fori(1, ROUNDS) as r:
                with pe.If(most > r * CAP):
                    moe_round(r)
            mm(psum[:, 4, 0:P], ident, ident, start=True, stop=True).then_inc(moe_done, 1)

        @block.scalar
        def _(act):
            a = Steps(act, act_step)
            fn = nc.scalar.activation
            empty = lambda ins, *key: a.empty("act", ins, *key)

            def squares(n, ready):
                for t in range(NT):
                    ready(t)
                    s = st[:, 2 * n + t:2 * n + t + 1]
                    a.link(fn(xn[:, t, :], x[:, t, :], ACT.Square, accum_out=s))
                    fn(s, s, ACT.Sqrt, scale=1.0 / D, bias=eps_col[:, 0:1]).then_inc(rms_ready, 1)

            n_roots = [0]

            def root(lo, n, d, k):
                n_roots[0] += 1
                act.wait_ge(var_ready, n_roots[0])
                s = st[:, lo:lo + n]
                fn(s, s, ACT.Sqrt, scale=1.0 / d, bias=eps_col[:, k:k + 1]).then_inc(root_ready, 1)

            nc.scalar.dma_start(cst[:], A["cst"]).then_inc(params_in, 16)
            nc.scalar.dma_start(cols[:], A["cols"]).then_inc(params_in, 16)
            nc.scalar.dma_start(rows[:], A["rows"].to_broadcast([P, ROWS["end"]])).then_inc(params_in, 16)
            nc.scalar.dma_start(t5b[:], A["t5"]).then_inc(t5_in, 16)
            nc.scalar.dma_start(onehot, A["onehot"]).then_inc(t5_in, 16)
            nc.scalar.dma_start(lora[:], A["lora"]).then_inc(params_in, 16)
            nc.scalar.dma_start(gup[:], A["gup"]).then_inc(params_in, 16)
            nc.scalar.dma_start(wr[:], A["wr"].rearrange("(k p) n -> p k n", p=P)).then_inc(params_in, 16)
            nc.scalar.dma_start(rpb_copies, rpb.unsqueeze(1).to_broadcast([8, GRID_W, RPB])).then_inc(rpb_copied, 16)
            act.wait_ge(eps_ready, 3)
            squares(0, lambda t: act.wait_ge(x_in, 16))
            wait_filled(act, "t5")
            empty(fn(tb_sb, bank("t5")[0:8, 0:REL], ACT.Copy), "t5")
            for u in range(5):
                lo = 512 * u
                for t in range(NT):
                    w = 256 if u == 4 else 512
                    wait_filled(act, "p1", u, t)
                    empty(fn(nat[:, t, lo:lo + w], bank("p1", u, t)[:, 0:w], ACT.Copy), "p1", u, t)
                if u in (2, 4):
                    root(*QK_SUMS[u // 2 - 1], HD, 0)
            dsts = {"qa": qaT, "ka": kaT, "qb": qbT, "kb": kbT}
            for name in ("qa", "ka", "qb", "kb"):
                nk = 2 if name == "kb" else 4
                for t in range(NT):
                    wait_filled(act, "qkT", name, t)
                    empty(fn(dsts[name][:, :, t * P:(t + 1) * P],
                             bank("qkT", name, t)[:, 0:nk * P].rearrange("p (k q) -> p k q", k=nk),
                             ACT.Copy, scale=colp(name)), "qkT", name, t)
            for i in range(9):
                if i < 8:
                    for par in range(2):
                        act.wait_ge(max_ready, 2 * i + par + 1)
                        for pair in range(2):
                            k = 4 * i + 2 * par + pair
                            pr = prob[:, i % 2, par, pair, :]
                            ins = fn(pr, pr, ACT.Exp, bias=negmax[:, k:k + 1], accum_out=sums[:, k:k + 1])
                            if i >= 4 or pair == 0:
                                a.link(ins)
                        if i >= 4:
                            k = 4 * i + 2 * par
                            ins = fn(esink[:, k:k + 2], esink[:, k:k + 2], ACT.Exp)
                        ins.then_inc(exp_ready, 1)
                    u, t = 5 + i // 2, i % 2
                    wait_filled(act, "p1", u, t)
                    empty(fn(sig[:, t, 512 * (u - 5):512 * (u - 5) + 512], bank("p1", u, t), ACT.Sigmoid), "p1", u, t)
                if i == 1:
                    act.wait_ge(t5_stored, 16)
                if i >= 1:
                    wait_filled(act, "PT", i - 1, 0)
                    empty(fn(probT[:, 2 * ((i - 1) % 2)].rearrange("p a k q -> p (a k q)"), bank("PT", i - 1, 0), ACT.Copy),
                          "PT", i - 1, 0)
            for br in range(2):
                for t in range(NT):
                    wait_filled(act, "oT", br, t)
                    empty(fn(featT[:, 4 * br:4 * br + 4, t * P:(t + 1) * P],
                             bank("oT", br, t).rearrange("p (k q) -> p k q", k=4), ACT.Copy), "oT", br, t)
            for t in range(NT):
                for h in range(2):
                    wait_filled(act, "yT", t, h)
                    empty(fn(featT[:, 4 * h:4 * h + 4, t * P:(t + 1) * P],
                             bank("yT", t, h).rearrange("p (k q) -> p k q", k=4), ACT.Copy), "yT", t, h)
            squares(1, lambda t: wait_emptied(act, "wo", 1, t))
            for u in range(FFK // 2):
                wait_filled(act, "gate", u)
                if u >= 2:
                    wait_emptied(act, "up", u - 2)
                empty(fn(silu_t[:, u % 2, :], bank("gate", u), ACT.Silu), "gate", u)

            squares(2, lambda t: wait_emptied(act, "down", t, 1))
            for c in RW_ORDER:
                wait_filled(act, "rw", c)
                if c == RW_ORDER[0]:
                    act.wait_ge(xn_ready, 3 * NT)
                empty(fn(fT[:, 2 * c:2 * c + 2, 1:257], bank("rw", c).rearrange("p (f t) -> p f t", f=2), ACT.Copy), "rw", c)
                if c == RW_ORDER[2]:
                    act.wait_ge(lerp_ready, 1)
                    fn(tanh_w[:], fT[0:64, 12, 1:257], ACT.Tanh).then_inc(lora_act, 1)
                    fn(sig_g[:], fT[:, 13, 1:257], ACT.Sigmoid).then_inc(lora_act, 1)

            def ret_move(u):
                for t in range(NT):
                    wait_filled(act, "p2", u, t)
                    empty(fn(retn[:, t, 512 * u:512 * u + 512], bank("p2", u, t), ACT.Silu if u == 3 else ACT.Copy),
                          "p2", u, t)

            ret_move(0)
            for name, dst, bias in (("z", sw, "w0"), ("za", sa, "a0")):
                for h in range(2):
                    wait_filled(act, name, h)
                    b = bank(name, h).rearrange("p (f t) -> p f t", f=2)
                    a.link(fn(dst[:, 2 * h, :], b[:, 0, :], ACT.Sigmoid, bias=colp(bias, 2 * h)))
                    empty(fn(dst[:, 2 * h + 1, :], b[:, 1, :], ACT.Sigmoid, bias=colp(bias, 2 * h + 1)), name, h)
            act.wait_ge(kk_ready, 1)
            fn(kk2, kk, ACT.Square).then_inc(kk2_ready, 1)
            ret_move(1)
            for h in range(2):
                wait_filled(act, "ss", h)
                empty(fn(kk2[:, 2 * h:2 * h + 2, :].rearrange("p a b -> p (a b)"), bank("ss", h), ACT.Sqrt), "ss", h)
            act.wait_ge(scan_ready, 1)
            a.link(fn(Einv, Ls, ACT.Exp, scale=DECAY))
            a.link(fn(Ein, Ls, ACT.Exp, scale=-DECAY))
            fn(Eex, Le, ACT.Exp, scale=-DECAY).then_inc(decay_ready, 1)
            ret_move(2)
            ret_move(3)
            for name, dst in (("q", rqT), ("k", rkT)):
                for t in range(NT):
                    wait_filled(act, "rT", name, t)
                    empty(fn(dst[:, :, t * P:(t + 1) * P], bank("rT", name, t).rearrange("p (k q) -> p k q", k=4), ACT.Copy),
                          "rT", name, t)
            for t in range(NT):
                root(48, RET_H, RET_D, 1)
            for w in "ABKV":
                for t in range(NT):
                    wait_filled(act, "natl", w, t)
                    empty(fn(natl[w][:, t, :], bank("natl", w, t), ACT.Copy), "natl", w, t)
            dst = {"P2": P2, "P4": P4, "P8T": P8T, "T16T": TT, "T32T": TT, "TT": TT, "Z1": Z, "Z2": Z}
            for name, who in INVERSE:
                if who == "act":
                    for t in range(NT):
                        for par in range(2):
                            key = ("inv", name, t, par)
                            wait_filled(act, *key)
                            empty(fn(dst[name][:, t, 4 * par:4 * par + 4, :].rearrange("p i q -> p (i q)"), bank(*key),
                                     ACT.Copy), *key)
                if name == "Z2":
                    for t in range(NT):
                        wait_filled(act, "Q", t)
                        empty(fn(Qn[:, t, :], bank("Q", t), ACT.Copy), "Q", t)
                    for t in range(NT):
                        wait_filled(act, "gn", t)
                        empty(fn(gnat[:, t, :], bank("gn", t), ACT.Copy), "gn", t)
            for t in range(NT):
                wait_filled(act, "WT", t)
                empty(fn(WT[:, :, t * P:(t + 1) * P], bank("WT", t).rearrange("p (i q) -> p i q", i=4), ACT.Copy), "WT", t)
            for c in range(NCH):
                r = slice(64 * (c % 2), 64 * (c % 2) + 64)
                wait_filled(act, "U", c, 1)
                empty(fn(Un[r, c // 2, 1, :], bank("U", c, 1)[r, 0:256], ACT.Copy), "U", c, 1)
                if c % 2:
                    for par in range(2):
                        wait_filled(act, "Y", c // 2, par)
                        yv = ynat[:, c // 2, :].rearrange("p (i a v) -> p i a v", i=4, a=2)[:, :, par, :]
                        empty(fn(yv, bank("Y", c // 2, par)[:, 0:256].rearrange("p (i v) -> p i v", i=4), ACT.Copy),
                              "Y", c // 2, par)
            for t in range(NT):
                root(48, RW_H, 64, 2)
            for t in range(NT):
                for h in range(2):
                    wait_filled(act, "mT", t, h)
                    empty(fn(featT[:, 4 * h:4 * h + 4, t * P:(t + 1) * P],
                             bank("mT", t, h).rearrange("p (k q) -> p k q", k=4), ACT.Copy), "mT", t, h)

            def resid3(t):
                wait_emptied(act, "wo2", 1, t)
                wait_filled(act, "mT", t, 1)
            squares(3, resid3)
            act.wait_ge(route_ready, 1)
            a.link(fn(rt[:, 480:488], rt[:, 480:488], ACT.Exp))
            fn(rt[:, 488:490], rt[:, 488:490], ACT.Exp).then_inc(exp_ready, 1)

            def moe_group(r, pair, gp):
                n = r * NG + pair * 2 + gp
                base = r * ALLQ + pair * 12 + gp * 6
                act.wait_ge(quads_read, base + 2)
                fn(sg, psum[:, 4, :], ACT.Silu).then_inc(silu_ready, 1)
                act.wait_ge(hT_filled, n + 1)
                fn(hhT.rearrange("p k s -> p (k s)"), psum[:, 7, :], ACT.Copy).then_inc(hT_ready, 1)
                act.wait_ge(quads_read, base + 5)
                fn(dd[:, 0, :], psum[:, 4, :], ACT.Copy).then_inc(d0_ready, 1)

            def moe_round(r):
                with act.Fori(0, NG // 2) as pair:
                    for gp in range(2):
                        moe_group(r, pair, gp)

            act.wait_ge(count_ready, 1)
            moe_round(0)
            most = act.value_load(cnt[0:1, 0:1], min_val=0, max_val=T)
            with act.Fori(1, ROUNDS) as r:
                with act.If(most > r * CAP):
                    moe_round(r)
            squares(4, lambda t: act.wait_ge(resid_ready, t + 1))

        @block.vector
        def _(dve):
            v = Steps(dve, dve_step)
            link = v.link
            empty = lambda ins, *key: v.empty("dve", ins, *key)
            tt, ts, stt = nc.vector.tensor_tensor, nc.vector.tensor_scalar, nc.vector.scalar_tensor_tensor
            red = nc.vector.tensor_reduce

            roots = [0]

            def root(ins, ap):
                ins.then_inc(var_ready, 1)
                roots[0] += 1
                dve.wait_ge(root_ready, roots[0])
                link(nc.vector.reciprocal(ap, ap))

            def norm(n):
                for t in range(NT):
                    dve.wait_ge(rms_ready, NT * n + t + 1)
                    s = st[:, 2 * n + t:2 * n + t + 1]
                    link(nc.vector.reciprocal(s, s))
                    ts(xn[:, t, :], x[:, t, :], s, None, ALU.mult).then_inc(xn_ready, 1)

            def norm_T(n):
                for t in range(NT):
                    for h in range(2):
                        wait_filled(dve, "nt", n, t, h)
                        gain = colp(f"norm{n}")[:, 4 * h:4 * h + 4].unsqueeze(2).to_broadcast([P, 4, P])
                        empty(tt(featT[:, 4 * h:4 * h + 4, t * P:(t + 1) * P],
                                 bank("nt", n, t, h).rearrange("p (k q) -> p k q", k=4), gain, ALU.mult), "nt", n, t, h)

            def bc(ap, n):
                return ap.unsqueeze(len(ap.shape)).to_broadcast([*ap.shape, n])

            for k, e in enumerate((EPS, 1e-5, 64e-5)):
                nc.vector.memset(eps_col[:, k:k + 1], e).then_inc(eps_ready, 1)
            dve.wait_ge(params_in, PARAMS_IN)
            norm(0)
            norm_T(0)
            dve.wait_ge(biasA_in, 16 * 16)
            flat = biasA.rearrange("p h j k -> p (h j) k")
            link(tt(flat, flat, con("winm").unsqueeze(1).to_broadcast([P, 48, 64]), ALU.mult))
            link(tt(flat, flat, con("wina").unsqueeze(1).to_broadcast([P, 48, 64]), ALU.add))
            tmp = area(L1, "prob", 4, 512)[:, 0, :]
            for units_, (s_lo, s_n) in zip((((0, 0, 8), (1, 512, 8)), ((3, 1536, 8), (4, 2048, 2))), QK_SUMS):
                at = s_lo
                sums_of = []
                for u, lo, H in units_:
                    for t in range(NT):
                        wait_emptied(dve, "p1", u, t)
                        q = nat[:, t, lo:lo + 64 * H]
                        link(tt(tmp[:, 0:64 * H], q, q, ALU.mult))
                        s = st[:, at:at + H]
                        at += H
                        sums_of.append(s)
                        ins = red(s, tmp[:, 0:64 * H].rearrange("p (h d) -> p h d", h=H), AX, ALU.add)
                        if at < s_lo + s_n:
                            link(ins)
                root(ins, st[:, s_lo:s_lo + s_n])
                for u, lo, H in units_:
                    for t in range(NT):
                        s = sums_of.pop(0)
                        q3 = nat[:, t, lo:lo + 64 * H].rearrange("p (h d) -> p h d", h=H)
                        if u == 4:
                            dst = kdup[:, t].rearrange("p v (c d) -> p v c d", c=2)
                            tt(dst, q3.unsqueeze(2).to_broadcast([P, 2, 2, 64]), bc(bc(s, 2), 64), ALU.mult)\
                                .then_inc(qk_ready, 1)
                        else:
                            tt(q3, q3, bc(s, 64), ALU.mult).then_inc(qk_ready, 1)

            def softmax_in(i):
                br, t, g = i // 4, i // 2 % 2, i % 2
                for par in range(2):
                    wait_filled(dve, "S", i, par)
                    if i >= 2:
                        wait_filled(dve, "PT", i - 2, par)
                    if br:
                        b = biasB[:, 4 * g + par:4 * g + par + 3:2, P - P * t:P - P * t + T]
                    else:
                        b = biasA[:, 4 * g + par:4 * g + par + 3:2, 2 - 2 * t:6 - 2 * t, :].rearrange("p h j k -> p h (j k)")
                    pr = prob[:, i % 2, par]
                    empty(stt(pr, bank("S", i, par).rearrange("p (a k) -> p a k", a=2), HD ** -0.5, b, ALU.mult, ALU.add),
                          "S", i, par)
                    k = 4 * i + 2 * par
                    m = negmax[:, k:k + 2]
                    link(red(m, pr, AX, ALU.max))
                    if br:
                        sk = row("sink")[:, 4 * g + par:4 * g + par + 3:2]
                        link(tt(m, m, sk, ALU.max))
                        link(tt(esink[:, k:k + 2], sk, m, ALU.subtract))
                    ts(m, m, -1.0, None, ALU.mult).then_inc(max_ready, 1)

            def weighted(i):
                br, t, g = i // 4, i // 2 % 2, i % 2
                wait_filled(dve, "PT", i, 1)
                empty(nc.vector.tensor_copy(probT[:, 2 * (i % 2) + 1].rearrange("p a k q -> p (a k q)"), bank("PT", i, 1)),
                      "PT", i, 1)
                s = sums[:, 4 * i:4 * i + 4]
                dve.wait_ge(exp_ready, 2 * i + 2)
                if br:
                    link(tt(s, s, esink[:, 4 * i:4 * i + 4], ALU.add))
                link(nc.vector.reciprocal(s, s))
                wait_filled(dve, "PV", i)
                dst = xn[:, t, 512 * br + 256 * g:512 * br + 256 * g + 256].rearrange("p (a b d) -> p a b d", a=2, b=2)
                empty(tt(dst, bank("PV", i)[:, 0:256].rearrange("p (a b d) -> p a b d", a=2, b=2),
                         bc(s.rearrange("p (b a) -> p a b", b=2), 64), ALU.mult), "PV", i)

            for i in range(9):
                if i == 1:
                    dve.wait_ge(t5_stored, 16)
                if i == 4:
                    dve.wait_ge(biasB_in, 16)
                if i < 8:
                    softmax_in(i)
                if i >= 1:
                    weighted(i - 1)
            for br in range(2):
                for t in range(NT):
                    for n in range(2):
                        wait_filled(dve, "br", br, t, n)
                        wait_emptied(dve, "p1", 8, 1)
                        g = sig[:, t, 1024 * br + 512 * n:1024 * br + 512 * n + 512]
                        empty(tt(g, g, bank("br", br, t, n), ALU.mult), "br", br, t, n)
                        if br:
                            ya = sig[:, t, 512 * n:512 * n + 512]
                            tt(ya, ya, g, ALU.add).then_inc(y_ready, 1)

            def add_resid(name):
                for n in range(2):
                    for t in range(NT):
                        wait_filled(dve, name, n, t)
                        xs = x[:, t, 512 * n:512 * n + 512]
                        empty(tt(xs, xs, bank(name, n, t), ALU.add), name, n, t)

            add_resid("wo")
            norm(1)
            norm_T(1)
            for u in range(FFK // 2):
                wait_filled(dve, "up", u)
                wait_emptied(dve, "gate", u)
                empty(tt(hT[:, 2 * u:2 * u + 2, :].rearrange("p f t -> p (f t)"), silu_t[:, u % 2, :], bank("up", u), ALU.mult),
                      "up", u)
            for t in range(NT):
                for n in range(2):
                    wait_filled(dve, "down", t, n)
                    xs = x[:, t, 512 * n:512 * n + 512]
                    empty(tt(xs, xs, bank("down", t, n), ALU.add), "down", t, n)

            link(nc.vector.memset(fT[:, :, 0:1], 0.0))
            norm(2)
            norm_T(2)

            def lerp(c0, n):
                wait_emptied(dve, "rw", c0 // 2 + (n - 1) // 2)
                cur = fT[:, c0:c0 + n, 1:257]
                link(tt(dtmp[:, 0:n, :], fT[:, c0:c0 + n, 0:256], cur, ALU.subtract))
                for c in range(n):
                    link(stt(fT[:, c0 + c, 1:257], dtmp[:, c, :], colp("mu", c0 + c), fT[:, c0 + c, 1:257],
                             ALU.mult, ALU.add))

            def percol(name):
                return bc(colp(name), T)

            lerp(12, 2)
            dve.sem_inc(lerp_ready, 1)
            lerp(4, 4)
            tt(kk, f_k, percol("k_k"), ALU.mult).then_inc(kk_ready, 1)
            lerp(0, 4)
            lerp(8, 4)
            wait_emptied(dve, "z", 1)
            for c in range(4):
                link(nc.vector.tensor_tensor_scan(Ls[:, c, :], con("reset"), sw[:, c, :], 0.0, ALU.mult, ALU.add))
            tt(Le, Ls, sw, ALU.subtract).then_inc(scan_ready, 1)
            wait_emptied(dve, "ss", 1)
            link(ts(kk2, kk2, 1e-12, None, ALU.max))
            link(nc.vector.reciprocal(kk2, kk2))
            link(tt(kk, kk, kk2, ALU.mult))
            wait_emptied(dve, "za", 1)
            for c in range(4):
                link(ts(dtmp[:, c, :], sa[:, c, :], 1.0, colp("k_a", c), ALU.subtract, ALU.mult))
            link(stt(kp, dtmp, 1.0, f_k, ALU.add, ALU.mult))
            link(tt(rk, f_r, kp, ALU.mult))
            link(tt(rk, rk, percol("r_k"), ALU.mult))
            link(tt(sa, kk, sa, ALU.mult))
            dve.wait_ge(decay_ready, 1)
            link(nc.vector.tensor_copy(PC[:], Ein.rearrange("p f (c s) -> p f c s", c=NCH)[:, :, :, CH - 1]))
            link(stt(At, kk, -1.0, Eex, ALU.mult, ALU.mult))
            link(tt(Bt, sa, Einv, ALU.mult))
            link(tt(f_k, kp, Einv, ALU.mult))
            link(tt(f_r, f_r, Ein, ALU.mult))
            for dst, src in ((BhT, Bt), (KhT, f_k)):
                for c in range(4):
                    ins = tt(dst[:, c, :].rearrange("p (c s) -> p c s", c=NCH), src[:, c, :].rearrange("p (c s) -> p c s", c=NCH),
                             bc(PC[:, c, :], CH), ALU.mult)
                    link(ins)
            dve.sem_inc(rw_ready, 1)
            for t in range(NT):
                wait_emptied(dve, "p2", 1, t)
                if t == 0:
                    wait_filled(dve, "nt", 2, 1, 1)
                xy = retn[:, t, 0:1024].rearrange("p (h c d) -> p h c d", h=8, c=2)
                x1, x2 = xy[:, :, 0, :], xy[:, :, 1, :]
                w4 = xn[:].rearrange("p t (a h d) -> p (t a) h d", a=2, h=8)
                cos = con("cos")[:, 64 * t:64 * t + 64].unsqueeze(1).to_broadcast([P, 8, 64])
                sin = con("sin")[:, 64 * t:64 * t + 64].unsqueeze(1).to_broadcast([P, 8, 64])
                link(tt(w4[:, 0], x1, cos, ALU.mult))
                link(tt(w4[:, 1], x2, sin, ALU.mult))
                link(tt(w4[:, 2], x1, sin, ALU.mult))
                link(tt(w4[:, 3], x2, cos, ALU.mult))
                link(tt(x1, w4[:, 0], w4[:, 1], ALU.subtract))
                tt(x2, w4[:, 2], w4[:, 3], ALU.add).then_inc(rot_ready, 1)
            for j in range(3):
                wait_filled(dve, "rs", j)
                dst = featT[:, 2 * j:2 * j + 2, :].rearrange("p a b -> p (a b)")
                lo = CST["dec"][0] + 512 * j
                empty(tt(dst, bank("rs", j), cst[:, lo:lo + 512], ALU.mult), "rs", j)

            def head_norm(y, work, H, src, emptied_key):
                d = 512 // H
                per = lambda ap: ap.rearrange("p (h d) -> p h d", h=H)
                s = st[:, 32:32 + H]
                q = st[:, 48:48 + H]
                link(red(s, per(src), AX, ALU.add))
                link(ts(s, s, 1.0 / d, None, ALU.mult))
                ins = tt(per(y), per(src), bc(s, d), ALU.subtract)
                if emptied_key:
                    empty(ins, *emptied_key)
                else:
                    link(ins)
                link(tt(work, y, y, ALU.mult))
                root(red(q, per(work), AX, ALU.add), q)
                link(tt(per(y), per(y), bc(q, d), ALU.mult))

            dve.wait_ge(rot_ready, NT)
            for t in range(NT):
                wait_filled(dve, "ro", t)
                y = xn[:, t, 0:512]
                head_norm(y, xn[:, t, 512:1024], RET_H, bank("ro", t), ("ro", t))
                link(tt(y, y, row("ret_gn"), ALU.mult))
                wait_emptied(dve, "p2", 3, t)
                tt(y, y, retn[:, t, 1536:2048], ALU.mult).then_inc(mixed_ready, 1)
            wait_filled(dve, "bonus")
            empty(nc.vector.tensor_copy(bonus, bank("bonus")[:, 0:16]), "bonus")

            def masked(dst, name, m, t, par, last):
                mask = con(m).unsqueeze(1).to_broadcast([P, 4, P])
                ins = tt(dst[:, t, 4 * par:4 * par + 4, :], bank("mat", name, t, par).rearrange("p (i q) -> p i q", i=4),
                         mask, ALU.mult)
                if last:
                    empty(ins, "mat", name, t, par)

            def mat(name, *outs):
                for t in range(NT):
                    for par in range(2):
                        wait_filled(dve, "mat", name, t, par)
                        for n, (dst, m) in enumerate(outs):
                            masked(dst, name, m, t, par, n == len(outs) - 1)

            dve.wait_ge(mixed_ready, NT)
            mat("AT", (AdT, "mAdT"), (o16T, "m16T"), (o32T, "m32T"))
            for t in range(NT):
                for par in range(2):
                    wait_filled(dve, "mat", "A", t, par)
                    masked(Ad, "A", "mAd", t, par, True)
                    hs = slice(4 * par, 4 * par + 4)
                    tt(X[:, t, hs, :], Ad[:, t, hs, :], ident.unsqueeze(1).to_broadcast([P, 4, P]), ALU.add)\
                        .then_inc(x0_ready, 1)
            dst = {"P2T": P2T, "P4T": P4T}
            extra = {"Aak": (AakT, "mlt"), "Arb": (ArbT, "mle"), "Ark": (ArkT, "mle")}
            for name, who in INVERSE:
                if who == "dve":
                    for t in range(NT):
                        for par in range(2):
                            key = ("inv", name, t, par)
                            wait_filled(dve, *key)
                            hs = slice(4 * par, 4 * par + 4)
                            flat = lambda m: m[:, t, hs, :].rearrange("p i q -> p (i q)")
                            if name in dst:
                                empty(nc.vector.tensor_copy(flat(dst[name]), bank(*key)), *key)
                            else:
                                dve.wait_ge(x0_ready, 2 * t + par + 1)
                                empty(tt(flat(X), flat(X), bank(*key), ALU.add), *key)
                for e in INV_EXTRA.get(name, ()):
                    mat(e, extra[e])
            for c in range(NCH):
                r = slice(64 * (c % 2), 64 * (c % 2) + 64)
                wait_filled(dve, "U", c, 0)
                empty(nc.vector.tensor_copy(Un[r, c // 2, 0, :], bank("U", c, 0)[r, 0:256]), "U", c, 0)
                if c < NCH - 1:
                    wait_filled(dve, "St", c)
                    b = bank("St", c)[:, 0:256].rearrange("p (i v) -> p i v", v=64)
                    if c == 0:
                        empty(nc.vector.tensor_copy(S[:, 1], b), "St", 0)
                    else:
                        link(tt(S[:, c + 1], S[:, c], bc(PC[:, :, c], 64), ALU.mult))
                        empty(tt(S[:, c + 1], S[:, c + 1], b, ALU.add), "St", c)
            for t in range(NT):
                for par in range(2):
                    wait_emptied(dve, "Y", t, par)
                y, w = ynat[:, t, :], ytmp[:, t, :]
                per = lambda ap: ap.rearrange("p (h d) -> p h d", h=RW_H)
                head_norm(y, w, RW_H, y, None)
                link(tt(y, y, row("rw_gn"), ALU.mult))
                link(tt(per(w), per(natl["V"][:, t, :]), bc(bonus[:, 8 * t:8 * t + 8], 64), ALU.mult))
                link(tt(y, y, w, ALU.add))
                wait_emptied(dve, "gn", t)
                tt(xn[:, t, 512:1024], y, gnat[:, t, :], ALU.mult).then_inc(mixed_ready, 1)
            add_resid("wo2")
            norm(3)
            norm_T(3)
            at = [192]

            def work(*shape):
                n = int(np.prod(shape))
                ap = rt[:, at[0]:at[0] + n]
                at[0] += n
                if len(shape) == 2:
                    ap = ap.rearrange("p (a b) -> p a b", a=shape[0])
                if len(shape) == 3:
                    ap = ap.rearrange("p (a b c) -> p a b c", a=shape[0], b=shape[1])
                return ap

            lg = work(NT, 36)
            ml = work(NT, E)
            eq = work(NT, E)
            oh1 = work(NT, E)
            oh4 = work(NT, 4)
            c4 = work(NT, 4)
            assert at[0] <= 480
            e4 = rt[:, 480:488].rearrange("p (a b) -> p a b", a=NT)
            e2 = rt[:, 488:490]
            gm, m1, m2, cm, gp, w1, w2 = (rt[:, 496 + 2 * n:498 + 2 * n] for n in range(7))
            oh2 = rt[:, 512:576].rearrange("p (t e) -> p t e", t=NT)
            for t in range(NT):
                wait_filled(dve, "logit", t)
                empty(tt(lg[:, t, :], bank("logit", t)[:, 0:36], row("brt"), ALU.add), "logit", t)

            def first_max(dst, vals, mx, scratch_, desc, n):
                link(red(mx, vals, AX, ALU.max))
                link(tt(scratch_, vals, bc(mx, n), ALU.is_equal))
                link(tt(scratch_, scratch_, con(desc).unsqueeze(1).to_broadcast([P, NT, n]), ALU.mult))
                link(red(cm, scratch_, AX, ALU.max))
                link(tt(dst, scratch_, bc(cm, n), ALU.is_equal))

            l4, l32 = lg[:, :, 0:4], lg[:, :, 4:36]
            first_max(oh4, l4, gm, c4, "desc4", 4)
            link(tt(e4, l4, bc(gm, 4), ALU.subtract))
            link(tt(ml.rearrange("p t (g e) -> p t g e", g=4), l32.rearrange("p t (g e) -> p t g e", g=4), bc(oh4, 8), ALU.mult))
            link(ts(c4, oh4, 1.0, -NEG, ALU.subtract, ALU.mult))
            ml4 = ml.rearrange("p t (g e) -> p t g e", g=4)
            link(tt(ml4, ml4, bc(c4, 8), ALU.add))
            first_max(oh1, ml, m1, eq, "desc32", E)
            link(stt(ml, oh1, 3 * NEG, ml, ALU.mult, ALU.add))
            first_max(oh2, ml, m2, eq, "desc32", E)
            link(tt(e2, m2, m1, ALU.subtract))
            tt(selr, oh1, oh2, ALU.add).then_inc(route_ready, 1)
            dve.wait_ge(exp_ready, 16 + 1)
            link(red(gp, e4, AX, ALU.add))
            link(nc.vector.reciprocal(gp, gp))
            link(ts(w1, e2, 1.0, None, ALU.add))
            link(nc.vector.reciprocal(w1, w1))
            link(tt(w1, w1, gp, ALU.mult))
            link(tt(w2, w1, e2, ALU.mult))
            link(tt(oh1, oh1, bc(w1, E), ALU.mult))
            link(tt(oh2, oh2, bc(w2, E), ALU.mult))
            link(tt(comb, oh1, oh2, ALU.add))
            for t in range(NT):
                wait_filled(dve, "rank", t)
                dve.wait_ge(route_ready, 1)
                link(ts(rank[:, t, :], bank("rank", t)[:, 0:E], 1000.0, None, ALU.add))
                empty(stt(rank[:, t, :], rank[:, t, :], 1.0, selr[:, t, :], ALU.mult, ALU.mult), "rank", t)
                link(ts(rank[:, t, :], rank[:, t, :], -1000.0, None, ALU.add))
            wait_filled(dve, "count")
            empty(red(rt[:, 492:493], bank("count")[:, 0:E], AX, ALU.max), "count")
            nc.vector.tensor_copy(cnt[:, 0:1], rt[:, 492:493]).then_inc(count_ready, 1)
            dve.wait_ge(mixed_ready, 2 * NT)
            link(nc.vector.memset(dd, 0.0))
            nc.vector.memset(GT, 0.0).then_inc(gt_ready, 1)

            def moe_group(r, pair, gp_):
                n = r * NG + pair * 2 + gp_
                base = r * ALLQ + pair * 12 + gp_ * 6
                e0 = pair * (2 * EG) + gp_ * EG
                es = slice(e0, e0 + EG) if isinstance(e0, int) else bass.ds(e0, EG)
                s0 = moe_base + n * MOE_STEPS
                nc.vector.tensor_copy(rank4.rearrange("p (t e) -> p t e", t=NT), rank[:, :, es]).then_inc(dve_step, 1)
                nc.vector.tensor_copy(comb4.rearrange("p (t e) -> p t e", t=NT), comb[:, :, es]).then_inc(dve_step, 1)
                dve.wait_ge(dve_step, s0 + 2)
                slots = con("slot").unsqueeze(1).to_broadcast([P, NT * EG, CAP])
                flat = lambda m: m.rearrange("p t e s -> p (t e) s")
                tt(flat(G), slots, bc(rank4, CAP), ALU.is_equal).then_inc(dve_step, 1)
                dve.wait_ge(dve_step, s0 + 3)
                ins = tt(flat(Gw), flat(G), bc(comb4, CAP), ALU.mult)
                ins.then_inc(onehot_ready, 1)
                for kb in range(2):
                    dve.wait_ge(gathered, 2 * n + kb + 1)
                    gain = bc(colp("norm3")[:, 4 * kb:4 * kb + 4], P)
                    tt(xg[:, 4 * kb:4 * kb + 4, :], psum[:, 6 + kb, :].rearrange("p (k s) -> p k s", k=4), gain, ALU.mult)\
                        .then_inc(xg_ready, 1)
                dve.wait_ge(quads_read, base + 4)
                dve.wait_ge(silu_ready, n + 1)
                tt(hh, sg, psum[:, 5, :], ALU.mult).then_inc(h_ready, 1)
                dve.wait_ge(gt_filled, n + 1)
                dve.wait_ge(scattered, n + 1)
                nc.vector.tensor_copy(GT.rearrange("p t q -> p (t q)"), psum[:, 6, 0:2 * P]).then_inc(gt_ready, 1)
                dve.wait_ge(quads_read, base + 6)
                nc.vector.tensor_copy(dd[:, 1, :], psum[:, 5, :]).then_inc(d1_ready, 1)

            MOE_STEPS = 3
            moe_base = v.n

            def moe_round(r):
                with dve.Fori(0, NG // 2) as pair:
                    for g in range(2):
                        moe_group(r, pair, g)

            dve.wait_ge(gt_ready, 1)
            moe_round(0)
            dve.wait_ge(count_ready, 1)
            most = dve.value_load(cnt[0:1, 0:1], min_val=0, max_val=T)
            with dve.Fori(1, ROUNDS) as r:
                with dve.If(most > r * CAP):
                    ts(rank, rank, -float(CAP), None, ALU.add).then_inc(shifted, 1)
                    dve.wait_ge(shifted, r)
                    nc.vector.memset(rt[:, 495:496], 0.0)
                    moe_round(r)
            dve.wait_ge(moe_done, 1)
            for t in range(NT):
                for n in range(2):
                    xs = x[:, t, 512 * n:512 * n + 512]
                    tt(xs, xs, psum[:, 2 * t + n, :], ALU.add).then_inc(sum_done, 1)
                dve.wait_ge(sum_done, 2 * t + 2)
                dve.sem_inc(resid_ready, 1)
            dve.wait_ge(gain_in, 16)
            for t in range(NT):
                dve.wait_ge(rms_ready, NT * 4 + t + 1)
                s = st[:, 8 + t:9 + t]
                nc.vector.reciprocal(s, s).then_inc(sum_done, 1)
                dve.wait_ge(sum_done, 4 + t + 1)
                gain = featT[:, 0:4, :].rearrange("p a b -> p (a b)")
                stt(xn[:, t, :], x[:, t, :], s, gain, ALU.mult, ALU.mult).then_inc(out_ready, 1)


def kernel(**inputs):
    import concourse.bacc as _bacc
    from concourse.bass_utils import run_bass_kernel_spmd as _run

    g = {k: np.asarray(v) for k, v in inputs.items()}
    pk = lambda a: np.ascontiguousarray(a.reshape(-1, P).T)
    two = lambda a: np.concatenate([a[0], a[0]])[:, None]
    arrays = {
        "x": g["x"][0],
        "cst": constants(),
        "onehot": t5_one_hot(),
        "cols": np.concatenate([
            pk(g["norm_mix"][0]), pk(g["norm_ffn"][0]), pk(g["norm1_gain_2"][0]), pk(g["norm2_gain_2"][0]),
            two(g["q_norm_a"]), two(g["k_norm_a"]), two(g["q_norm_b"]), two(g["k_norm_b"]),
            pk(g["rwkv_mu_2"][0]), pk(g["rwkv_w0_2"][0]), pk(g["rwkv_a0_2"][0]), pk(g["rwkv_k_k_2"][0]),
            pk(g["rwkv_k_a_2"][0]), pk(g["rwkv_r_k_2"][0].reshape(-1))], 1),
        "rows": np.concatenate([g["sink_b"][0], g["b_route_group_2"][0], g["b_route_expert_2"][0],
                                g["ret_gn_gain_2"][0], g["rwkv_gn_gain_2"][0]])[None, :],
        "final_gain": g["final_norm_gain_2"][None, :],
        "rpb": g["rpb_a"][0].transpose(2, 0, 1).reshape(8, -1),
        "t5": np.concatenate([g["t5_table"], np.ones((1, 8), np.float32)]),
        "lora": np.concatenate([g["rwkv_w_up_2"][0], g["rwkv_a_up_2"][0]]),
        "gup": g["rwkv_g_up_2"][0],
        "wr": np.concatenate([g["w_route_group_2"][0], g["w_route_expert_2"][0]], 1),
    }
    for name in ("w_in", "w_branch_a", "w_branch_b", "w_out", "w_gate", "w_up", "w_down", "w_in_2", "w_out_2",
                 "w_gate_2", "w_up_2", "w_down_2"):
        arrays[name] = g[name][0]
    arrays = {k: np.ascontiguousarray(a) for k, a in arrays.items()}
    nc = _bacc.Bacc("TRN2", target_bir_lowering=False, num_devices=1)
    A = {k: nc.dram_tensor(f"in_{k}", a.shape, F32, kind="ExternalInput").ap() for k, a in arrays.items()}
    out = nc.dram_tensor("out", (T, D), F32, kind="ExternalOutput").ap()
    build(nc, A, out)
    r = _run(nc, [{f"in_{k}": a for k, a in arrays.items()}], core_ids=[0])
    return r.results[0]["out"].reshape(1, T, D)
```

```python
from contextlib import ExitStack

import numpy as np

import concourse.bass as bass
from concourse import mybir

F32 = mybir.dt.float32
F32R = mybir.dt.float32r
I32 = mybir.dt.int32
ALU = mybir.AluOpType
ACT = mybir.ActivationFunctionType
AX = mybir.AxisListType.X

P = 128
T = 256
NT = T // P
D = 1024
DK = D // P
HD = 64
GRID_W = 64
EPS = 1e-6
NEG = -1e30

A_W = 512
NQKV = 3 * A_W + 512 + 256
FFN = 2816
FFK = FFN // P
REL = 2 * T - 1
EXT = T + P
KW = 16
RET_H, RET_D = 4, 128
RW_H = 8
CH = 64
NCH = T // CH
DECAY = float(np.exp(-0.5))
FTC = 14
E = 32
EG = 4
CAP = 32
NG = E // EG
DE = 512
ROUNDS = T // CAP
QK_SUMS = ((192, 32), (224, 20))

SLOT = 4096
NSLOT = 3
QUAD = 2 * SLOT
NQ = 4
B0 = NSLOT * SLOT


def layout(*fields, base=0):
    at, out = base, {}
    for name, size in fields:
        out[name] = (at, at + size)
        at += size
    out["end"] = at
    return out


L1 = layout(("nat", NT * NQKV), ("sig", NT * 2048), ("biasA", 8 * 6 * 64), ("biasB", 8 * EXT),
            ("qaT", 1024), ("kaT", 1024), ("qbT", 1024), ("kbT", 512), ("prob", 2048), ("probT", 2048),
            ("spare", 2048), base=B0)
LF = layout(("hTh", FFK * T), ("hTl", FFK * T), ("silu", 1024), base=B0)
LM = layout(("M", 14 * 1024), ("fT", FTC * 257), ("RT", 2048), ("gap", 498), ("N", 4096), base=B0)
LE = layout(("G", 256), ("Gw", 256), ("GT", 256), ("sg", 512), ("h", 512), ("hT", 512), base=NQ * QUAD)
ARENA = max(L1["end"], LM["end"], LE["end"])
CHUNK = 2048


def place(lo):
    return (lo, lo + CHUNK // 2)


W_SIG = (place(L1["sig"][0]), place(L1["sig"][0] + CHUNK))
W_QK = place(L1["qaT"][0])
W_NAT = (L1["nat"][0], L1["nat"][0] + NQKV)
W_PROB, W_PROBT, W_SPARE = (place(L1[n][0]) for n in ("prob", "probT", "spare"))
W_FFN = place(LF["end"])
assert LM["N"] == (W_PROBT[0], W_SPARE[0] + CHUNK) and L1["prob"][0] >= LF["end"] + CHUNK

CST = layout(("ident", 128), ("reset", T), ("winm", 64), ("wina", 64), ("slot", CAP), ("desc4", 4), ("desc32", 32),
             ("mAdT", 128), ("mAd", 128), ("m16T", 128), ("m32T", 128), ("mlt", 128), ("mle", 128),
             ("same", 128), ("sel", 2), ("before", 128), ("ones", 128), ("cos", 128), ("sin", 128),
             ("dec", 1536))
COLS = layout(("norm0", 8), ("norm1", 8), ("norm2", 8), ("norm3", 8), ("qa", 1), ("ka", 1), ("qb", 1), ("kb", 1),
              ("mu", FTC), ("w0", 4), ("a0", 4), ("k_k", 4), ("k_a", 4), ("r_k", 4))
ROWS = layout(("sink", 8), ("brt", 36), ("ret_gn", 512), ("rw_gn", 512))


def constants():
    c = np.zeros((P, CST["end"]), np.float32)

    def put(name, a):
        lo, hi = CST[name]
        c[:, lo:hi] = np.asarray(a, np.float32).reshape(P, hi - lo)

    p, i = np.arange(P)[:, None], np.arange(P)[None, :]
    put("ident", p == i)
    put("reset", np.broadcast_to(np.arange(T) % CH != 0, (P, T)))
    col, key = p % GRID_W, np.arange(GRID_W)[None, :]
    start = np.clip(col - KW // 2, 0, GRID_W - KW)
    win = (key >= start) & (key < start + KW)
    put("winm", win)
    put("wina", np.where(win, 0.0, NEG))
    put("slot", np.broadcast_to(np.arange(CAP), (P, CAP)))
    put("desc4", np.broadcast_to(np.arange(4, 0, -1), (P, 4)))
    put("desc32", np.broadcast_to(np.arange(32, 0, -1), (P, 32)))
    put("mAdT", (p < i) & (p // 16 == i // 16))
    put("mAd", (i < p) & (p // 16 == i // 16))
    put("m16T", (p < i) & (p // 32 == i // 32) & (p // 16 != i // 16))
    put("m32T", (p < i) & (p // 64 == i // 64) & (p // 32 != i // 32))
    put("mlt", (p < i) & (p // 64 == i // 64))
    put("mle", (p <= i) & (p // 64 == i // 64))
    put("same", p // 64 == i // 64)
    put("sel", p // 64 == np.arange(2)[None, :])
    put("before", p < i)
    put("ones", np.ones((P, P)))
    half = RET_D // 2
    inv = np.float32(10000.0) ** (-np.arange(half, dtype=np.float32) / np.float32(half))
    ang = np.arange(T, dtype=np.float32)[:, None] * inv[None, :]
    tile = lambda a: a.reshape(NT, P, -1).transpose(1, 0, 2)
    put("cos", tile(np.cos(ang)))
    put("sin", tile(np.sin(ang)))
    logg = np.log(1.0 - np.exp2(-5.0 - np.arange(RET_H)))
    t = np.arange(T)
    seen = (t[:, None] // CH) <= (t[None, :] // CH)
    dec = np.exp(logg[:, None, None] * np.abs(t[None, :, None] - t[None, None, :])) * seen * RET_D ** -0.5
    first = dec[:, :P, :].transpose(1, 0, 2).reshape(P, -1)
    second = dec[:, P:, P:].transpose(1, 0, 2).reshape(P, -1)
    put("dec", np.concatenate([first, second], 1))
    return c


def t5_one_hot():
    rel = np.arange(-(T - 1), T)
    half, exact = 16, 8
    n = np.abs(rel)
    large = exact + (np.log(np.maximum(n, 1) / exact) / np.log(128 / exact) * (half - exact)).astype(np.int32)
    bucket = (rel > 0) * half + np.where(n < exact, n, np.minimum(large, half - 1))
    m = np.zeros((33, REL), np.float32)
    m[bucket, np.arange(REL)] = 1.0
    m[32] = np.where(n <= 128, 0.0, NEG)
    return m


def plan_fills():
    f = []

    def add(who, *key):
        f.append((key, who))

    def norm(n):
        for t in range(NT):
            for b in range(2):
                add("dve", "nt", n, t, b)

    def turn_qk(*names):
        for s in names:
            for t in range(NT):
                add("act", "qkT", s, t)

    norm(0)
    for u in range(5):
        if u == 4:
            turn_qk("qa", "ka")
        for c in range(1 if u == 4 else 2):
            add("act", "p1", u, c)
        if u == 2:
            add("act", "t5")
    for i in range(9):
        if i < 8:
            add("dve", "S", i, 0)
            add("dve", "S", i, 1)
        if i >= 1:
            add("act", "PT", i - 1, 0)
            add("dve", "PT", i - 1, 1)
        if i < 8:
            if i == 0:
                turn_qk("qb", "kb")
            add("act", "p1", 5 + i // 2, i % 2)
        if i == 8:
            for key in ((0, 0), (0, 1), (1, 0)):
                add("dve", "oT", *key)
        if i >= 1:
            add("dve", "PV", i - 1)
    for br in range(2):
        if br == 1:
            add("dve", "oT", 1, 1)
        for n in range(2):
            for t in range(NT):
                add("dve", "br", br, n, t)
    for b in range(2):
        for t in range(NT):
            add("dve", "yT", t, b)
    for n in range(2):
        for c in range(2):
            add("dve", "wo", n, c)
    norm(1)
    for u in range(FFK // 2):
        add("act", "gate", u)
        add("dve", "up", u)
    for t in range(NT):
        for n in range(2):
            add("dve", "down", t, n)
    norm(2)
    for c in RW_ORDER:
        add("act", "rw", c)
        if c == 3:
            for k in ("z", "za"):
                for b in range(2):
                    add("act", k, b)
        if c == 0:
            for b in range(2):
                add("act", "ss", b)
    for u in range(3):
        for c in range(2):
            add("act", "p2", u, c)
    for s in ("q", "k"):
        for t in range(NT):
            add("act", "rT", s, t)
    for j in range(3):
        add("dve", "rs", j)
    add("act", "p2", 3, 0)
    for t in range(NT):
        add("dve", "ro", t)
    add("act", "p2", 3, 1)
    for w in ("A", "B", "K", "V"):
        for t in range(NT):
            add("act", "natl", w, t)
    add("dve", "bonus")
    for m in ("AT", "A"):
        for t in range(NT):
            for par in range(2):
                add("dve", "mat", m, t, par)
    for n, (name, who) in enumerate(INVERSE):
        for t in range(NT):
            for par in range(2):
                add(who, "inv", name, t, par)
        for extra in INV_EXTRA.get(name, ()):
            for t in range(NT):
                for par in range(2):
                    add("dve", "mat", extra, t, par)
        if name == "Z2":
            for t in range(NT):
                add("act", "Q", t)
            for t in range(NT):
                add("act", "gn", t)
    for t in range(NT):
        add("act", "WT", t)
    for c in range(NCH):
        add("dve", "U", c, 0)
        add("act", "U", c, 1)
        for t, par in Y_AFTER.get(c, ()):
            add("act", "Y", t, par)
        if c < NCH - 1:
            add("dve", "St", c)
    for t in range(NT):
        for b in range(2):
            add("act", "mT", t, b)
    for n in range(2):
        for t in range(NT):
            add("dve", "wo2", n, t)
    norm(3)
    for t in range(NT):
        add("dve", "logit", t)
    for t in range(NT):
        add("dve", "rank", t)
    add("dve", "count")
    return f


Y_AFTER = {2: ((0, 0),), 3: ((0, 1), (1, 0), (1, 1))}
RW_ORDER = (6, 2, 3, 0, 1, 4, 5)
INVERSE = (("P2", "act"), ("P2T", "dve"), ("X1", "dve"), ("P4", "act"), ("P4T", "dve"), ("X2", "dve"),
           ("P8T", "act"), ("X3", "dve"), ("T16T", "act"), ("Z1", "act"), ("X4", "dve"), ("T32T", "act"),
           ("Z2", "act"), ("X5", "dve"), ("TT", "act"))
INV_EXTRA = {"X3": ("Aak",), "T32T": ("Arb",), "TT": ("Ark",)}


def build(nc, A, out):
    fills = plan_fills()
    index = {key: n for n, (key, _) in enumerate(fills)}
    turn, seen = {}, {"act": 0, "dve": 0}
    for key, who in fills:
        turn[key] = seen[who]
        seen[who] += 1
    who_of = dict(fills)

    with ExitStack() as ctx:
        def sb(name, shape, dt=F32):
            return ctx.enter_context(nc.sbuf_tensor(name, shape, dt))

        def sem(name):
            return ctx.enter_context(nc.semaphore(name))

        def sb_rounded(name, shape):
            offset = -(-nc.sbuf_base // 32) * 32
            whole = sb(name, shape)
            return whole, nc.alloc_sbuf_tensor_at(name + "_rounded", shape, F32R, offset=offset)

        arena_at = -(-nc.sbuf_base // 32) * 32
        arena = sb("arena", [P, ARENA])
        ring_r = nc.alloc_sbuf_tensor_at("ring_rounded", [P, NSLOT * SLOT], F32R, offset=arena_at)
        hi_r = {hi: nc.alloc_sbuf_tensor_at(f"hi_rounded_{n}", [P, 2 * (hi[1] - hi[0])], F32R, offset=arena_at + 4 * hi[0])
                for n, hi in enumerate((*W_SIG, W_QK, W_NAT, W_PROB, W_PROBT, W_SPARE, W_FFN))}
        x = sb("x", [P, NT, D])
        xn = sb("xn", [P, NT, D])
        featT, featR = sb_rounded("featT", [P, DK, T])
        featL, featLR = sb_rounded("featL", [P, DK, T])
        cst = sb("cst", [P, CST["end"]])
        cols = sb("cols", [P, COLS["end"]])
        rows = sb("rows", [P, ROWS["end"]])
        lora = sb("lora", [P, 512])
        gup = sb("gup", [P, 512])
        wr = sb("wr", [P, DK, 36])
        t5b = sb("t5b", [33, 8])
        st = sb("st", [P, 512])
        rt = sb("rt", [P, 1024])
        cnt = sb("cnt", [P, 2], I32)
        psum = ctx.enter_context(nc.psum_tensor("psum", [P, 8, 512], F32))

        def area(lay, name, *shape, of=None):
            lo, hi = lay[name]
            v = (arena if of is None else of)[:, lo:hi]
            if len(shape) == 2:
                v = v.rearrange("p (a b) -> p a b", a=shape[0])
            elif len(shape) == 3:
                v = v.rearrange("p (a b c) -> p a b c", a=shape[0], b=shape[1])
            elif len(shape) == 4:
                v = v.rearrange("p (a b c d) -> p a b c d", a=shape[0], b=shape[1], c=shape[2])
            return v

        def piece(lo, *shape, of=None):
            n = int(np.prod(shape))
            return area({"v": (lo, lo + n)}, "v", *shape, of=of)

        def con(name):
            lo, hi = CST[name]
            return cst[:, lo:hi]

        def colp(name, k=None):
            lo, hi = COLS[name]
            return cols[:, lo:hi] if k is None else cols[:, lo + k:lo + k + 1]

        def row(name):
            lo, hi = ROWS[name]
            return rows[:, lo:hi]

        ident = con("ident")
        nat = area(L1, "nat", NT, NQKV)
        sig = area(L1, "sig", NT, 2048)
        biasA = area(L1, "biasA", 8, 6, 64)
        biasB = area(L1, "biasB", 8, EXT)
        qaT, kaT, qbT = (area(L1, n, 4, T) for n in ("qaT", "kaT", "qbT"))
        kbT = area(L1, "kbT", 2, T)
        kdup = piece(L1["prob"][0] + 1024, NT, 2, P)
        negmax, esink, sums = (st[:, 64 + 32 * n:96 + 32 * n] for n in range(3))
        bonus = st[:, 160:176]
        eps_col = st[:, 176:179]
        warm = sb("warm", [P, 1])
        tanh_w = sb("tanh_w", [64, T])
        sig_g = sb("sig_g", [P, T])
        prob = area(L1, "prob", 2, 2, 2, T)
        probT = area(L1, "probT", 4, 2, 2, P)
        onehot = arena[0:33, L1["biasB"][0]:L1["biasB"][0] + REL]
        tb_sb = arena[0:8, L1["biasB"][0] + 512:L1["biasB"][0] + 512 + REL]
        hTh, hTl = (area(LF, n, FFK, T) for n in ("hTh", "hTl"))
        hT_parts = [nc.alloc_sbuf_tensor_at(n + "_rounded", [P, FFK, T], F32R, offset=arena_at + 4 * LF[n][0])
                    for n in ("hTh", "hTl")]
        silu_t = area(LF, "silu", 2, 512)
        M0 = LM["M"][0]
        mslot = lambda n: piece(M0 + 1024 * n, 4, T)
        fT = area(LM, "fT", FTC, 257)
        f_r, f_k, f_v = (fT[:, 4 * n:4 * n + 4, 1:257] for n in range(3))
        At, Bt = (piece(LM["RT"][0] + 1024 * n, 4, T) for n in range(2))
        natl = {w: piece(LM["N"][0] + 1024 * n, NT, 512) for n, w in enumerate("ABKV")}
        dtmp, kk, kk2, sw, sa, Ls, Le = (mslot(n) for n in range(7))
        Einv, Ein, Eex, kp, rk, BhT, KhT = sw, Ls, Le, kk2, dtmp, sa, kk2
        retn = piece(M0 + 7 * 1024, NT, 2048)
        rqT, rkT = (piece(M0 + n * 1024, 4, T) for n in (11, 6))
        rsc = (mslot(3), piece(M0 + 5 * 1024, 4, P))
        mats = [piece(M0 + 2048 * n, NT, 8, P) for n in range(7)]
        AdT, Ad, o16T, o32T, X, P2, P2T = mats
        P4T, P4, P8T, TT, Z = AdT, Ad, P2, P2T, Ad
        AakT, ArbT, ArkT = AdT, P2, Ad
        Qn = piece(M0 + 2048 * 2, NT, 512)
        WT = piece(M0 + 2048 * 2 + 1024, 4, T)
        Un = piece(M0 + 2048 * 3, NT, 2, 256)
        gnat = piece(M0 + 2048 * 3 + 1024, NT, 512)
        ynat = piece(M0 + 2048 * 4, NT, 512)
        ytmp = piece(M0 + 2048 * 4 + 1024, NT, 512)
        S = piece(LM["RT"][0], NCH, 4, 64)
        PC = sb("PC", [P, 4, NCH])
        quad = [piece(QUAD * n, EG, 4, 512) for n in range(NQ)]
        xg = featL[:, 0:4, :].rearrange("p a b -> p (a b)").rearrange("p (k s) -> p k s", k=DK)
        G, Gw = (area(LE, n, NT, EG, CAP) for n in ("G", "Gw"))
        GT = area(LE, "GT", NT, P)
        sg, hh = (arena[:, LE[n][0]:LE[n][1]] for n in ("sg", "h"))
        hhT = area(LE, "hT", 4, P)
        dd = featL[:, 4:8, :].rearrange("p a b -> p (a b)").rearrange("p (n c) -> p n c", n=2)
        rank = rt[:, 0:64].rearrange("p (t e) -> p t e", t=NT)
        comb = rt[:, 64:128].rearrange("p (t e) -> p t e", t=NT)
        rank4, comb4 = rt[:, 576:584], rt[:, 584:592]
        selr = rt[:, 128:192].rearrange("p (t e) -> p t e", t=NT)

        x_in = [sem(f"x_in{t}") for t in range(NT)]
        ident_in = sem("ident_in")
        params_in = sem("params_in")
        rpb_copied = sem("rpb_copied")
        biasA_in = sem("biasA_in")
        t5_in = sem("t5_in")
        t5_stored = sem("t5_stored")
        biasB_in = sem("biasB_in")
        gain_in = sem("gain_in")
        first_in = sem("first_in")
        slot_in = [sem(f"slot_in{n}") for n in range(NSLOT)]
        down_read = sem("down_read")
        hi_ready = sem("hi_ready")
        lo_ready = {w: sem(f"lo_ready_{w}") for w in ("dve", "pool")}
        feat_hi = sem("feat_hi")
        feat_lo = sem("feat_lo")
        hT_hi = sem("hT_hi")
        hT_lo = sem("hT_lo")
        filled = sem("psum_filled")
        emptied = {w: sem(f"psum_emptied_{w}") for w in ("act", "dve")}
        dve_step = sem("dve_step")
        act_step = sem("act_step")
        rms_ready = sem("rms_ready")
        var_ready = sem("var_ready")
        root_ready = sem("root_ready")
        eps_ready = sem("eps_ready")
        xn_ready = sem("xn_ready")
        resid_ready = sem("resid_ready")
        qk_ready = sem("qk_ready")
        max_ready = sem("max_ready")
        exp_ready = sem("exp_ready")
        gates_ready = sem("gates_ready")
        y_ready = sem("y_ready")
        lerp_ready = sem("lerp_ready")
        lora_act = sem("lora_act")
        kk_ready = sem("kk_ready")
        kk2_ready = sem("kk2_ready")
        scan_ready = sem("scan_ready")
        decay_ready = sem("decay_ready")
        rot_ready = sem("rot_ready")
        rw_ready = sem("rw_ready")
        x0_ready = sem("x0_ready")
        mixed_ready = sem("mixed_ready")
        route_ready = sem("route_ready")
        count_ready = sem("count_ready")
        quad_in = [sem(f"quad_in{n}") for n in range(NQ)]
        quads_read = sem("quads_read")
        onehot_ready = sem("onehot_ready")
        gathered = sem("gathered")
        xg_ready = sem("xg_ready")
        silu_ready = sem("silu_ready")
        h_ready = sem("h_ready")
        gt_filled = sem("gt_filled")
        gt_ready = sem("gt_ready")
        hT_filled = sem("hT_filled")
        hT_ready = sem("hT_ready")
        d0_ready = sem("d0_ready")
        d1_ready = sem("d1_ready")
        scattered = sem("scattered")
        moe_done = sem("moe_done")
        shifted = sem("shifted")
        sum_done = sem("sum_done")
        out_ready = sem("out_ready")
        out_done = sem("out_done")

        rpb = A["rpb"]
        RPB = rpb.shape[1]
        rpb_copies = nc.dram_tensor("rpb_copies", (8, GRID_W, RPB), F32, kind="Internal").ap()
        t5_copies = nc.dram_tensor("t5_copies", (8, P, REL), F32, kind="Internal").ap()

        def kxn(w, lo, n):
            return w[:, lo:lo + n].rearrange("(k p) n -> p k n", p=P)

        units, uname = [], {}

        def unit(name, *parts):
            uname[name] = len(units)
            units.append(parts)

        w_in, w_in2 = A["w_in"], A["w_in_2"]
        for u in range(9):
            lo = 512 * u if u < 4 else (2048 if u == 4 else NQKV + 512 * (u - 5))
            n = 256 if u == 4 else 512
            unit(("p1", u), (0, DK, n, kxn(w_in, lo, n)))
        unit(("br", 0), (0, 4, D, kxn(A["w_branch_a"], 0, D)))
        unit(("br", 1), (0, 4, D, kxn(A["w_branch_b"], 0, D)))
        for n in range(2):
            unit(("wo", n), (0, DK, 512, kxn(A["w_out"], 512 * n, 512)))
        for u in range(FFK // 2):
            unit(("ffn", u), (0, DK, 256, kxn(A["w_gate"], 256 * u, 256)),
                 (2048, DK, 256, kxn(A["w_up"], 256 * u, 256)))
        for u in range(-(-FFK // 4)):
            kn = min(4, FFK - 4 * u)
            unit(("down", u), (0, kn, D, A["w_down"][512 * u:512 * u + kn * P, :].rearrange("(k p) n -> p k n", p=P)))
        unit(("rw", 3), (0, DK, 256, kxn(w_in2, 2048 + 1536, 256)))
        for u in (1, 0, 2):
            unit(("rw", u), (0, DK, 512, kxn(w_in2, 2048 + 512 * u, 512)))
        for u in range(4):
            unit(("p2", u), (0, DK, 512, kxn(w_in2, 512 * u, 512)))
        for n in range(2):
            unit(("wo2", n), (0, DK, 512, kxn(A["w_out_2"], 512 * n, 512)))
        loads_so_far, unit_level = [0] * NSLOT, []
        for n, parts in enumerate(units):
            loads_so_far[n % NSLOT] += 16 * len(parts)
            unit_level.append(loads_so_far[n % NSLOT])
        last_fill = {}
        for u in range(9):
            last_fill[("p1", u)] = ("p1", u, 0 if u == 4 else 1)
        for br in range(2):
            last_fill[("br", br)] = ("br", br, 1, 1)
        for n in range(2):
            last_fill[("wo", n)] = ("wo", n, 1)
            last_fill[("wo2", n)] = ("wo2", n, 1)
        for u in range(FFK // 2):
            last_fill[("ffn", u)] = ("up", u)
        last_fill[("rw", 3)] = ("rw", 6)
        for u in range(3):
            last_fill[("rw", u)] = ("rw", 2 * u + 1)
        for u in range(4):
            last_fill[("p2", u)] = ("p2", u, 1)
        last_fill[("down", 5)] = ("down", 1, 1)
        names = list(uname)

        def wview(name, part=0, of=None):
            n = uname[name]
            off, k, w, _ = units[n][part]
            return piece((n % NSLOT) * SLOT + off, k, w, of=of)

        chunks, chunk_of, chunk_last = [], {}, []

        def chunk(name, c, view, hi, last, by):
            chunk_of[name, c] = len(chunks)
            chunks.append((name, view, hi, by))
            chunk_last.append(last)

        def cols256(name, c):
            return lambda of: wview(name, 0, of)[:, :, 256 * c:256 * c + 256]

        ring = (*W_SIG, W_QK, W_SPARE)
        for n in range(9):
            u, c = n // 2, n % 2
            chunk(("p1", u), c, cols256(("p1", u), c), ring[n % 4], ("p1", u, c), "dve")
        for n in range(8):
            u, c = 5 + n // 2, n % 2
            chunk(("p1", u), c, cols256(("p1", u), c), (W_SPARE, W_NAT)[n % 2], ("p1", u, c), "pool" if n > 1 else "dve")
        ring = (W_SPARE, W_NAT, W_QK, W_PROB)
        for br in range(2):
            for c in range(2):
                chunk(("br", br), c, lambda of, br=br, c=c: wview(("br", br), 0, of)[:, :, 512 * c:512 * c + 512], ring[2 * br + c],
                      ("br", br, c, 1), "pool")
        for n in range(4):
            chunk(("wo", n // 2), n % 2, cols256(("wo", n // 2), n % 2), ring[n], ("wo", n // 2, n % 2), "pool")
        ring = (W_FFN, W_PROBT, W_PROB, W_SPARE)
        for n in range(FFK):
            u, c = n // 2, n % 2
            chunk(("ffn", u), c, lambda of, u=u, c=c: wview(("ffn", u), c, of), ring[n % 4], (("gate", "up")[c], u),
                  "pool" if n < 4 else "dve")
        for n in range(FFK // 2):
            chunk(("down", n // 2), n % 2, lambda of, n=n: wview(("down", n // 2), 0, of)[:, 2 * (n % 2):2 * (n % 2) + 2, :],
                  ring[(FFK + n) % 4],
                  ("down", 1, 1) if n == FFK // 2 - 1 else None, "dve")
        ring = (W_PROBT, W_SPARE, W_FFN)
        for n, c in enumerate(RW_ORDER):
            chunk(("rw", c // 2), c % 2, cols256(("rw", c // 2), c % 2), ring[n % 3], ("rw", c), "dve" if n < 1 else "pool")
        for n in range(8):
            chunk(("p2", n // 2), n % 2, cols256(("p2", n // 2), n % 2), ring[(n + len(RW_ORDER)) % 3], ("p2", n // 2, n % 2),
                  "pool")
        before, lo_level, taken, made = [], [], {}, {"dve": 0, "pool": 0}
        for g, (_, _, hi, by) in enumerate(chunks):
            before.append(taken.get(hi))
            taken[hi] = g
            made[by] += 1
            lo_level.append(made[by])

        def hi_view(g):
            _, view, hi, _ = chunks[g]
            view, rounded, high = view(arena), view(ring_r), hi_r[hi]
            k, n = view.shape[1], view.shape[2]
            step = hi[1] - hi[0]
            if step == CHUNK // 2:
                return high[:].rearrange("p (k n) -> p k n", k=k), view, rounded
            high = high[:].rearrange("p (a r) -> p a r", a=2)[:, :, 0:CHUNK // 2].rearrange("p a (k n) -> p a k n", n=n)
            return [high] + [w.rearrange("p (a k) n -> p a k n", a=2) for w in (view, rounded)]

        def hi_cols(g, k, lo, n):
            _, view, hi, _ = chunks[g]
            at_ = k * view(arena).shape[2] + lo
            at_ = hi[at_ // (CHUNK // 2)] - hi[0] + at_ % (CHUNK // 2)
            return hi_r[hi][:, at_:at_ + n]

        def lo_cols(g, k, lo, n):
            return chunks[g][1](ring_r)[:, k, lo:lo + n]

        def wait_chunk_read(eng, g):
            if chunk_last[g]:
                wait_filled(eng, *chunk_last[g])
            else:
                name, c = next(key for key, n in chunk_of.items() if n == g)
                eng.wait_ge(down_read, 2 * name[1] + c + 1)

        def wait_split(eng, g):
            eng.wait_ge(lo_ready[chunks[g][3]], lo_level[g])

        def low_part(eng, tensor_tensor, g):
            eng.wait_ge(hi_ready, g + 1)
            high, view, low = hi_view(g)
            tensor_tensor(low, view, high.bitcast(F32), ALU.subtract).then_inc(lo_ready[chunks[g][3]], 1)

        def wait_filled(eng, *key):
            eng.wait_ge(filled, index[key] + 1)

        def wait_emptied(eng, *key):
            eng.wait_ge(emptied[who_of[key]], turn[key] + 1)

        def bank(*key):
            return psum[:, index[key] % 8, :]

        class Steps:

            def __init__(self, eng, s):
                self.eng, self.sem, self.n, self.drains = eng, s, 0, 0

            def link(self, ins):
                ins.then_inc(self.sem, 1)
                self.n += 1
                self.eng.wait_ge(self.sem, self.n)

            def empty(self, who, ins, *key):
                assert who_of[key] == who and turn[key] == self.drains, (key, turn[key], self.drains)
                self.drains += 1
                ins.then_inc(emptied[who], 1)
                self.eng.wait_ge(emptied[who], self.drains)

        PARAMS_IN = 16 * 5
        block = ctx.enter_context(nc.Block())

        moe_w = {"gate": A["w_gate_2"], "up": A["w_up_2"], "down": A["w_down_2"]}
        QUADS_PER_GROUP = 6
        ALLQ = NG * QUADS_PER_GROUP

        def quad_slot(q):
            return (2, 3, 1, 0)[q % NQ]

        @block.sync
        def _(sp):
            for t in range(NT):
                nc.sync.dma_start(x[:, t, :], A["x"][t * P:(t + 1) * P, :]).then_inc(x_in[t], 16)
            for n, parts in enumerate(units):
                if n >= NSLOT:
                    old = names[n - NSLOT]
                    if old in last_fill:
                        wait_filled(sp, *last_fill[old])
                    else:
                        sp.wait_ge(down_read, 2 * old[1] + 2)
                if n == 0:
                    off, k, w, src = parts[0]
                    for h in range(2):
                        cols_ = slice(w // 2 * h, w // 2 * (h + 1))
                        nc.sync.dma_start(piece(off, k, w)[:, :, cols_], src[:, :, cols_]).then_inc((first_in, slot_in[0])[h], 16)
                    continue
                for off, k, w, src in parts:
                    nc.sync.dma_start(piece((n % NSLOT) * SLOT + off, k, w), src).then_inc(slot_in[n % NSLOT], 16)

            def load_quad(pair, q):
                gp, q6 = q // QUADS_PER_GROUP, q % QUADS_PER_GROUP
                kind, half = ("gate", "up", "down")[q6 // 2], q6 % 2
                for j in range(EG):
                    e = pair * (2 * EG) + (gp * EG + j)
                    if isinstance(e, int):
                        w = moe_w[kind][e]
                    else:
                        w = moe_w[kind][bass.ds(e, 1)].rearrange("a k n -> (a k) n")
                    w = w[:, 512 * half:512 * half + 512] if kind == "down" else w[512 * half:512 * half + 512, :]
                    nc.sync.dma_start(quad[quad_slot(q)][:, j], w.rearrange("(k p) n -> p k n", p=P))\
                        .then_inc(quad_in[quad_slot(q)], 16)

            def moe_stream(r, first):
                for q in range(NQ):
                    if first and q == 0:
                        sp.wait_ge(mixed_ready, 2 * NT)
                    if first and q >= 2:
                        wait_filled(sp, "wo2", q - 2, 1)
                    if not first and q == 0:
                        sp.wait_ge(quads_read, r * ALLQ)
                    load_quad(0, q)
                with sp.Fori(0, NG // 2 - 1) as pair:
                    for q in range(NQ, 12 + NQ):
                        sp.wait_ge(quads_read, r * ALLQ + pair * 12 + (q - NQ + 1))
                        load_quad(pair + q // 12, q % 12)
                for q in range(NQ, 12):
                    sp.wait_ge(quads_read, r * ALLQ + (ALLQ - 12 + q - NQ + 1))
                    load_quad(NG // 2 - 1, q)

            moe_stream(0, True)
            sp.wait_ge(count_ready, 1)
            most = sp.value_load(cnt[0:1, 0:1], min_val=0, max_val=T)
            with sp.Fori(1, ROUNDS) as r:
                with sp.If(most > r * CAP):
                    moe_stream(r, False)
            for t in range(NT):
                sp.wait_ge(out_ready, t + 1)
                nc.sync.dma_start(out[t * P:(t + 1) * P, :], xn[:, t, :]).then_inc(out_done, 16)
            sp.wait_ge(out_done, 16 * NT)

        @block.gpsimd
        def _(pool):
            pool.wait_ge(rpb_copied, 16)
            for h in range(8):
                for half in range(2):
                    src = bass.AP(tensor=rpb_copies.tensor, offset=h * GRID_W * RPB + (5 - half) * 31 + 15,
                                  ap=[[RPB - 1, GRID_W], [31, 6], [1, GRID_W]])
                    nc.gpsimd.dma_start(biasA[64 * half:64 * half + 64, h], src).then_inc(biasA_in, 16)
            wait_emptied(pool, "t5")
            nc.gpsimd.dma_start(t5_copies, tb_sb.unsqueeze(1).to_broadcast([8, P, REL])).then_inc(t5_stored, 16)
            pool.wait_ge(t5_stored, 16)
            src = bass.AP(tensor=t5_copies.tensor, offset=P - 1, ap=[[REL - 1, P], [P * REL, 8], [1, EXT]])
            nc.gpsimd.dma_start(biasB, src).then_inc(biasB_in, 16)
            for g, c in enumerate(chunks):
                if c[3] == "pool":
                    low_part(pool, nc.gpsimd.tensor_tensor, g)
            wait_filled(pool, "logit", NT - 1)
            nc.gpsimd.dma_start(featT[:, 0:4, :].rearrange("p a b -> p (a b)"),
                                A["final_gain"].to_broadcast([P, D])).then_inc(gain_in, 16)

        @block.tensor
        def _(pe):
            at = [0]

            def begin(*key):
                n = index[key]
                assert n == at[0], (key, n, at[0])
                at[0] += 1
                if n >= 8:
                    wait_emptied(pe, *fills[n - 8][0])
                return psum[:, n % 8, :]

            def end(ins):
                ins.then_inc(filled, 1)

            def have(name):
                n = uname[name]
                pe.wait_ge(slot_in[n % NSLOT], unit_level[n])

            mm, tr = nc.tensor.matmul, nc.tensor.transpose

            def transposes(key, sources, ready):
                b = begin(*key).rearrange("p (k q) -> p k q", q=P)
                ready()
                for k, s in enumerate(sources):
                    ins = tr(b[:, k, :], s, ident)
                end(ins)

            def norm_T(n):
                for t in range(NT):
                    for h in range(2):
                        transposes(("nt", n, t, h), [xn[:, t, (4 * h + k) * P:(4 * h + k + 1) * P] for k in range(4)],
                                   lambda: pe.wait_ge(xn_ready, NT * n + t + 1))

            def mm3(o, lhs, rhs, start, stop):
                mm(o, lhs[0], rhs[0], start=start, stop=False, skip_group_check=True)
                mm(o, lhs[0], rhs[1], start=False, stop=False, skip_group_check=True)
                return mm(o, lhs[1], rhs[0], start=False, stop=stop, skip_group_check=True)

            def project(key, name, c):
                b = begin(*key).rearrange("p (t n) -> p t n", t=NT)
                g = chunk_of[name, c]
                wait_split(pe, g)
                for t in range(NT):
                    for k in range(DK):
                        ins = mm3(b[:, t, :], [f[:, k, t * P:(t + 1) * P] for f in (featR, featLR)],
                                  [part(g, k, 0, 256) for part in (hi_cols, lo_cols)], k == 0, k == DK - 1)
                end(ins)

            def features(key, name, c, width=256):
                b = begin(*key).rearrange("p (f t) -> p f t", f=2)
                g = chunk_of[name, c]
                wait_split(pe, g)
                for f in range(2):
                    for k in range(DK):
                        ins = mm3(b[:, f, :], [part(g, k, P * f, P) for part in (hi_cols, lo_cols)],
                                  [r[:, k, :] for r in (featR, featLR)], k == 0, k == DK - 1)
                end(ins)

            pe.wait_ge(ident_in, 32)
            norm_T(0)
            pe.wait_ge(feat_lo, 4)
            offs = {"qa": 0, "ka": 512, "qb": 1536}
            def turn_qk(*names):
                for name in names:
                    s = ("qa", "ka", "qb", "kb").index(name)
                    for t in range(NT):
                        if name == "kb":
                            src = [kdup[:, t, kv, :] for kv in range(2)]
                        else:
                            src = [nat[:, t, offs[name] + P * k:offs[name] + P * (k + 1)] for k in range(4)]
                        transposes(("qkT", name, t), src, lambda: pe.wait_ge(qk_ready, 2 * s + t + 1))

            for u in range(5):
                if u == 4:
                    turn_qk("qa", "ka")
                for c in range(1 if u == 4 else 2):
                    project(("p1", u, c), ("p1", u), c)
                if u == 2:
                    b = begin("t5")
                    pe.wait_ge(params_in, PARAMS_IN)
                    pe.wait_ge(t5_in, 32)
                    end(mm(b[0:8, 0:REL], t5b[:], onehot, start=True, stop=True))
            def turn_out(br, t):
                transposes(("oT", br, t), [xn[:, t, 512 * br + P * k:512 * br + P * (k + 1)] for k in range(4)],
                           lambda: wait_emptied(pe, "PV", 4 * br + 2 * t + 1))

            def scores(i):
                br, t, g = i // 4, i // 2 % 2, i % 2
                banks = [begin("S", i, par).rearrange("p (a k) -> p a k", a=2) for par in range(2)]
                for name in ("qa", "ka") if br == 0 else ("qb", "kb"):
                    wait_emptied(pe, "qkT", name, 1)
                for pair in range(2):
                    for par in range(2):
                        rows_ = slice(64 * par, 64 * par + 64)
                        q = (qbT if br else qaT)[rows_, 2 * g + pair, t * P:(t + 1) * P]
                        k = kbT[rows_, g, :] if br else kaT[rows_, 2 * g + pair, :]
                        ins = mm(banks[par][:, pair, :], q, k, start=True, stop=True)
                        if pair == 1:
                            end(ins)

            def turned(i):
                for par in range(2):
                    b = begin("PT", i, par).rearrange("p (a k q) -> p a k q", a=2, k=2)
                    pe.wait_ge(exp_ready, 2 * i + par + 1)
                    for pair in range(2):
                        for kt in range(NT):
                            ins = tr(b[:, pair, kt, :], prob[:, i % 2, par, pair, kt * P:(kt + 1) * P], ident)
                    end(ins)

            def weighted(i):
                br, t, g = i // 4, i // 2 % 2, i % 2
                b = begin("PV", i)
                for par in range(2):
                    wait_emptied(pe, "PT", i, par)
                for h in range(4):
                    for kt in range(NT):
                        v0 = 2176 + 64 * g if br else 1024 + 64 * (4 * g + h)
                        ins = mm(b[:, 64 * h:64 * h + 64], probT[:, 2 * (i % 2) + h % 2, h // 2, kt, :],
                                 nat[:, kt, v0:v0 + 64], start=kt == 0, stop=kt == NT - 1)
                end(ins)

            for i in range(9):
                if i < 8:
                    scores(i)
                if i >= 1:
                    turned(i - 1)
                if i == 0:
                    turn_qk("qb", "kb")
                if i < 8:
                    u, c = 5 + i // 2, i % 2
                    project(("p1", u, c), ("p1", u), c)
                if i == 8:
                    for key in ((0, 0), (0, 1), (1, 0)):
                        turn_out(*key)
                if i >= 1:
                    weighted(i - 1)
            for br in range(2):
                if br == 1:
                    turn_out(1, 1)
                for n in range(2):
                    g = chunk_of[("br", br), n]
                    wait_split(pe, g)
                    for t in range(NT):
                        b = begin("br", br, n, t)
                        wait_emptied(pe, "oT", br, t)
                        for k in range(4):
                            ins = mm3(b, [f[:, 4 * br + k, t * P:(t + 1) * P] for f in (featR, featLR)],
                                      [part(g, k, 0, 512) for part in (hi_cols, lo_cols)], k == 0, k == 3)
                        end(ins)
            for h in range(2):
                for t in range(NT):
                    transposes(("yT", t, h), [sig[:, t, (4 * h + k) * P:(4 * h + k + 1) * P] for k in range(4)],
                               lambda: pe.wait_ge(y_ready, 2 * h + t + 1))
            wait_emptied(pe, "yT", 1, 1)
            for n in range(2):
                for c in range(2):
                    project(("wo", n, c), ("wo", n), c)
            norm_T(1)
            pe.wait_ge(feat_lo, 8)
            for u in range(FFK // 2):
                for c, name in enumerate(("gate", "up")):
                    features((name, u), ("ffn", u), c)
            banks = {(t, n): begin("down", t, n) for t in range(NT) for n in range(2)}
            for u in range(FFK // 2):
                g = chunk_of[("down", u // 2), u % 2]
                wait_split(pe, g)
                pe.wait_ge(hT_lo, u + 1)
                for t in range(NT):
                    for n in range(2):
                        for k in range(2):
                            ins = mm3(banks[t, n], [h[:, 2 * u + k, t * P:(t + 1) * P] for h in hT_parts],
                                      [part(g, k, 512 * n, 512) for part in (hi_cols, lo_cols)],
                                      u == 0 and k == 0, u == FFK // 2 - 1 and k == 1)
                        if u == FFK // 2 - 1:
                            end(ins)
                if u < FFK // 2 - 1:
                    ins.then_inc(down_read, 1)

            norm_T(2)
            pe.wait_ge(feat_lo, 12)
            def lora_up(name, lo, sem_, src):
                for h in range(2):
                    b = begin(name, h).rearrange("p (f t) -> p f t", f=2)
                    pe.wait_ge(sem_, 1)
                    for f in range(2):
                        c = 2 * h + f
                        ins = mm(b[:, f, :], lora[lo:lo + 64, P * c:P * c + P], src, start=True, stop=True)
                    end(ins)

            for c in RW_ORDER:
                features(("rw", c), ("rw", c // 2), c % 2)
                if c == 3:
                    lora_up("z", 0, lora_act, tanh_w[:])
                    lora_up("za", 64, lerp_ready, fT[64:128, 12, 1:257])
                if c == 0:
                    for h in range(2):
                        b = begin("ss", h)
                        pe.wait_ge(kk2_ready, 1)
                        end(mm(b, con("same"), kk2[:, 2 * h:2 * h + 2, :].rearrange("p a b -> p (a b)"), start=True, stop=True))
            for u in range(3):
                for c in range(2):
                    project(("p2", u, c), ("p2", u), c)
            for s, name in enumerate(("q", "k")):
                for t in range(NT):
                    transposes(("rT", name, t), [retn[:, t, 512 * s + P * k:512 * s + P * (k + 1)] for k in range(4)],
                               lambda: pe.wait_ge(rot_ready, t + 1))
            for j in range(3):
                b = begin("rs", j)
                for name in ("q", "k"):
                    wait_emptied(pe, "rT", name, 1)
                if j < 2:
                    for a in range(2):
                        ins = mm(b[:, T * a:T * a + T], rkT[:, 2 * j + a, 0:P], rqT[:, 2 * j + a, :], start=True, stop=True)
                else:
                    for a in range(4):
                        ins = mm(b[:, P * a:P * a + P], rkT[:, a, P:T], rqT[:, a, P:T], start=True, stop=True)
                end(ins)
            project(("p2", 3, 0), ("p2", 3), 0)
            for t in range(NT):
                b = begin("ro", t)
                wait_emptied(pe, "rs", 2 * t if t else 1)
                for a in range(4):
                    for kt in range(t + 1):
                        lhs = rsc[0][:, a, t * P:(t + 1) * P] if kt == 0 else rsc[1][:, a, :]
                        ins = mm(b[:, P * a:P * a + P], lhs, retn[:, kt, 1024 + P * a:1024 + P * (a + 1)],
                                 start=kt == 0, stop=kt == t)
                end(ins)
            project(("p2", 3, 1), ("p2", 3), 1)
            src = {"A": At, "B": BhT, "K": KhT, "V": f_v}
            for w in "ABKV":
                for t in range(NT):
                    transposes(("natl", w, t), [src[w][:, k, t * P:(t + 1) * P] for k in range(4)],
                               lambda: pe.wait_ge(rw_ready, 1))
            b = begin("bonus")
            for t in range(NT):
                for k in range(4):
                    ins = mm(b[:, 8 * t + 2 * k:8 * t + 2 * k + 2], rk[:, k, t * P:(t + 1) * P], con("sel"),
                             start=True, stop=True)
            end(ins)

            sides = {"AT": (Bt, At), "A": (At, Bt), "Aak": (f_k, At), "Arb": (Bt, f_r), "Ark": (f_k, f_r)}

            def mat(name):
                lhs, rhs = sides[name]
                for t in range(NT):
                    for par in range(2):
                        b = begin("mat", name, t, par).rearrange("p (i q) -> p i q", i=4)
                        for i in range(4):
                            r = slice(64 * par, 64 * par + 64)
                            ins = mm(b[:, i, :], lhs[r, i, t * P:(t + 1) * P], rhs[r, i, t * P:(t + 1) * P],
                                     start=True, stop=True)
                        end(ins)

            mat("AT")
            mat("A")
            steps = {
                "P2": (AdT, Ad, ("mat A",)), "P2T": (Ad, AdT, ()),
                "X1": (P2T, X, ("P2T", "X0")), "P4": (P2T, P2, ("P2",)), "P4T": (P2, P2T, ()),
                "X2": (P4T, X, ("P4T", "X1")), "P8T": (P4, P4T, ("P4",)), "X3": (P8T, X, ("P8T", "X2")),
                "T16T": (X, None, ("X3",)), "Z1": (o16T, X, ()), "X4": (TT, Z, ("Z1", "T16T")),
                "T32T": (X, None, ("X4",)), "Z2": (o32T, X, ()), "X5": (TT, Z, ("Z2", "T32T")),
                "TT": (X, None, ("X5",)),
            }
            for name, _ in INVERSE:
                lhs, rhs, needs = steps[name]
                for t in range(NT):
                    for par in range(2):
                        b = begin("inv", name, t, par).rearrange("p (i q) -> p i q", i=4)
                        for need in needs:
                            if need == "mat A":
                                wait_emptied(pe, "mat", "A", t, par)
                            elif need == "X0":
                                pe.wait_ge(x0_ready, 2 * t + par + 1)
                            else:
                                wait_emptied(pe, "inv", need, t, par)
                        for i in range(4):
                            h = 4 * par + i
                            if rhs is None:
                                ins = tr(b[:, i, :], lhs[:, t, h, :], ident)
                            else:
                                ins = mm(b[:, i, :], lhs[:, t, h, :], rhs[:, t, h, :], start=True, stop=True)
                        end(ins)
                for extra in INV_EXTRA.get(name, ()):
                    mat(extra)
                if name == "Z2":
                    for t in range(NT):
                        b = begin("Q", t)
                        for par in range(2):
                            wait_emptied(pe, "mat", "Aak", t, par)
                        wait_emptied(pe, "natl", "V", t)
                        for h in range(8):
                            ins = mm(b[:, 64 * h:64 * h + 64], AakT[:, t, 4 * (h % 2) + h // 2, :],
                                     natl["V"][:, t, 64 * h:64 * h + 64], start=True, stop=True)
                        end(ins)
                    for t in range(NT):
                        b = begin("gn", t)
                        pe.wait_ge(lora_act, 2)
                        end(mm(b, sig_g[:, t * P:(t + 1) * P], gup[:], start=True, stop=True))
            for t in range(NT):
                b = begin("WT", t).rearrange("p (i q) -> p i q", i=4)
                for par in range(2):
                    wait_emptied(pe, "inv", "TT", t, par)
                for h in range(8):
                    ins = mm(b[64 * (h % 2):64 * (h % 2) + 64, h // 2, :], natl["A"][:, t, 64 * h:64 * h + 64],
                             TT[:, t, 4 * (h % 2) + h // 2, :], start=True, stop=True, skip_group_check=True)
                end(ins)
            def state_add(b, c, side, right):
                t, r = c // 2, slice(64 * (c % 2), 64 * (c % 2) + 64)
                for h in range(8):
                    par, i = h % 2, h // 2
                    ins = mm(b[64 * par:64 * par + 64, i, :], natl[side][r, t, 64 * h:64 * h + 64], right(r, t, par, i),
                             start=side == "K" and i == 0, stop=side == "B", skip_group_check=True)
                return ins

            def outputs(t, par):
                b = begin("Y", t, par)
                for p2 in range(2):
                    wait_emptied(pe, "U", 2 * t + 1, p2)
                    wait_emptied(pe, "mat", "Ark", t, p2)
                for i in range(4):
                    h = 2 * i + par
                    mm(b[:, 64 * i:64 * i + 64], ArbT[:, t, 4 * par + i, :], Un[:, t, par, 64 * i:64 * i + 64],
                       start=True, stop=False, skip_group_check=True)
                    ins = mm(b[:, 64 * i:64 * i + 64], ArkT[:, t, 4 * par + i, :], natl["V"][:, t, 64 * h:64 * h + 64],
                             start=False, stop=False, skip_group_check=True)
                    r = slice(64 * par, 64 * par + 64)
                    for cc in (2 * t, 2 * t + 1):
                        if cc > 0:
                            ins = mm(b[64 * (cc % 2):64 * (cc % 2) + 64, 64 * i:64 * i + 64],
                                     f_r[r, i, CH * cc:CH * cc + CH], S[r, cc, i, :],
                                     start=False, stop=cc % 2 == 1, skip_group_check=True)
                end(ins)

            for c in range(NCH):
                t, ro = c // 2, 64 * (c % 2)
                tok = slice(CH * c, CH * c + CH)
                banks = [begin("U", c, par) for par in range(2)]
                state = None
                if c < NCH - 1 and c not in Y_AFTER:
                    state = begin("St", c).rearrange("p (i v) -> p i v", v=64)
                    state_add(state, c, "K", lambda r, t, par, i: natl["V"][r, t, 64 * (2 * i + par):64 * (2 * i + par) + 64])
                wait_emptied(pe, "Q", t)
                wait_emptied(pe, "WT", t)
                for with_state in range(2 if c else 1):
                    if with_state:
                        wait_emptied(pe, "St", c - 1)
                    for par in range(2):
                        r = slice(64 * par, 64 * par + 64)
                        for i in range(4):
                            h = 2 * i + par
                            o = banks[par][ro:ro + 64, 64 * i:64 * i + 64]
                            if with_state:
                                ins = mm(o, WT[r, i, tok], S[r, c, i, :], start=False, stop=True, skip_group_check=True)
                            else:
                                ins = mm(o, TT[:, t, 4 * par + i, ro:ro + 64], Qn[:, t, 64 * h:64 * h + 64],
                                         start=i == 0, stop=c == 0, skip_group_check=True)
                        if with_state or c == 0:
                            end(ins)
                for y in Y_AFTER.get(c, ()):
                    outputs(*y)
                if c < NCH - 1:
                    if state is None:
                        state = begin("St", c).rearrange("p (i v) -> p i v", v=64)
                        state_add(state, c, "K", lambda r, t, par, i: natl["V"][r, t, 64 * (2 * i + par):64 * (2 * i + par) + 64])
                    for par in range(2):
                        wait_emptied(pe, "U", c, par)
                    end(state_add(state, c, "B", lambda r, t, par, i: Un[r, t, par, 64 * i:64 * i + 64]))
            for t in range(NT):
                for h in range(2):
                    transposes(("mT", t, h), [xn[:, t, (4 * h + k) * P:(4 * h + k + 1) * P] for k in range(4)],
                               lambda: pe.wait_ge(mixed_ready, t + 1 + NT * h))
            wait_emptied(pe, "mT", 1, 1)
            for n in range(2):
                have(("wo2", n))
                for t in range(NT):
                    b = begin("wo2", n, t)
                    for k in range(DK):
                        ins = mm(b, featT[:, k, t * P:(t + 1) * P], wview(("wo2", n))[:, k, :], start=k == 0, stop=k == DK - 1)
                    end(ins)
            norm_T(3)
            for t in range(NT):
                b = begin("logit", t)
                wait_emptied(pe, "nt", 3, t, 1)
                for k in range(DK):
                    ins = mm(b[:, 0:36], featT[:, k, t * P:(t + 1) * P], wr[:, k, :], start=k == 0, stop=k == DK - 1)
                end(ins)
            for t in range(NT):
                b = begin("rank", t)
                pe.wait_ge(route_ready, 1)
                if t:
                    mm(b[:, 0:E], con("ones"), selr[:, 0, :], start=True, stop=False)
                end(mm(b[:, 0:E], con("before"), selr[:, t, :], start=t == 0, stop=True))
            b = begin("count")
            for t in range(NT):
                ins = mm(b[:, 0:E], con("ones"), selr[:, t, :], start=t == 0, stop=t == NT - 1)
            end(ins)

            wait_emptied(pe, "count")
            ybank = {(t, n): psum[:, 2 * t + n, :] for t in range(NT) for n in range(2)}
            pe.wait_ge(gt_ready, 1)
            for t in range(NT):
                for n in range(2):
                    ins = mm(ybank[t, n], GT[:, t, :], dd[:, n, :], start=True, stop=False, skip_group_check=True)
            ins.then_inc(scattered, 1)

            def moe_group(r, pair, gp):
                n = r * NG + pair * 2 + gp
                base = r * ALLQ + pair * 12 + gp * 6

                def quad_ready(q):
                    pe.wait_ge(quad_in[quad_slot(q)], r * (12 * 64) + pair * (3 * 64) + (q // NQ + 1) * 64)
                    return quad[quad_slot(q)]

                pe.wait_ge(onehot_ready, n + 1)
                for kb in range(2):
                    b = psum[:, 6 + kb, :].rearrange("p (k s) -> p k s", k=4)
                    for k in range(4):
                        for t in range(NT):
                            ins = mm(b[:, k, :], xn[:, t, (4 * kb + k) * P:(4 * kb + k + 1) * P],
                                     G[:, t].rearrange("p e s -> p (e s)"), start=t == 0, stop=t == NT - 1)
                    ins.then_inc(gathered, 1)
                pe.wait_ge(xg_ready, 2 * n + 2)
                for m in range(2):
                    for half in range(2):
                        w = quad_ready(6 * gp + 2 * m + half)
                        for k in range(4):
                            for j in range(EG):
                                ins = mm(psum[32 * j:32 * j + 32, 4 + m, :], xg[:, 4 * half + k, 32 * j:32 * j + 32],
                                         w[:, j, k, :], start=half == 0 and k == 0, stop=half == 1 and k == 3,
                                         skip_group_check=True)
                        ins.then_inc(quads_read, 1)
                b = psum[:, 6, 0:2 * P].rearrange("p (t q) -> p t q", t=NT)
                for t in range(NT):
                    ins = tr(b[:, t, :], Gw[:, t].rearrange("p e s -> p (e s)"), ident)
                ins.then_inc(gt_filled, 1)
                pe.wait_ge(h_ready, n + 1)
                b = psum[:, 7, :].rearrange("p (k s) -> p k s", k=4)
                for k in range(4):
                    ins = tr(b[:, k, :], hh[:, k * P:(k + 1) * P], ident)
                ins.then_inc(hT_filled, 1)
                pe.wait_ge(hT_ready, n + 1)
                for half in range(2):
                    w = quad_ready(6 * gp + 4 + half)
                    for k in range(4):
                        for j in range(EG):
                            ins = mm(psum[32 * j:32 * j + 32, 4 + half, :], hhT[:, k, 32 * j:32 * j + 32], w[:, j, k, :],
                                     start=k == 0, stop=k == 3, skip_group_check=True)
                    ins.then_inc(quads_read, 1)
                pe.wait_ge(gt_ready, n + 2)
                pe.wait_ge(d0_ready, n + 1)
                pe.wait_ge(d1_ready, n + 1)
                for t in range(NT):
                    for k in range(2):
                        ins = mm(ybank[t, k], GT[:, t, :], dd[:, k, :], start=False, stop=False, skip_group_check=True)
                ins.then_inc(scattered, 1)

            def moe_round(r):
                with pe.Fori(0, NG // 2) as pair:
                    for gp in range(2):
                        moe_group(r, pair, gp)

            moe_round(0)
            pe.wait_ge(count_ready, 1)
            most = pe.value_load(cnt[0:1, 0:1], min_val=0, max_val=T)
            with pe.Fori(1, ROUNDS) as r:
                with pe.If(most > r * CAP):
                    moe_round(r)
            mm(psum[:, 4, 0:P], ident, ident, start=True, stop=True).then_inc(moe_done, 1)

        @block.scalar
        def _(act):
            a = Steps(act, act_step)
            fn = nc.scalar.activation
            empty = lambda ins, *key: a.empty("act", ins, *key)

            def squares(n, ready):
                fn(warm[:], eps_col[:, 0:1], ACT.Sqrt)
                for t in range(NT):
                    ready(t)
                    s = st[:, 2 * n + t:2 * n + t + 1]
                    a.link(fn(xn[:, t, :], x[:, t, :], ACT.Square, accum_out=s))
                    fn(s, s, ACT.Sqrt, scale=1.0 / D, bias=eps_col[:, 0:1]).then_inc(rms_ready, 1)

            n_roots = [0]

            def root(lo, n, d, k):
                n_roots[0] += 1
                act.wait_ge(var_ready, n_roots[0])
                s = st[:, lo:lo + n]
                fn(s, s, ACT.Sqrt, scale=1.0 / d, bias=eps_col[:, k:k + 1]).then_inc(root_ready, 1)

            def high_part(g, *also):
                name = chunks[g][0]
                if g == 0:
                    act.wait_ge(first_in, 16)
                else:
                    act.wait_ge(slot_in[uname[name] % NSLOT], unit_level[uname[name]])
                if before[g] is not None:
                    wait_chunk_read(act, before[g])
                for key in also:
                    wait_filled(act, *key)
                high, view, _ = hi_view(g)
                fn(high, view, ACT.Copy).then_inc(hi_ready, 1)

            def high_features(n):
                for t in range(NT):
                    for h in range(2):
                        wait_emptied(act, "nt", n, t, h)
                        fn(featR[:, 4 * h:4 * h + 4, t * P:(t + 1) * P],
                           featL[:, 4 * h:4 * h + 4, t * P:(t + 1) * P], ACT.Copy).then_inc(feat_hi, 1)

            ident_lo, ident_hi = CST["ident"]
            nc.scalar.dma_start(cst[:, ident_lo:ident_hi], A["cst"][:, ident_lo:ident_hi]).then_inc(ident_in, 16)
            nc.scalar.dma_start(cols[:], A["cols"]).then_inc(ident_in, 16)
            act.wait_ge(eps_ready, 3)
            squares(0, lambda t: act.wait_ge(x_in[t], 16))
            high_part(0)
            high_features(0)
            high_part(1)
            nc.scalar.dma_start(t5b[:], A["t5"]).then_inc(t5_in, 16)
            nc.scalar.dma_start(onehot, A["onehot"]).then_inc(t5_in, 16)
            nc.scalar.dma_start(cst[:, ident_hi:], A["cst"][:, ident_hi:]).then_inc(params_in, 16)
            nc.scalar.dma_start(rows[:], A["rows"].to_broadcast([P, ROWS["end"]])).then_inc(params_in, 16)
            nc.scalar.dma_start(rpb_copies, rpb.unsqueeze(1).to_broadcast([8, GRID_W, RPB])).then_inc(rpb_copied, 16)
            nc.scalar.dma_start(lora[:], A["lora"]).then_inc(params_in, 16)
            nc.scalar.dma_start(gup[:], A["gup"]).then_inc(params_in, 16)
            nc.scalar.dma_start(wr[:], A["wr"].rearrange("(k p) n -> p k n", p=P)).then_inc(params_in, 16)
            high_part(2)
            high_part(3)
            dsts = {"qa": qaT, "ka": kaT, "qb": qbT, "kb": kbT}

            def qk_moved(*names):
                for name in names:
                    nk = 2 if name == "kb" else 4
                    for t in range(NT):
                        wait_filled(act, "qkT", name, t)
                        empty(fn(dsts[name][:, :, t * P:(t + 1) * P],
                                 bank("qkT", name, t)[:, 0:nk * P].rearrange("p (k q) -> p k q", k=nk),
                                 ACT.Copy, scale=colp(name)), "qkT", name, t)

            act.wait_ge(ident_in, 32)
            for n in range(9):
                u, c = n // 2, n % 2
                if n == 8:
                    qk_moved("qa", "ka")
                wait_filled(act, "p1", u, c)
                if n + 4 < 9:
                    high_part(n + 4)
                elif n == 8:
                    high_part(9)
                lo = 512 * u + 256 * c
                empty(fn(nat[:, :, lo:lo + 256], bank("p1", u, c).rearrange("p (t n) -> p t n", t=NT), ACT.Copy), "p1", u, c)
                if n == 5:
                    wait_filled(act, "t5")
                    empty(fn(tb_sb, bank("t5")[0:8, 0:REL], ACT.Copy), "t5")
                if n == 5:
                    root(*QK_SUMS[0], HD, 0)
            def high_moved(*key):
                h, t = key[1:] if key[0] == "oT" else (key[2], key[1])
                wait_filled(act, *key)
                fn(featR[:, 4 * h:4 * h + 4, t * P:(t + 1) * P],
                   bank(*key).rearrange("p (k q) -> p k q", k=4), ACT.Copy).then_inc(feat_hi, 1)

            def gates(br):
                g = sig[:, :, 1024 * br:1024 * br + 1024]
                fn(g, g, ACT.Sigmoid).then_inc(gates_ready, 1)

            first = {n: chunk_of[n, 0] for n in (("p1", 5), ("br", 0), ("wo", 0), ("ffn", 0), ("down", 0), ("rw", 3), ("p2", 0))}
            root(*QK_SUMS[1], HD, 0)
            for i in range(9):
                if i >= 1:
                    wait_filled(act, "PT", i - 1, 0)
                    empty(fn(probT[:, 2 * ((i - 1) % 2)].rearrange("p a k q -> p (a k q)"), bank("PT", i - 1, 0), ACT.Copy),
                          "PT", i - 1, 0)
                if i == 0:
                    qk_moved("qb", "kb")
                if i < 8:
                    for par in range(2):
                        act.wait_ge(max_ready, 2 * i + par + 1)
                        for pair in range(2):
                            k = 4 * i + 2 * par + pair
                            pr = prob[:, i % 2, par, pair, :]
                            ins = fn(pr, pr, ACT.Exp, bias=negmax[:, k:k + 1], accum_out=sums[:, k:k + 1])
                            if i >= 4 or pair == 0:
                                a.link(ins)
                        if i >= 4:
                            k = 4 * i + 2 * par
                            ins = fn(esink[:, k:k + 2], esink[:, k:k + 2], ACT.Exp)
                        ins.then_inc(exp_ready, 1)
                    u, c = 5 + i // 2, i % 2
                    if i == 0:
                        high_part(first["p1", 5] + 1)
                    wait_filled(act, "p1", u, c)
                    ins = fn(sig[:, :, 256 * i:256 * i + 256], bank("p1", u, c).rearrange("p (t n) -> p t n", t=NT), ACT.Copy)
                    empty(ins, "p1", u, c)
                    high_part(first["p1", 5] + i + 2)
            for key in ((0, 0), (0, 1), (1, 0)):
                high_moved("oT", *key)
            gates(0)
            high_part(first["br", 0] + 2, ("S", 7, 1))
            high_part(first["br", 0] + 3, ("PT", 7, 1))
            high_moved("oT", 1, 1)
            gates(1)
            for n in range(3):
                high_part(first["wo", 0] + n)
            for h in range(2):
                for t in range(NT):
                    high_moved("yT", t, h)
            high_part(first["wo", 0] + 3)
            for n in range(2):
                high_part(first["ffn", 0] + n, ("PV", 7))
            squares(1, lambda t: wait_emptied(act, "wo", 1, 1))
            high_features(1)
            for n in range(2, 4):
                high_part(first["ffn", 0] + n)
            for u in range(FFK // 2):
                high_part(first["ffn", 0] + 2 * u + 4)
                wait_filled(act, "gate", u)
                if u >= 2:
                    wait_emptied(act, "up", u - 2)
                empty(fn(silu_t[:, u % 2, :], bank("gate", u), ACT.Silu), "gate", u)
                high_part(first["ffn", 0] + 2 * u + 5)
                wait_emptied(act, "up", u)
                fn(hT_parts[0][:, 2 * u:2 * u + 2, :], hTl[:, 2 * u:2 * u + 2, :], ACT.Copy).then_inc(hT_hi, 1)
            for g in range(first["down", 0] + 4, first["rw", 3] + 2):
                high_part(g)

            squares(2, lambda t: wait_emptied(act, "down", t, 1))
            high_features(2)
            high_part(first["rw", 3] + 2)
            for n, c in enumerate(RW_ORDER):
                wait_filled(act, "rw", c)
                high_part(first["rw", 3] + n + 3)
                if c == RW_ORDER[0]:
                    act.wait_ge(xn_ready, 3 * NT)
                empty(fn(fT[:, 2 * c:2 * c + 2, 1:257], bank("rw", c).rearrange("p (f t) -> p f t", f=2), ACT.Copy), "rw", c)
                if c == 2:
                    act.wait_ge(lerp_ready, 1)
                    fn(tanh_w[:], fT[0:64, 12, 1:257], ACT.Tanh).then_inc(lora_act, 1)
                    fn(sig_g[:], fT[:, 13, 1:257], ACT.Sigmoid).then_inc(lora_act, 1)
                if c == 3:
                    for name, dst, bias in (("z", sw, "w0"), ("za", sa, "a0")):
                        for h in range(2):
                            wait_filled(act, name, h)
                            b = bank(name, h).rearrange("p (f t) -> p f t", f=2)
                            a.link(fn(dst[:, 2 * h, :], b[:, 0, :], ACT.Sigmoid, bias=colp(bias, 2 * h)))
                            empty(fn(dst[:, 2 * h + 1, :], b[:, 1, :], ACT.Sigmoid, bias=colp(bias, 2 * h + 1)), name, h)
                    act.wait_ge(kk_ready, 1)
                    fn(kk2, kk, ACT.Square).then_inc(kk2_ready, 1)
                if c == 0:
                    for h in range(2):
                        wait_filled(act, "ss", h)
                        empty(fn(kk2[:, 2 * h:2 * h + 2, :].rearrange("p a b -> p (a b)"), bank("ss", h), ACT.Sqrt), "ss", h)
                if c == 1:
                    act.wait_ge(scan_ready, 1)
                    a.link(fn(Einv, Ls, ACT.Exp, scale=DECAY))
                    a.link(fn(Ein, Ls, ACT.Exp, scale=-DECAY))
                    fn(Eex, Le, ACT.Exp, scale=-DECAY).then_inc(decay_ready, 1)

            def ret_move(u, c):
                wait_filled(act, "p2", u, c)
                if 2 * u + c + 3 < 8:
                    high_part(first["p2", 0] + 2 * u + c + 3)
                lo = 512 * u + 256 * c
                empty(fn(retn[:, :, lo:lo + 256], bank("p2", u, c).rearrange("p (t n) -> p t n", t=NT),
                         ACT.Silu if u == 3 else ACT.Copy), "p2", u, c)

            for u in range(3):
                for c in range(2):
                    ret_move(u, c)
            for name, dst in (("q", rqT), ("k", rkT)):
                for t in range(NT):
                    wait_filled(act, "rT", name, t)
                    empty(fn(dst[:, :, t * P:(t + 1) * P], bank("rT", name, t).rearrange("p (k q) -> p k q", k=4), ACT.Copy),
                          "rT", name, t)
            ret_move(3, 0)
            ret_move(3, 1)
            for t in range(NT):
                root(48, RET_H, RET_D, 1)
            for w in "ABKV":
                for t in range(NT):
                    wait_filled(act, "natl", w, t)
                    empty(fn(natl[w][:, t, :], bank("natl", w, t), ACT.Copy), "natl", w, t)
            dst = {"P2": P2, "P4": P4, "P8T": P8T, "T16T": TT, "T32T": TT, "TT": TT, "Z1": Z, "Z2": Z}
            for name, who in INVERSE:
                if who == "act":
                    for t in range(NT):
                        for par in range(2):
                            key = ("inv", name, t, par)
                            wait_filled(act, *key)
                            empty(fn(dst[name][:, t, 4 * par:4 * par + 4, :].rearrange("p i q -> p (i q)"), bank(*key),
                                     ACT.Copy), *key)
                if name == "Z2":
                    for t in range(NT):
                        wait_filled(act, "Q", t)
                        empty(fn(Qn[:, t, :], bank("Q", t), ACT.Copy), "Q", t)
                    for t in range(NT):
                        wait_filled(act, "gn", t)
                        empty(fn(gnat[:, t, :], bank("gn", t), ACT.Copy), "gn", t)
            for t in range(NT):
                wait_filled(act, "WT", t)
                empty(fn(WT[:, :, t * P:(t + 1) * P], bank("WT", t).rearrange("p (i q) -> p i q", i=4), ACT.Copy), "WT", t)
            for c in range(NCH):
                r = slice(64 * (c % 2), 64 * (c % 2) + 64)
                wait_filled(act, "U", c, 1)
                empty(fn(Un[r, c // 2, 1, :], bank("U", c, 1)[r, 0:256], ACT.Copy), "U", c, 1)
                for t, par in Y_AFTER.get(c, ()):
                    wait_filled(act, "Y", t, par)
                    yv = ynat[:, t, :].rearrange("p (i a v) -> p i a v", i=4, a=2)[:, :, par, :]
                    empty(fn(yv, bank("Y", t, par)[:, 0:256].rearrange("p (i v) -> p i v", i=4), ACT.Copy), "Y", t, par)
            for t in range(NT):
                root(48, RW_H, 64, 2)
            for t in range(NT):
                for h in range(2):
                    wait_filled(act, "mT", t, h)
                    empty(fn(featT[:, 4 * h:4 * h + 4, t * P:(t + 1) * P],
                             bank("mT", t, h).rearrange("p (k q) -> p k q", k=4), ACT.Copy), "mT", t, h)

            def resid3(t):
                wait_emptied(act, "wo2", 1, t)
                wait_filled(act, "mT", t, 1)
            squares(3, resid3)
            act.wait_ge(route_ready, 1)
            a.link(fn(rt[:, 480:488], rt[:, 480:488], ACT.Exp))
            fn(rt[:, 488:490], rt[:, 488:490], ACT.Exp).then_inc(exp_ready, 1)

            def moe_group(r, pair, gp):
                n = r * NG + pair * 2 + gp
                base = r * ALLQ + pair * 12 + gp * 6
                act.wait_ge(quads_read, base + 2)
                fn(sg, psum[:, 4, :], ACT.Silu).then_inc(silu_ready, 1)
                act.wait_ge(hT_filled, n + 1)
                fn(hhT.rearrange("p k s -> p (k s)"), psum[:, 7, :], ACT.Copy).then_inc(hT_ready, 1)
                act.wait_ge(quads_read, base + 5)
                fn(dd[:, 0, :], psum[:, 4, :], ACT.Copy).then_inc(d0_ready, 1)

            def moe_round(r):
                with act.Fori(0, NG // 2) as pair:
                    for gp in range(2):
                        moe_group(r, pair, gp)

            act.wait_ge(count_ready, 1)
            moe_round(0)
            most = act.value_load(cnt[0:1, 0:1], min_val=0, max_val=T)
            with act.Fori(1, ROUNDS) as r:
                with act.If(most > r * CAP):
                    moe_round(r)
            squares(4, lambda t: act.wait_ge(resid_ready, t + 1))

        @block.vector
        def _(dve):
            v = Steps(dve, dve_step)
            link = v.link
            empty = lambda ins, *key: v.empty("dve", ins, *key)
            tt, ts, stt = nc.vector.tensor_tensor, nc.vector.tensor_scalar, nc.vector.scalar_tensor_tensor
            red = nc.vector.tensor_reduce

            roots = [0]

            def root(ins, ap):
                ins.then_inc(var_ready, 1)
                roots[0] += 1
                dve.wait_ge(root_ready, roots[0])
                link(nc.vector.reciprocal(ap, ap))

            def norm(n):
                for t in range(NT):
                    dve.wait_ge(rms_ready, NT * n + t + 1)
                    s = st[:, 2 * n + t:2 * n + t + 1]
                    link(nc.vector.reciprocal(s, s))
                    ts(xn[:, t, :], x[:, t, :], s, None, ALU.mult).then_inc(xn_ready, 1)

            highs = [0]

            def norm_T(n, *weights):
                places = [(t, h) for t in range(NT) for h in range(2)]
                view = lambda f, t, h: f[:, 4 * h:4 * h + 4, t * P:(t + 1) * P]
                for t, h in places:
                    wait_filled(dve, "nt", n, t, h)
                    gain = colp(f"norm{n}")[:, 4 * h:4 * h + 4].unsqueeze(2).to_broadcast([P, 4, P])
                    empty(tt(view(featL if n < 3 else featT, t, h),
                             bank("nt", n, t, h).rearrange("p (k q) -> p k q", k=4), gain, ALU.mult), "nt", n, t, h)
                for g in weights:
                    low_part(dve, tt, g)
                if n < 3:
                    for t, h in places:
                        highs[0] += 1
                        dve.wait_ge(feat_hi, highs[0])
                        low = view(featL, t, h)
                        tt(view(featLR, t, h), low, view(featR, t, h).bitcast(F32), ALU.subtract).then_inc(feat_lo, 1)

            def low_moved(*key):
                h, t = key[1:] if key[0] == "oT" else (key[2], key[1])
                highs[0] += 1
                dve.wait_ge(feat_hi, highs[0])
                empty(tt(featLR[:, 4 * h:4 * h + 4, t * P:(t + 1) * P], bank(*key).rearrange("p (k q) -> p k q", k=4),
                         featR[:, 4 * h:4 * h + 4, t * P:(t + 1) * P].bitcast(F32), ALU.subtract), *key)

            def bc(ap, n):
                return ap.unsqueeze(len(ap.shape)).to_broadcast([*ap.shape, n])

            for k, e in enumerate((EPS, 1e-5, 64e-5)):
                nc.vector.memset(eps_col[:, k:k + 1], e).then_inc(eps_ready, 1)
            dve.wait_ge(ident_in, 32)
            norm(0)
            norm_T(0, 0)
            for g in range(1, 6):
                low_part(dve, tt, g)
            tmp = area(L1, "prob", 4, 512)[:, 0:2, :]
            for units_, (s_lo, s_n), lows in zip((((0, 0, 8), (1, 512, 8)), ((3, 1536, 8), (4, 2048, 2))), QK_SUMS, ((6, 7), ())):
                at = s_lo
                sums_of = []
                for u, lo, H in units_:
                    wait_emptied(dve, "p1", u, 0 if u == 4 else 1)
                    q = nat[:, :, lo:lo + 64 * H]
                    link(tt(tmp[:, :, 0:64 * H], q, q, ALU.mult))
                    s = st[:, at:at + 2 * H].rearrange("p (t h) -> p t h", t=NT)
                    at += 2 * H
                    sums_of.append(s)
                    ins = red(s, tmp[:, :, 0:64 * H].rearrange("p t (h d) -> p t h d", h=H), AX, ALU.add)
                    if at < s_lo + s_n:
                        link(ins)
                        for g in lows:
                            low_part(dve, tt, g)
                root(ins, st[:, s_lo:s_lo + s_n])
                for u, lo, H in units_:
                    s_both = sums_of.pop(0)
                    for t in range(NT):
                        s = s_both[:, t]
                        q3 = nat[:, t, lo:lo + 64 * H].rearrange("p (h d) -> p h d", h=H)
                        if u == 4:
                            dst = kdup[:, t].rearrange("p v (c d) -> p v c d", c=2)
                            tt(dst, q3.unsqueeze(2).to_broadcast([P, 2, 2, 64]), bc(bc(s, 2), 64), ALU.mult)                                .then_inc(qk_ready, 1)
                        else:
                            tt(q3, q3, bc(s, 64), ALU.mult).then_inc(qk_ready, 1)
                if lows:
                    low_part(dve, tt, 8)
                    dve.wait_ge(params_in, PARAMS_IN)
                    dve.wait_ge(biasA_in, 16 * 16)
                    flat = biasA.rearrange("p h j k -> p (h j) k")
                    link(tt(flat, flat, con("winm").unsqueeze(1).to_broadcast([P, 48, 64]), ALU.mult))
                    link(tt(flat, flat, con("wina").unsqueeze(1).to_broadcast([P, 48, 64]), ALU.add))
            low_part(dve, tt, chunk_of[("p1", 5), 0])

            def softmax_in(i):
                br, t, g = i // 4, i // 2 % 2, i % 2
                for par in range(2):
                    wait_filled(dve, "S", i, par)
                    if i >= 2:
                        wait_filled(dve, "PT", i - 2, par)
                    if br:
                        b = biasB[:, 4 * g + par:4 * g + par + 3:2, P - P * t:P - P * t + T]
                    else:
                        b = biasA[:, 4 * g + par:4 * g + par + 3:2, 2 - 2 * t:6 - 2 * t, :].rearrange("p h j k -> p h (j k)")
                    pr = prob[:, i % 2, par]
                    empty(stt(pr, bank("S", i, par).rearrange("p (a k) -> p a k", a=2), HD ** -0.5, b, ALU.mult, ALU.add),
                          "S", i, par)
                    k = 4 * i + 2 * par
                    m = negmax[:, k:k + 2]
                    link(red(m, pr, AX, ALU.max))
                    if br:
                        sk = row("sink")[:, 4 * g + par:4 * g + par + 3:2]
                        link(tt(m, m, sk, ALU.max))
                        link(tt(esink[:, k:k + 2], sk, m, ALU.subtract))
                    ts(m, m, -1.0, None, ALU.mult).then_inc(max_ready, 1)

            def weighted(i):
                br, t, g = i // 4, i // 2 % 2, i % 2
                wait_filled(dve, "PT", i, 1)
                empty(nc.vector.tensor_copy(probT[:, 2 * (i % 2) + 1].rearrange("p a k q -> p (a k q)"), bank("PT", i, 1)),
                      "PT", i, 1)
                if i == 7:
                    for key in ((0, 0), (0, 1), (1, 0)):
                        low_moved("oT", *key)
                s = sums[:, 4 * i:4 * i + 4]
                dve.wait_ge(exp_ready, 2 * i + 2)
                if br:
                    link(tt(s, s, esink[:, 4 * i:4 * i + 4], ALU.add))
                link(nc.vector.reciprocal(s, s))
                wait_filled(dve, "PV", i)
                dst = xn[:, t, 512 * br + 256 * g:512 * br + 256 * g + 256].rearrange("p (a b d) -> p a b d", a=2, b=2)
                empty(tt(dst, bank("PV", i)[:, 0:256].rearrange("p (a b d) -> p a b d", a=2, b=2),
                         bc(s.rearrange("p (b a) -> p a b", b=2), 64), ALU.mult), "PV", i)

            for i in range(9):
                if i == 4:
                    dve.wait_ge(biasB_in, 16)
                if i < 8:
                    softmax_in(i)
                if i == 0:
                    low_part(dve, tt, chunk_of[("p1", 5), 1])
                if i >= 1:
                    weighted(i - 1)
            for br in range(2):
                if br == 1:
                    low_moved("oT", 1, 1)
                for n in range(2):
                    for t in range(NT):
                        wait_filled(dve, "br", br, n, t)
                        dve.wait_ge(gates_ready, br + 1)
                        g = sig[:, t, 1024 * br + 512 * n:1024 * br + 512 * n + 512]
                        empty(tt(g, g, bank("br", br, n, t), ALU.mult), "br", br, n, t)
                        if br:
                            ya = sig[:, t, 512 * n:512 * n + 512]
                            tt(ya, ya, g, ALU.add).then_inc(y_ready, 1)
            for h in range(2):
                for t in range(NT):
                    low_moved("yT", t, h)

            first = {n: chunk_of[n, 0] for n in (("ffn", 0), ("down", 0), ("rw", 3))}
            for n in range(4):
                wait_filled(dve, "wo", n // 2, n % 2)
                xs = x[:, :, 256 * n:256 * n + 256]
                empty(tt(xs, xs, bank("wo", n // 2, n % 2).rearrange("p (t n) -> p t n", t=NT), ALU.add), "wo", n // 2, n % 2)
            norm(1)
            norm_T(1)
            for u in range(FFK // 2):
                low_part(dve, tt, first["ffn", 0] + 2 * u + 4)
                wait_filled(dve, "up", u)
                wait_emptied(dve, "gate", u)
                h = hTl[:, 2 * u:2 * u + 2, :]
                empty(tt(h.rearrange("p f t -> p (f t)"), silu_t[:, u % 2, :], bank("up", u), ALU.mult), "up", u)
                low_part(dve, tt, first["ffn", 0] + 2 * u + 5)
                dve.wait_ge(hT_hi, u + 1)
                tt(hT_parts[1][:, 2 * u:2 * u + 2, :], h, hT_parts[0][:, 2 * u:2 * u + 2, :].bitcast(F32), ALU.subtract).then_inc(hT_lo, 1)
            for g in range(first["down", 0] + 4, first["rw", 3] + 1):
                low_part(dve, tt, g)
            for t in range(NT):
                for n in range(2):
                    wait_filled(dve, "down", t, n)
                    xs = x[:, t, 512 * n:512 * n + 512]
                    empty(tt(xs, xs, bank("down", t, n), ALU.add), "down", t, n)

            link(nc.vector.memset(fT[:, :, 0:1], 0.0))
            norm(2)
            norm_T(2)

            def lerp(c0, n, diff=dtmp):
                wait_emptied(dve, "rw", c0 // 2 + (n - 1) // 2)
                cur = fT[:, c0:c0 + n, 1:257]
                link(tt(diff[:, 0:n, :], fT[:, c0:c0 + n, 0:256], cur, ALU.subtract))
                for c in range(n):
                    link(stt(fT[:, c0 + c, 1:257], diff[:, c, :], colp("mu", c0 + c), fT[:, c0 + c, 1:257],
                             ALU.mult, ALU.add))

            def percol(name):
                return bc(colp(name), T)

            lerp(12, 2)
            dve.sem_inc(lerp_ready, 1)
            lerp(4, 4)
            tt(kk, f_k, percol("k_k"), ALU.mult).then_inc(kk_ready, 1)
            wait_emptied(dve, "z", 1)
            for c in range(4):
                link(nc.vector.tensor_tensor_scan(Ls[:, c, :], con("reset"), sw[:, c, :], 0.0, ALU.mult, ALU.add))
            tt(Le, Ls, sw, ALU.subtract).then_inc(scan_ready, 1)
            wait_emptied(dve, "za", 1)
            for c in range(4):
                link(ts(dtmp[:, c, :], sa[:, c, :], 1.0, colp("k_a", c), ALU.subtract, ALU.mult))
            wait_emptied(dve, "ss", 1)
            link(ts(kk2, kk2, 1e-12, None, ALU.max))
            link(nc.vector.reciprocal(kk2, kk2))
            link(tt(kk, kk, kk2, ALU.mult))
            link(stt(kp, dtmp, 1.0, f_k, ALU.add, ALU.mult))
            link(tt(sa, kk, sa, ALU.mult))
            lerp(0, 4)
            link(tt(rk, f_r, kp, ALU.mult))
            link(tt(rk, rk, percol("r_k"), ALU.mult))
            dve.wait_ge(decay_ready, 1)
            link(nc.vector.tensor_copy(PC[:], Ein.rearrange("p f (c s) -> p f c s", c=NCH)[:, :, :, CH - 1]))
            link(stt(At, kk, -1.0, Eex, ALU.mult, ALU.mult))
            link(tt(Bt, sa, Einv, ALU.mult))
            link(tt(f_k, kp, Einv, ALU.mult))
            link(tt(f_r, f_r, Ein, ALU.mult))
            for dst, src in ((BhT, Bt), (KhT, f_k)):
                for c in range(4):
                    ins = tt(dst[:, c, :].rearrange("p (c s) -> p c s", c=NCH), src[:, c, :].rearrange("p (c s) -> p c s", c=NCH),
                             bc(PC[:, c, :], CH), ALU.mult)
                    link(ins)
            lerp(8, 4, kk)
            dve.sem_inc(rw_ready, 1)
            for t in range(NT):
                wait_emptied(dve, "p2", 1, 1)
                if t == 0:
                    wait_filled(dve, "nt", 2, 1, 1)
                xy = retn[:, t, 0:1024].rearrange("p (h c d) -> p h c d", h=8, c=2)
                x1, x2 = xy[:, :, 0, :], xy[:, :, 1, :]
                w4 = xn[:].rearrange("p t (a h d) -> p (t a) h d", a=2, h=8)
                cos = con("cos")[:, 64 * t:64 * t + 64].unsqueeze(1).to_broadcast([P, 8, 64])
                sin = con("sin")[:, 64 * t:64 * t + 64].unsqueeze(1).to_broadcast([P, 8, 64])
                link(tt(w4[:, 0], x1, cos, ALU.mult))
                link(tt(w4[:, 1], x2, sin, ALU.mult))
                link(tt(w4[:, 2], x1, sin, ALU.mult))
                link(tt(w4[:, 3], x2, cos, ALU.mult))
                link(tt(x1, w4[:, 0], w4[:, 1], ALU.subtract))
                tt(x2, w4[:, 2], w4[:, 3], ALU.add).then_inc(rot_ready, 1)
            for j in range(3):
                wait_filled(dve, "rs", j)
                dst = (rsc[0][:, 2 * j:2 * j + 2, :] if j < 2 else rsc[1]).rearrange("p a b -> p (a b)")
                lo = CST["dec"][0] + 512 * j
                empty(tt(dst, bank("rs", j), cst[:, lo:lo + 512], ALU.mult), "rs", j)

            def head_norm(y, work, H, src, emptied_key):
                d = 512 // H
                per = lambda ap: ap.rearrange("p (h d) -> p h d", h=H)
                s = st[:, 32:32 + H]
                q = st[:, 48:48 + H]
                link(red(s, per(src), AX, ALU.add))
                link(ts(s, s, 1.0 / d, None, ALU.mult))
                ins = tt(per(y), per(src), bc(s, d), ALU.subtract)
                if emptied_key:
                    empty(ins, *emptied_key)
                else:
                    link(ins)
                link(tt(work, y, y, ALU.mult))
                root(red(q, per(work), AX, ALU.add), q)
                link(tt(per(y), per(y), bc(q, d), ALU.mult))

            dve.wait_ge(rot_ready, NT)
            for t in range(NT):
                wait_filled(dve, "ro", t)
                y = xn[:, t, 0:512]
                head_norm(y, xn[:, t, 512:1024], RET_H, bank("ro", t), ("ro", t))
                link(tt(y, y, row("ret_gn"), ALU.mult))
                wait_emptied(dve, "p2", 3, 1)
                tt(y, y, retn[:, t, 1536:2048], ALU.mult).then_inc(mixed_ready, 1)
            wait_filled(dve, "bonus")
            empty(nc.vector.tensor_copy(bonus, bank("bonus")[:, 0:16]), "bonus")

            def masked(dst, name, m, t, par, last):
                mask = con(m).unsqueeze(1).to_broadcast([P, 4, P])
                ins = tt(dst[:, t, 4 * par:4 * par + 4, :], bank("mat", name, t, par).rearrange("p (i q) -> p i q", i=4),
                         mask, ALU.mult)
                if last:
                    empty(ins, "mat", name, t, par)

            def mat(name, *outs):
                for t in range(NT):
                    for par in range(2):
                        wait_filled(dve, "mat", name, t, par)
                        for n, (dst, m) in enumerate(outs):
                            masked(dst, name, m, t, par, n == len(outs) - 1)

            dve.wait_ge(mixed_ready, NT)
            mat("AT", (AdT, "mAdT"), (o16T, "m16T"), (o32T, "m32T"))
            for t in range(NT):
                for par in range(2):
                    wait_filled(dve, "mat", "A", t, par)
                    masked(Ad, "A", "mAd", t, par, True)
                    hs = slice(4 * par, 4 * par + 4)
                    tt(X[:, t, hs, :], Ad[:, t, hs, :], ident.unsqueeze(1).to_broadcast([P, 4, P]), ALU.add)\
                        .then_inc(x0_ready, 1)
            dst = {"P2T": P2T, "P4T": P4T}
            extra = {"Aak": (AakT, "mlt"), "Arb": (ArbT, "mle"), "Ark": (ArkT, "mle")}
            for name, who in INVERSE:
                if who == "dve":
                    for t in range(NT):
                        for par in range(2):
                            key = ("inv", name, t, par)
                            wait_filled(dve, *key)
                            hs = slice(4 * par, 4 * par + 4)
                            flat = lambda m: m[:, t, hs, :].rearrange("p i q -> p (i q)")
                            if name in dst:
                                empty(nc.vector.tensor_copy(flat(dst[name]), bank(*key)), *key)
                            else:
                                dve.wait_ge(x0_ready, 2 * t + par + 1)
                                empty(tt(flat(X), flat(X), bank(*key), ALU.add), *key)
                for e in INV_EXTRA.get(name, ()):
                    mat(e, extra[e])
            for c in range(NCH):
                r = slice(64 * (c % 2), 64 * (c % 2) + 64)
                wait_filled(dve, "U", c, 0)
                empty(nc.vector.tensor_copy(Un[r, c // 2, 0, :], bank("U", c, 0)[r, 0:256]), "U", c, 0)
                if c < NCH - 1:
                    if c:
                        link(tt(S[:, c + 1], S[:, c], bc(PC[:, :, c], 64), ALU.mult))
                    wait_filled(dve, "St", c)
                    b = bank("St", c)[:, 0:256].rearrange("p (i v) -> p i v", v=64)
                    if c == 0:
                        empty(nc.vector.tensor_copy(S[:, 1], b), "St", 0)
                    else:
                        empty(tt(S[:, c + 1], S[:, c + 1], b, ALU.add), "St", c)
            for t in range(NT):
                for par in range(2):
                    wait_emptied(dve, "Y", t, par)
                y, w = ynat[:, t, :], ytmp[:, t, :]
                per = lambda ap: ap.rearrange("p (h d) -> p h d", h=RW_H)
                head_norm(y, w, RW_H, y, None)
                link(tt(y, y, row("rw_gn"), ALU.mult))
                link(tt(per(w), per(natl["V"][:, t, :]), bc(bonus[:, 8 * t:8 * t + 8], 64), ALU.mult))
                link(tt(y, y, w, ALU.add))
                wait_emptied(dve, "gn", t)
                tt(xn[:, t, 512:1024], y, gnat[:, t, :], ALU.mult).then_inc(mixed_ready, 1)
            for n in range(2):
                for t in range(NT):
                    wait_filled(dve, "wo2", n, t)
                    xs = x[:, t, 512 * n:512 * n + 512]
                    empty(tt(xs, xs, bank("wo2", n, t), ALU.add), "wo2", n, t)
            norm(3)
            norm_T(3)
            at = [192]

            def work(*shape):
                n = int(np.prod(shape))
                ap = rt[:, at[0]:at[0] + n]
                at[0] += n
                if len(shape) == 2:
                    ap = ap.rearrange("p (a b) -> p a b", a=shape[0])
                if len(shape) == 3:
                    ap = ap.rearrange("p (a b c) -> p a b c", a=shape[0], b=shape[1])
                return ap

            lg = work(NT, 36)
            ml = work(NT, E)
            eq = work(NT, E)
            oh1 = work(NT, E)
            oh4 = work(NT, 4)
            c4 = work(NT, 4)
            assert at[0] <= 480
            e4 = rt[:, 480:488].rearrange("p (a b) -> p a b", a=NT)
            e2 = rt[:, 488:490]
            gm, m1, m2, cm, gp, w1, w2 = (rt[:, 496 + 2 * n:498 + 2 * n] for n in range(7))
            oh2 = rt[:, 512:576].rearrange("p (t e) -> p t e", t=NT)
            for t in range(NT):
                wait_filled(dve, "logit", t)
                empty(tt(lg[:, t, :], bank("logit", t)[:, 0:36], row("brt"), ALU.add), "logit", t)

            def first_max(dst, vals, mx, scratch_, desc, n):
                link(red(mx, vals, AX, ALU.max))
                link(tt(scratch_, vals, bc(mx, n), ALU.is_equal))
                link(tt(scratch_, scratch_, con(desc).unsqueeze(1).to_broadcast([P, NT, n]), ALU.mult))
                link(red(cm, scratch_, AX, ALU.max))
                link(tt(dst, scratch_, bc(cm, n), ALU.is_equal))

            l4, l32 = lg[:, :, 0:4], lg[:, :, 4:36]
            first_max(oh4, l4, gm, c4, "desc4", 4)
            link(tt(e4, l4, bc(gm, 4), ALU.subtract))
            link(tt(ml.rearrange("p t (g e) -> p t g e", g=4), l32.rearrange("p t (g e) -> p t g e", g=4), bc(oh4, 8), ALU.mult))
            link(ts(c4, oh4, 1.0, -NEG, ALU.subtract, ALU.mult))
            ml4 = ml.rearrange("p t (g e) -> p t g e", g=4)
            link(tt(ml4, ml4, bc(c4, 8), ALU.add))
            first_max(oh1, ml, m1, eq, "desc32", E)
            link(stt(ml, oh1, 3 * NEG, ml, ALU.mult, ALU.add))
            first_max(oh2, ml, m2, eq, "desc32", E)
            link(tt(e2, m2, m1, ALU.subtract))
            tt(selr, oh1, oh2, ALU.add).then_inc(route_ready, 1)
            dve.wait_ge(exp_ready, 16 + 1)
            link(red(gp, e4, AX, ALU.add))
            link(nc.vector.reciprocal(gp, gp))
            link(ts(w1, e2, 1.0, None, ALU.add))
            link(nc.vector.reciprocal(w1, w1))
            link(tt(w1, w1, gp, ALU.mult))
            link(tt(w2, w1, e2, ALU.mult))
            link(tt(oh1, oh1, bc(w1, E), ALU.mult))
            link(tt(oh2, oh2, bc(w2, E), ALU.mult))
            link(tt(comb, oh1, oh2, ALU.add))
            for t in range(NT):
                wait_filled(dve, "rank", t)
                dve.wait_ge(route_ready, 1)
                link(ts(rank[:, t, :], bank("rank", t)[:, 0:E], 1000.0, None, ALU.add))
                empty(stt(rank[:, t, :], rank[:, t, :], 1.0, selr[:, t, :], ALU.mult, ALU.mult), "rank", t)
                link(ts(rank[:, t, :], rank[:, t, :], -1000.0, None, ALU.add))
            wait_filled(dve, "count")
            empty(red(rt[:, 492:493], bank("count")[:, 0:E], AX, ALU.max), "count")
            nc.vector.tensor_copy(cnt[:, 0:1], rt[:, 492:493]).then_inc(count_ready, 1)
            dve.wait_ge(mixed_ready, 2 * NT)
            link(nc.vector.memset(dd, 0.0))
            nc.vector.memset(GT, 0.0).then_inc(gt_ready, 1)

            def moe_group(r, pair, gp_):
                n = r * NG + pair * 2 + gp_
                base = r * ALLQ + pair * 12 + gp_ * 6
                e0 = pair * (2 * EG) + gp_ * EG
                es = slice(e0, e0 + EG) if isinstance(e0, int) else bass.ds(e0, EG)
                s0 = moe_base + n * MOE_STEPS
                nc.vector.tensor_copy(rank4.rearrange("p (t e) -> p t e", t=NT), rank[:, :, es]).then_inc(dve_step, 1)
                nc.vector.tensor_copy(comb4.rearrange("p (t e) -> p t e", t=NT), comb[:, :, es]).then_inc(dve_step, 1)
                dve.wait_ge(dve_step, s0 + 2)
                slots = con("slot").unsqueeze(1).to_broadcast([P, NT * EG, CAP])
                flat = lambda m: m.rearrange("p t e s -> p (t e) s")
                tt(flat(G), slots, bc(rank4, CAP), ALU.is_equal).then_inc(dve_step, 1)
                dve.wait_ge(dve_step, s0 + 3)
                ins = tt(flat(Gw), flat(G), bc(comb4, CAP), ALU.mult)
                ins.then_inc(onehot_ready, 1)
                for kb in range(2):
                    dve.wait_ge(gathered, 2 * n + kb + 1)
                    gain = bc(colp("norm3")[:, 4 * kb:4 * kb + 4], P)
                    tt(xg[:, 4 * kb:4 * kb + 4, :], psum[:, 6 + kb, :].rearrange("p (k s) -> p k s", k=4), gain, ALU.mult)\
                        .then_inc(xg_ready, 1)
                dve.wait_ge(quads_read, base + 4)
                dve.wait_ge(silu_ready, n + 1)
                tt(hh, sg, psum[:, 5, :], ALU.mult).then_inc(h_ready, 1)
                dve.wait_ge(gt_filled, n + 1)
                dve.wait_ge(scattered, n + 1)
                nc.vector.tensor_copy(GT.rearrange("p t q -> p (t q)"), psum[:, 6, 0:2 * P]).then_inc(gt_ready, 1)
                dve.wait_ge(quads_read, base + 6)
                nc.vector.tensor_copy(dd[:, 1, :], psum[:, 5, :]).then_inc(d1_ready, 1)

            MOE_STEPS = 3
            moe_base = v.n

            def moe_round(r):
                with dve.Fori(0, NG // 2) as pair:
                    for g in range(2):
                        moe_group(r, pair, g)

            dve.wait_ge(gt_ready, 1)
            moe_round(0)
            dve.wait_ge(count_ready, 1)
            most = dve.value_load(cnt[0:1, 0:1], min_val=0, max_val=T)
            with dve.Fori(1, ROUNDS) as r:
                with dve.If(most > r * CAP):
                    ts(rank, rank, -float(CAP), None, ALU.add).then_inc(shifted, 1)
                    dve.wait_ge(shifted, r)
                    nc.vector.memset(rt[:, 495:496], 0.0)
                    moe_round(r)
            dve.wait_ge(moe_done, 1)
            for t in range(NT):
                for n in range(2):
                    xs = x[:, t, 512 * n:512 * n + 512]
                    tt(xs, xs, psum[:, 2 * t + n, :], ALU.add).then_inc(sum_done, 1)
                dve.wait_ge(sum_done, 2 * t + 2)
                dve.sem_inc(resid_ready, 1)
            dve.wait_ge(gain_in, 16)
            for t in range(NT):
                dve.wait_ge(rms_ready, NT * 4 + t + 1)
                s = st[:, 8 + t:9 + t]
                nc.vector.reciprocal(s, s).then_inc(sum_done, 1)
                dve.wait_ge(sum_done, 4 + t + 1)
                gain = featT[:, 0:4, :].rearrange("p a b -> p (a b)")
                stt(xn[:, t, :], x[:, t, :], s, gain, ALU.mult, ALU.mult).then_inc(out_ready, 1)


def kernel(**inputs):
    import concourse.bacc as _bacc
    from concourse.bass_utils import run_bass_kernel_spmd as _run

    g = {k: np.asarray(v) for k, v in inputs.items()}
    pk = lambda a: np.ascontiguousarray(a.reshape(-1, P).T)
    two = lambda a: np.concatenate([a[0], a[0]])[:, None]
    arrays = {
        "x": g["x"][0],
        "cst": constants(),
        "onehot": t5_one_hot(),
        "cols": np.concatenate([
            pk(g["norm_mix"][0]), pk(g["norm_ffn"][0]), pk(g["norm1_gain_2"][0]), pk(g["norm2_gain_2"][0]),
            two(g["q_norm_a"]), two(g["k_norm_a"]), two(g["q_norm_b"]), two(g["k_norm_b"]),
            pk(g["rwkv_mu_2"][0]), pk(g["rwkv_w0_2"][0]), pk(g["rwkv_a0_2"][0]), pk(g["rwkv_k_k_2"][0]),
            pk(g["rwkv_k_a_2"][0]), pk(g["rwkv_r_k_2"][0].reshape(-1))], 1),
        "rows": np.concatenate([g["sink_b"][0], g["b_route_group_2"][0], g["b_route_expert_2"][0],
                                g["ret_gn_gain_2"][0], g["rwkv_gn_gain_2"][0]])[None, :],
        "final_gain": g["final_norm_gain_2"][None, :],
        "rpb": g["rpb_a"][0].transpose(2, 0, 1).reshape(8, -1),
        "t5": np.concatenate([g["t5_table"], np.ones((1, 8), np.float32)]),
        "lora": np.concatenate([g["rwkv_w_up_2"][0], g["rwkv_a_up_2"][0]]),
        "gup": g["rwkv_g_up_2"][0],
        "wr": np.concatenate([g["w_route_group_2"][0], g["w_route_expert_2"][0]], 1),
    }
    for name in ("w_in", "w_branch_a", "w_branch_b", "w_out", "w_gate", "w_up", "w_down", "w_in_2", "w_out_2",
                 "w_gate_2", "w_up_2", "w_down_2"):
        arrays[name] = g[name][0]
    arrays = {k: np.ascontiguousarray(a) for k, a in arrays.items()}
    nc = _bacc.Bacc("TRN2", target_bir_lowering=False, num_devices=1)
    A = {k: nc.dram_tensor(f"in_{k}", a.shape, F32, kind="ExternalInput").ap() for k, a in arrays.items()}
    out = nc.dram_tensor("out", (T, D), F32, kind="ExternalOutput").ap()
    build(nc, A, out)
    r = _run(nc, [{f"in_{k}": a for k, a in arrays.items()}], core_ids=[0])
    return r.results[0]["out"].reshape(1, T, D)
```

```python
from contextlib import ExitStack

import numpy as np

import concourse.bass as bass
from concourse import mybir

F32 = mybir.dt.float32
F32R = mybir.dt.float32r
I32 = mybir.dt.int32
ALU = mybir.AluOpType
ACT = mybir.ActivationFunctionType
AX = mybir.AxisListType.X

P = 128
T = 256
NT = T // P
D = 1024
DK = D // P
HD = 64
GRID_W = 64
EPS = 1e-6
NEG = -1e30
CHOSEN = 1024.0

A_W = 512
NQKV = 3 * A_W + 512 + 256
FFN = 2816
FFK = FFN // P
REL = 2 * T - 1
EXT = T + P
KW = 16
RET_H, RET_D = 4, 128
RW_H = 8
CH = 64
NCH = T // CH
DECAY = float(np.exp(-0.5))
FTC = 14
E = 32
EG = 4
CAP = 32
NG = E // EG
DE = 512
ROUNDS = T // CAP
QK_SUMS = ((192, 32), (224, 20))

SLOT = 4096
NSLOT = 3
QUAD = 2 * SLOT
NQ = 4
B0 = NSLOT * SLOT


def layout(*fields, base=0):
    at, out = base, {}
    for name, size in fields:
        out[name] = (at, at + size)
        at += size
    out["end"] = at
    return out


L1 = layout(("nat", NT * NQKV), ("sig", NT * 2048), ("biasA", 8 * 6 * 64), ("biasB", 8 * EXT),
            ("qaT", 1024), ("kaT", 1024), ("qbT", 1024), ("kbT", 512), ("prob", 2048), ("probT", 2048),
            ("spare", 2048), base=B0)
LF = layout(("hTh", FFK * T), ("hTl", FFK * T), ("silu", 1024), base=B0)
LM = layout(("M", 14 * 1024), ("fT", FTC * 257), ("RT", 2048), ("gap", 498), ("N", 4096), base=B0)
LE = layout(("G", 256), ("Gw", 256), ("GT", 256), ("sg", 512), ("h", 512), ("hT", 512), base=NQ * QUAD)
ARENA = max(L1["end"], LM["end"], LE["end"])
CHUNK = 2048


def place(lo):
    return (lo, lo + CHUNK // 2)


W_SIG = (place(L1["sig"][0]), place(L1["sig"][0] + CHUNK))
W_QK = place(L1["qaT"][0])
W_NAT = (L1["nat"][0], L1["nat"][0] + NQKV)
W_PROB, W_PROBT, W_SPARE = (place(L1[n][0]) for n in ("prob", "probT", "spare"))
W_RING = (place(SLOT), place(SLOT + CHUNK), place(LM["M"][0] + CHUNK))
W_FFN = place(LF["end"])
assert LM["N"] == (W_PROBT[0], W_SPARE[0] + CHUNK) and L1["prob"][0] >= LF["end"] + 3 * CHUNK

CST = layout(("ident", 128), ("reset", T), ("winm", 64), ("wina", 64), ("slot", CAP), ("desc", 8),
             ("mAdT", 128), ("mAd", 128), ("m16T", 128), ("m32T", 128), ("mlt", 128), ("mle", 128),
             ("same", 128), ("sel", 2), ("before", 128), ("ones", 128), ("cos", 128), ("sin", 128),
             ("dec", 1536))
COLS = layout(("norm0", 8), ("norm1", 8), ("norm2", 8), ("norm3", 8), ("qa", 1), ("ka", 1), ("qb", 1), ("kb", 1),
              ("mu", FTC), ("w0", 4), ("a0", 4), ("k_k", 4), ("k_a", 4), ("r_k", 4))
ROWS = layout(("sink", 8), ("brt", 36), ("ret_gn", 512), ("rw_gn", 512))


def constants():
    c = np.zeros((P, CST["end"]), np.float32)

    def put(name, a):
        lo, hi = CST[name]
        c[:, lo:hi] = np.asarray(a, np.float32).reshape(P, hi - lo)

    p, i = np.arange(P)[:, None], np.arange(P)[None, :]
    put("ident", p == i)
    put("reset", np.broadcast_to(np.arange(T) % CH != 0, (P, T)))
    col, key = p % GRID_W, np.arange(GRID_W)[None, :]
    start = np.clip(col - KW // 2, 0, GRID_W - KW)
    win = (key >= start) & (key < start + KW)
    put("winm", win)
    put("wina", np.where(win, 0.0, NEG))
    put("slot", np.broadcast_to(CHOSEN + np.arange(CAP), (P, CAP)))
    put("desc", np.broadcast_to(np.arange(8, 0, -1), (P, 8)))
    put("mAdT", (p < i) & (p // 16 == i // 16))
    put("mAd", (i < p) & (p // 16 == i // 16))
    put("m16T", (p < i) & (p // 32 == i // 32) & (p // 16 != i // 16))
    put("m32T", (p < i) & (p // 64 == i // 64) & (p // 32 != i // 32))
    put("mlt", (p < i) & (p // 64 == i // 64))
    put("mle", (p <= i) & (p // 64 == i // 64))
    put("same", p // 64 == i // 64)
    put("sel", p // 64 == np.arange(2)[None, :])
    put("before", p < i)
    put("ones", np.ones((P, P)))
    half = RET_D // 2
    inv = np.float32(10000.0) ** (-np.arange(half, dtype=np.float32) / np.float32(half))
    ang = np.arange(T, dtype=np.float32)[:, None] * inv[None, :]
    tile = lambda a: a.reshape(NT, P, -1).transpose(1, 0, 2)
    put("cos", tile(np.cos(ang)))
    put("sin", tile(np.sin(ang)))
    logg = np.log(1.0 - np.exp2(-5.0 - np.arange(RET_H)))
    t = np.arange(T)
    seen = (t[:, None] // CH) <= (t[None, :] // CH)
    dec = np.exp(logg[:, None, None] * np.abs(t[None, :, None] - t[None, None, :])) * seen * RET_D ** -0.5
    first = dec[:, :P, :].transpose(1, 0, 2).reshape(P, -1)
    second = dec[:, P:, P:].transpose(1, 0, 2).reshape(P, -1)
    put("dec", np.concatenate([first, second], 1))
    return c


def t5_one_hot():
    rel = np.arange(-(T - 1), T)
    half, exact = 16, 8
    n = np.abs(rel)
    large = exact + (np.log(np.maximum(n, 1) / exact) / np.log(128 / exact) * (half - exact)).astype(np.int32)
    bucket = (rel > 0) * half + np.where(n < exact, n, np.minimum(large, half - 1))
    m = np.zeros((33, REL), np.float32)
    m[bucket, np.arange(REL)] = 1.0
    m[32] = np.where(n <= 128, 0.0, NEG)
    return m


def plan_fills():
    f = []

    def add(who, *key):
        f.append((key, who))

    def norm():
        for t in range(NT):
            for b in range(2):
                add("dve", "nt", 0, t, b)

    def turn_qk(*names):
        for s in names:
            for t in range(NT):
                add("act", "qkT", s, t)

    norm()
    for u in range(5):
        if u == 4:
            turn_qk("qa", "ka")
        for c in range(1 if u == 4 else 2):
            add("act", "p1", u, c)
        if u == 2:
            add("act", "t5")
    for i in range(9):
        if i < 8:
            add("dve", "S", i, 0)
            add("dve", "S", i, 1)
        if i >= 1:
            add("act", "PT", i - 1, 0)
            add("dve", "PT", i - 1, 1)
        if i < 8:
            if i == 0:
                turn_qk("qb", "kb")
            add("act", "p1", 5 + i // 2, i % 2)
        if i == 8:
            for key in ((0, 0), (0, 1), (1, 0)):
                add("dve", "oT", *key)
        if i >= 1:
            add("dve", "PV", i - 1)
    for br in range(2):
        if br == 1:
            add("dve", "oT", 1, 1)
        for n in range(2):
            for t in range(NT):
                add("dve", "br", br, n, t)
    for b in range(2):
        for t in range(NT):
            add("dve", "yT", t, b)
    for j in range(4):
        add("dve", "wo", j // 2, j % 2)
        if j:
            add("dve", "nt", 1, j - 1)
    add("dve", "nt", 1, 3)
    for u in range(FFK // 2):
        add("dve", "gate", u)
        if u == 0:
            add("act", "rb", 1)
        add("dve", "up", u)
    for n in range(2):
        for t in range(NT):
            add("dve", "down", t, n)
    for j in range(4):
        add("dve", "nt", 2, j)
    for c in RW_ORDER:
        add("dve", "rw", c)
        if c == 6:
            add("act", "rb", 2)
        if c == 3:
            for k in ("z", "za"):
                for b in range(2):
                    add("act", k, b)
        if c == 0:
            for b in range(2):
                add("act", "ss", b)
    for u in range(3):
        for c in range(2):
            add("act", "p2", u, c)
    for s in ("q", "k"):
        for t in range(NT):
            add("act", "rT", s, t)
    for j in range(3):
        add("dve", "rs", j)
    add("act", "p2", 3, 0)
    for t in range(NT):
        add("dve", "ro", t)
    add("act", "p2", 3, 1)
    for w in ("A", "B", "K", "V"):
        for t in range(NT):
            add("act", "natl", w, t)
    add("dve", "bonus")
    for m in ("AT", "A"):
        for t in range(NT):
            for par in range(2):
                add("dve", "mat", m, t, par)
    for n, (name, who) in enumerate(INVERSE):
        for t in range(NT):
            for par in range(2):
                add(who, "inv", name, t, par)
        for extra in INV_EXTRA.get(name, ()):
            for t in range(NT):
                for par in range(2):
                    add("dve", "mat", extra, t, par)
        if name == "Z2":
            for t in range(NT):
                add("act", "Q", t)
            for t in range(NT):
                add("act", "gn", t)
    for t in range(NT):
        add("act", "WT", t)
    for c in range(NCH):
        add("dve", "U", c, 0)
        add("act", "U", c, 1)
        for t, par in Y_AFTER.get(c, ()):
            add("act", "Y", t, par)
        if c < NCH - 1:
            add("dve", "St", c)
    for t in range(NT):
        for h in range(2):
            add("dve", "mT", t, h)
    for j in range(4):
        add("dve", "wo2", j // 2, j % 2)
        if j:
            add("dve", "nt", 3, j - 1)
    add("dve", "nt", 3, 3)
    for t in range(NT):
        add("dve", "logit", t)
    add("dve", "count")
    for t in range(NT):
        add("dve", "rank", t)
    return f


Y_AFTER = {2: ((0, 0),), 3: ((0, 1), (1, 0), (1, 1))}
RW_ORDER = (6, 2, 3, 0, 1, 4, 5)
INVERSE = (("P2", "act"), ("P2T", "dve"), ("X1", "dve"), ("P4", "act"), ("P4T", "dve"), ("X2", "dve"),
           ("P8T", "act"), ("X3", "dve"), ("T16T", "act"), ("Z1", "act"), ("X4", "dve"), ("T32T", "act"),
           ("Z2", "act"), ("X5", "dve"), ("TT", "act"))
INV_EXTRA = {"X3": ("Aak",), "T32T": ("Arb",), "TT": ("Ark",)}


def build(nc, A, out):
    fills = plan_fills()
    index = {key: n for n, (key, _) in enumerate(fills)}
    turn, seen = {}, {"act": 0, "dve": 0}
    for key, who in fills:
        turn[key] = seen[who]
        seen[who] += 1
    who_of = dict(fills)
    last = {index[key] % 8 for key in (("rank", 0), ("rank", 1), ("count",))}
    MB = [b for b in range(8) if b not in last]
    MB += sorted(last)

    with ExitStack() as ctx:
        def sb(name, shape, dt=F32):
            return ctx.enter_context(nc.sbuf_tensor(name, shape, dt))

        def sem(name):
            return ctx.enter_context(nc.semaphore(name))

        def sb_rounded(name, shape):
            offset = -(-nc.sbuf_base // 32) * 32
            whole = sb(name, shape)
            return whole, nc.alloc_sbuf_tensor_at(name + "_rounded", shape, F32R, offset=offset)

        arena_at = -(-nc.sbuf_base // 32) * 32
        arena = sb("arena", [P, ARENA])
        ring_r = nc.alloc_sbuf_tensor_at("ring_rounded", [P, NSLOT * SLOT], F32R, offset=arena_at)
        hi_r = {hi: nc.alloc_sbuf_tensor_at(f"hi_rounded_{n}", [P, 2 * (hi[1] - hi[0])], F32R, offset=arena_at + 4 * hi[0])
                for n, hi in enumerate((*W_SIG, *W_RING, W_QK, W_NAT, W_PROB, W_PROBT, W_SPARE, W_FFN))}
        x = sb("x", [P, NT, D])
        xn = sb("xn", [P, NT, D])
        featT, featR = sb_rounded("featT", [P, DK, T])
        featL, featLR = sb_rounded("featL", [P, DK, T])
        cst = sb("cst", [P, CST["end"]])
        cols = sb("cols", [P, COLS["end"]])
        rows = sb("rows", [P, ROWS["end"]])
        lora = sb("lora", [P, 512])
        gup = sb("gup", [P, 512])
        wr = sb("wr", [P, DK, 36])
        t5b = sb("t5b", [33, 8])
        st = sb("st", [P, 512])
        rt = sb("rt", [P, 1024])
        cnt = sb("cnt", [P, 2], I32)
        psum = ctx.enter_context(nc.psum_tensor("psum", [P, 8, 512], F32))

        def area(lay, name, *shape, of=None):
            lo, hi = lay[name]
            v = (arena if of is None else of)[:, lo:hi]
            if len(shape) == 2:
                v = v.rearrange("p (a b) -> p a b", a=shape[0])
            elif len(shape) == 3:
                v = v.rearrange("p (a b c) -> p a b c", a=shape[0], b=shape[1])
            elif len(shape) == 4:
                v = v.rearrange("p (a b c d) -> p a b c d", a=shape[0], b=shape[1], c=shape[2])
            return v

        def piece(lo, *shape, of=None):
            n = int(np.prod(shape))
            return area({"v": (lo, lo + n)}, "v", *shape, of=of)

        def con(name):
            lo, hi = CST[name]
            return cst[:, lo:hi]

        def colp(name, k=None):
            lo, hi = COLS[name]
            return cols[:, lo:hi] if k is None else cols[:, lo + k:lo + k + 1]

        def row(name):
            lo, hi = ROWS[name]
            return rows[:, lo:hi]

        ident = con("ident")
        nat = area(L1, "nat", NT, NQKV)
        sig = area(L1, "sig", NT, 2048)
        biasA = area(L1, "biasA", 8, 6, 64)
        biasB = area(L1, "biasB", 8, EXT)
        qaT, kaT, qbT = (area(L1, n, 4, T) for n in ("qaT", "kaT", "qbT"))
        kbT = area(L1, "kbT", 2, T)
        kdup = piece(L1["prob"][0] + 1024, NT, 2, P)
        negmax, esink, sums = (st[:, 64 + 32 * n:96 + 32 * n] for n in range(3))
        bonus = st[:, 160:176]
        eps_col = st[:, 176:179]
        warm = sb("warm", [P, 1])
        tanh_w = sb("tanh_w", [64, T])
        sig_g = sb("sig_g", [P, T])
        prob = area(L1, "prob", 2, 2, 2, T)
        probT = area(L1, "probT", 4, 2, 2, P)
        onehot = arena[0:33, L1["biasB"][0]:L1["biasB"][0] + REL]
        tb_sb = arena[0:8, L1["biasB"][0] + 512:L1["biasB"][0] + 512 + REL]
        hTh, hTl = (area(LF, n, FFK, T) for n in ("hTh", "hTl"))
        hT_parts = [nc.alloc_sbuf_tensor_at(n + "_rounded", [P, FFK, T], F32R, offset=arena_at + 4 * LF[n][0])
                    for n in ("hTh", "hTl")]
        silu_t = area(LF, "silu", 2, 512)
        router_in = piece(W_SPARE[0], DK, T)
        bonus_v = piece(LM["M"][0], NT, 512)
        ffn_v = piece(LF["end"] + 2 * CHUNK, DK, T)
        ffn_parts = [nc.alloc_sbuf_tensor_at(f"ffn_in_rounded_{n}", [P, DK, T], F32R,
                                             offset=arena_at + 4 * (LF["end"] + CHUNK * (n + 1))) for n in range(2)]
        M0 = LM["M"][0]
        mslot = lambda n: piece(M0 + 1024 * n, 4, T)
        fT = area(LM, "fT", FTC, 257)
        f_r, f_k, f_v = (fT[:, 4 * n:4 * n + 4, 1:257] for n in range(3))
        At, Bt = (piece(LM["RT"][0] + 1024 * n, 4, T) for n in range(2))
        natl = {w: piece(LM["N"][0] + 1024 * n, NT, 512) for n, w in enumerate("ABKV")}
        dtmp, kk, kk2, sw, sa, Ls, Le = (mslot(n) for n in range(7))
        Einv, Ein, Eex, kp, rk, BhT, KhT = sw, Ls, Le, kk2, dtmp, sa, kk2
        retn = piece(M0 + 7 * 1024, NT, 2048)
        rqT, rkT = (piece(M0 + n * 1024, 4, T) for n in (11, 6))
        rsc = (mslot(3), piece(M0 + 5 * 1024, 4, P))
        mats = [piece(M0 + 2048 * n, NT, 8, P) for n in range(7)]
        AdT, Ad, o16T, o32T, X, P2, P2T = mats
        P4T, P4, P8T, TT, Z = AdT, Ad, P2, P2T, Ad
        AakT, ArbT, ArkT = AdT, P2, Ad
        Qn = piece(M0 + 2048 * 2, NT, 512)
        WT = piece(M0 + 2048 * 2 + 1024, 4, T)
        Un = piece(M0 + 2048 * 3, NT, 2, 256)
        gnat = piece(M0 + 1024, NT, 512)
        AtP, frP = (f[:].rearrange("p (a k) t -> p a k t", a=2) for f in (featL, featT))
        ynat, ytmp = natl["A"], natl["B"]
        S = piece(LM["RT"][0], NCH, 4, 64)
        PC = sb("PC", [P, 4, NCH])
        quad = [piece(QUAD * n, 4, EG, 512) for n in range(NQ)]
        xg = featL[:, 0:4, :].rearrange("p a b -> p (a b)").rearrange("p (k s) -> p k s", k=DK)
        G, Gw = (area(LE, n, NT, EG, CAP) for n in ("G", "Gw"))
        GT = area(LE, "GT", NT, P)
        sg, hh = (arena[:, LE[n][0]:LE[n][1]] for n in ("sg", "h"))
        hhT = area(LE, "hT", 4, P)
        dd = featL[:, 4:8, :].rearrange("p a b -> p (a b)").rearrange("p (n c) -> p n c", n=2)
        diag = rt[:, 0:NT * P].rearrange("p (t q) -> p t q", t=NT)
        inv_rows = rt[:, 256:256 + T]
        rank = rt[:, 0:64].rearrange("p (t e) -> p t e", t=NT)
        comb = rt[:, 64:128].rearrange("p (t e) -> p t e", t=NT)
        selr = rt[:, 128:192].rearrange("p (t e) -> p t e", t=NT)
        lg, one1, one2 = (rt[:, lo:lo + 80].rearrange("p (t g e) -> p t g e", t=NT, g=5) for lo in (192, 272, 352))
        oh1, oh2 = (rt[:, lo:lo + 64].rearrange("p (t e) -> p t e", t=NT) for lo in (432, 496))
        m1, m2, cm = (rt[:, lo:lo + 10] for lo in (560, 570, 580))
        e4 = rt[:, 590:598].rearrange("p (t g) -> p t g", t=NT)
        e2, gp, w1, w2 = (rt[:, 598 + 2 * n:600 + 2 * n] for n in range(4))

        x_in = [sem(f"x_in{t}") for t in range(NT)]
        ident_in = sem("ident_in")
        params_in = sem("params_in")
        rpb_copied = sem("rpb_copied")
        biasA_in = sem("biasA_in")
        t5_in = sem("t5_in")
        t5_stored = sem("t5_stored")
        biasB_in = sem("biasB_in")
        gain_in = sem("gain_in")
        first_in = sem("first_in")
        slot_in = [sem(f"slot_in{n}") for n in range(NSLOT)]
        down_read = sem("down_read")
        hi_ready = sem("hi_ready")
        lo_ready = {w: sem(f"lo_ready_{w}") for w in ("dve", "pool")}
        feat_hi = sem("feat_hi")
        feat_lo = sem("feat_lo")
        hT_hi = sem("hT_hi")
        hT_lo = sem("hT_lo")
        filled = sem("psum_filled")
        emptied = {w: sem(f"psum_emptied_{w}") for w in ("act", "dve")}
        dve_step = sem("dve_step")
        act_step = sem("act_step")
        rms_ready = sem("rms_ready")
        var_ready = sem("var_ready")
        root_ready = sem("root_ready")
        eps_ready = sem("eps_ready")
        xn_ready = sem("xn_ready")
        diag_ready = sem("diag_ready")
        silu_done = sem("silu_done")
        h_scaled = sem("h_scaled")
        resid_done = [sem(f"resid_done{t}") for t in range(NT)]
        qk_ready = sem("qk_ready")
        max_ready = sem("max_ready")
        exp_ready = sem("exp_ready")
        gates_ready = sem("gates_ready")
        y_ready = sem("y_ready")
        lerp_ready = sem("lerp_ready")
        lora_act = sem("lora_act")
        kk_ready = sem("kk_ready")
        kk2_ready = sem("kk2_ready")
        scan_ready = sem("scan_ready")
        decay_ready = sem("decay_ready")
        rot_ready = sem("rot_ready")
        rw_ready = sem("rw_ready")
        x0_ready = sem("x0_ready")
        mixed_ready = sem("mixed_ready")
        group_ready = sem("group_ready")
        e2_ready = sem("e2_ready")
        route_ready = sem("route_ready")
        share_ready = sem("share_ready")
        share_step = sem("share_step")
        comb_ready = sem("comb_ready")
        count_ready = sem("count_ready")
        quad_in = [[sem(f"quad_in{n}_{k}") for k in range(4)] for n in range(NQ)]
        pieces_read = sem("pieces_read")
        onehot_ready = sem("onehot_ready")
        shares_ready = sem("shares_ready")
        zeros = sem("zeros")
        at_copied = sem("at_copied")
        padded = [sem(f"padded_{n}") for n in ("A", "r")]
        beside = sem("beside")
        merge_ready = sem("merge_ready")
        oh1_ready = sem("oh1_ready")
        gathered = sem("gathered")
        xg_ready = sem("xg_ready")
        silu_ready = sem("silu_ready")
        h_ready = sem("h_ready")
        gt_filled = sem("gt_filled")
        gt_ready = sem("gt_ready")
        hT_filled = sem("hT_filled")
        hT_ready = sem("hT_ready")
        d0_ready = sem("d0_ready")
        d1_ready = sem("d1_ready")
        scattered = sem("scattered")
        shifted = sem("shifted")
        factor_ready = sem("factor_ready")
        out_ready = sem("out_ready")
        out_done = sem("out_done")

        rpb = A["rpb"]
        RPB = rpb.shape[1]
        rpb_copies = nc.dram_tensor("rpb_copies", (8, GRID_W, RPB), F32, kind="Internal").ap()
        t5_copies = nc.dram_tensor("t5_copies", (8, P, REL), F32, kind="Internal").ap()

        def kxn(w, lo, n):
            return w[:, lo:lo + n].rearrange("(k p) n -> p k n", p=P)

        units, uname = [], {}

        def unit(name, *parts):
            uname[name] = len(units)
            units.append(parts)

        w_in, w_in2 = A["w_in"], A["w_in_2"]
        for u in range(9):
            lo = 512 * u if u < 4 else (2048 if u == 4 else NQKV + 512 * (u - 5))
            n = 256 if u == 4 else 512
            unit(("p1", u), (0, DK, n, kxn(w_in, lo, n)))
        unit(("br", 0), (0, 4, D, kxn(A["w_branch_a"], 0, D)))
        unit(("br", 1), (0, 4, D, kxn(A["w_branch_b"], 0, D)))
        for n in range(2):
            unit(("wo", n), (0, DK, 512, kxn(A["w_out"], 512 * n, 512)))
        for u in range(FFK // 2):
            unit(("ffn", u), (0, DK, 256, kxn(A["w_gate"], 256 * u, 256)),
                 (2048, DK, 256, kxn(A["w_up"], 256 * u, 256)))
        for u in range(-(-FFK // 4)):
            kn = min(4, FFK - 4 * u)
            unit(("down", u), (0, kn, D, A["w_down"][512 * u:512 * u + kn * P, :].rearrange("(k p) n -> p k n", p=P)))
        unit(("rw", 3), (0, DK, 256, kxn(w_in2, 2048 + 1536, 256)))
        for u in (1, 0, 2):
            unit(("rw", u), (0, DK, 512, kxn(w_in2, 2048 + 512 * u, 512)))
        for u in range(4):
            unit(("p2", u), (0, DK, 512, kxn(w_in2, 512 * u, 512)))
        for n in range(2):
            unit(("wo2", n), (0, DK, 512, kxn(A["w_out_2"], 512 * n, 512)))
        loads_so_far, unit_level = [0] * NSLOT, []
        for n, parts in enumerate(units):
            loads_so_far[n % NSLOT] += 16 * len(parts)
            unit_level.append(loads_so_far[n % NSLOT])
        last_fill = {}
        for u in range(9):
            last_fill[("p1", u)] = ("p1", u, 0 if u == 4 else 1)
        for br in range(2):
            last_fill[("br", br)] = ("br", br, 1, 1)
        for n in range(2):
            last_fill[("wo", n)] = ("wo", n, 1)
            last_fill[("wo2", n)] = ("wo2", n, 1)
        for u in range(FFK // 2):
            last_fill[("ffn", u)] = ("up", u)
        last_fill[("rw", 3)] = ("rw", 6)
        for u in range(3):
            last_fill[("rw", u)] = ("rw", 2 * u + 1)
        for u in range(4):
            last_fill[("p2", u)] = ("p2", u, 1)
        last_fill[("down", 5)] = ("down", 1, 1)
        names = list(uname)

        def wview(name, part=0, of=None):
            n = uname[name]
            off, k, w, _ = units[n][part]
            return piece((n % NSLOT) * SLOT + off, k, w, of=of)

        chunks, chunk_of, chunk_last = [], {}, []

        def chunk(name, c, view, hi, last, by):
            chunk_of[name, c] = len(chunks)
            chunks.append((name, view, hi, by))
            chunk_last.append(last)

        def cols256(name, c):
            return lambda of: wview(name, 0, of)[:, :, 256 * c:256 * c + 256]

        ring = (*W_SIG, W_QK, W_SPARE)
        for n in range(9):
            u, c = n // 2, n % 2
            chunk(("p1", u), c, cols256(("p1", u), c), ring[n % 4], ("p1", u, c), "dve")
        for n in range(8):
            u, c = 5 + n // 2, n % 2
            chunk(("p1", u), c, cols256(("p1", u), c), (W_SPARE, W_NAT)[n % 2], ("p1", u, c), "pool" if n > 1 else "dve")
        ring = (W_SPARE, W_NAT, W_QK, W_PROB)
        for br in range(2):
            for c in range(2):
                chunk(("br", br), c, lambda of, br=br, c=c: wview(("br", br), 0, of)[:, :, 512 * c:512 * c + 512], ring[2 * br + c],
                      ("br", br, c, 1), "pool")
        ring = (W_SPARE, W_NAT, W_FFN, W_PROB)
        for n in range(4):
            chunk(("wo", n // 2), n % 2, cols256(("wo", n // 2), n % 2), ring[n], ("wo", n // 2, n % 2), "pool")
        ring = (W_FFN, W_PROBT, W_PROB, W_SPARE)
        for n in range(FFK):
            u, c = n // 2, n % 2
            chunk(("ffn", u), c, lambda of, u=u, c=c: wview(("ffn", u), c, of), ring[n % 4], (("gate", "up")[c], u),
                  "pool" if n < 4 else "dve")
        for n in range(FFK // 2):
            chunk(("down", n // 2), n % 2, lambda of, n=n: wview(("down", n // 2), 0, of)[:, 2 * (n % 2):2 * (n % 2) + 2, :],
                  ring[(FFK + n) % 4],
                  ("down", 1, 1) if n == FFK // 2 - 1 else None, "dve")
        ring = (W_PROBT, W_SPARE, W_FFN)
        for n, c in enumerate(RW_ORDER):
            chunk(("rw", c // 2), c % 2, cols256(("rw", c // 2), c % 2), ring[n % 3], ("rw", c), "dve" if n < 2 else "pool")
        for n in range(8):
            chunk(("p2", n // 2), n % 2, cols256(("p2", n // 2), n % 2), ring[(n + len(RW_ORDER)) % 3], ("p2", n // 2, n % 2),
                  "pool")
        for n in range(4):
            chunk(("wo2", n // 2), n % 2, cols256(("wo2", n // 2), n % 2), W_RING[n % 3], ("wo2", n // 2, n % 2), "dve")
        before, lo_level, taken, made = [], [], {}, {"dve": 0, "pool": 0}
        for g, (_, _, hi, by) in enumerate(chunks):
            before.append(taken.get(hi))
            taken[hi] = g
            made[by] += 1
            lo_level.append(made[by])

        def hi_view(g):
            _, view, hi, _ = chunks[g]
            view, rounded, high = view(arena), view(ring_r), hi_r[hi]
            k, n = view.shape[1], view.shape[2]
            step = hi[1] - hi[0]
            if step == CHUNK // 2:
                return high[:].rearrange("p (k n) -> p k n", k=k), view, rounded
            high = high[:].rearrange("p (a r) -> p a r", a=2)[:, :, 0:CHUNK // 2].rearrange("p a (k n) -> p a k n", n=n)
            return [high] + [w.rearrange("p (a k) n -> p a k n", a=2) for w in (view, rounded)]

        def hi_cols(g, k, lo, n):
            _, view, hi, _ = chunks[g]
            at_ = k * view(arena).shape[2] + lo
            at_ = hi[at_ // (CHUNK // 2)] - hi[0] + at_ % (CHUNK // 2)
            return hi_r[hi][:, at_:at_ + n]

        def lo_cols(g, k, lo, n):
            return chunks[g][1](ring_r)[:, k, lo:lo + n]

        def wait_chunk_read(eng, g):
            if chunk_last[g]:
                wait_filled(eng, *chunk_last[g])
            else:
                name, c = next(key for key, n in chunk_of.items() if n == g)
                eng.wait_ge(down_read, 2 * name[1] + c + 1)

        def wait_split(eng, g):
            eng.wait_ge(lo_ready[chunks[g][3]], lo_level[g])

        def low_part(eng, tensor_tensor, g):
            eng.wait_ge(hi_ready, g + 1)
            high, view, low = hi_view(g)
            tensor_tensor(low, view, high.bitcast(F32), ALU.subtract).then_inc(lo_ready[chunks[g][3]], 1)

        def wait_filled(eng, *key):
            eng.wait_ge(filled, index[key] + 1)

        def wait_emptied(eng, *key):
            eng.wait_ge(emptied[who_of[key]], turn[key] + 1)

        def bank(*key):
            return psum[:, index[key] % 8, :]

        class Steps:

            def __init__(self, eng, s):
                self.eng, self.sem, self.n, self.drains = eng, s, 0, 0

            def link(self, ins):
                ins.then_inc(self.sem, 1)
                self.n += 1
                self.eng.wait_ge(self.sem, self.n)

            def empty(self, who, ins, *key):
                assert who_of[key] == who and turn[key] == self.drains, (key, turn[key], self.drains)
                self.drains += 1
                ins.then_inc(emptied[who], 1)
                self.eng.wait_ge(emptied[who], self.drains)

        PARAMS_IN = 16 * 5
        block = ctx.enter_context(nc.Block())

        moe_w = {"gate": A["w_gate_2"], "up": A["w_up_2"], "down": A["w_down_2"]}
        QUADS_PER_GROUP = 6
        ALLQ = NG * QUADS_PER_GROUP

        RELEASED = ((("inv", "TT", NT - 1, 1), ((0, 2),)), (("mat", "Ark", NT - 1, 1), ((1, 1),)),
                    (("U", NCH - 1, 1), ((0, 0), (1, 0))), (("Y", 1, 1), ((0, 1), (0, 3), (1, 2), (1, 3))))

        def quad_slot(q):
            return (2, 3, 1, 0)[q % NQ]

        def bc(ap, n):
            return ap.unsqueeze(len(ap.shape)).to_broadcast([*ap.shape, n])

        @block.sync
        def _(sp):
            for t in range(NT):
                nc.sync.dma_start(x[:, t, :], A["x"][t * P:(t + 1) * P, :]).then_inc(x_in[t], 16)
            for n, parts in enumerate(units):
                if n >= NSLOT:
                    old = names[n - NSLOT]
                    if old in last_fill:
                        wait_filled(sp, *last_fill[old])
                    else:
                        sp.wait_ge(down_read, 2 * old[1] + 2)
                if n == 0:
                    off, k, w, src = parts[0]
                    for h in range(2):
                        cols_ = slice(w // 2 * h, w // 2 * (h + 1))
                        nc.sync.dma_start(piece(off, k, w)[:, :, cols_], src[:, :, cols_]).then_inc((first_in, slot_in[0])[h], 16)
                    continue
                for off, k, w, src in parts:
                    nc.sync.dma_start(piece((n % NSLOT) * SLOT + off, k, w), src).then_inc(slot_in[n % NSLOT], 16)

            def load_quad(pair, q, read=None, pieces=range(4)):
                gp, q6 = q // QUADS_PER_GROUP, q % QUADS_PER_GROUP
                kind, half = ("gate", "up", "down")[q6 // 2], q6 % 2
                e0 = pair * (2 * EG) + gp * EG
                w = moe_w[kind][e0:e0 + EG] if isinstance(e0, int) else moe_w[kind][bass.ds(e0, EG)]
                w = w[:, :, 512 * half:512 * half + 512] if kind == "down" else w[:, 512 * half:512 * half + 512, :]
                for k in pieces:
                    if read is not None:
                        sp.wait_ge(pieces_read, read + (k + 1))
                    nc.sync.dma_start(quad[quad_slot(q)][:, k], w[:, k * P:(k + 1) * P, :].rearrange("j p n -> p j n"))\
                        .then_inc(quad_in[quad_slot(q)][k], 16)

            def moe_stream(r, first):
                if first:
                    for key, pieces in RELEASED:
                        wait_filled(sp, *key)
                        for q, k in pieces:
                            load_quad(0, q, pieces=(k,))
                    sp.wait_ge(mixed_ready, 2 * NT)
                    wait_filled(sp, "wo2", 0, 1)
                    load_quad(0, 2, pieces=range(3))
                    wait_filled(sp, "wo2", 1, 0)
                    load_quad(0, 2, pieces=(3,))
                    wait_filled(sp, "wo2", 1, 1)
                    load_quad(0, 3)
                else:
                    sp.wait_ge(pieces_read, r * (4 * ALLQ))
                    for q in range(NQ):
                        load_quad(0, q)
                with sp.Fori(0, NG // 2 - 1) as pair:
                    for q in range(NQ, 12 + NQ):
                        load_quad(pair + q // 12, q % 12, r * (4 * ALLQ) + pair * 48 + 4 * (q - NQ))
                for q in range(NQ, 12):
                    load_quad(NG // 2 - 1, q, r * (4 * ALLQ) + 4 * (ALLQ - 12 + q - NQ))

            moe_stream(0, True)
            sp.wait_ge(count_ready, 1)
            most = sp.value_load(cnt[0:1, 0:1], min_val=0, max_val=T)
            with sp.If(most > CAP):
                with sp.Fori(1, ROUNDS) as r:
                    with sp.If(most > r * CAP):
                        moe_stream(r, False)
            for t in range(NT):
                for n in range(2):
                    sp.wait_ge(out_ready, 2 * t + n + 1)
                    cols_ = slice(512 * n, 512 * n + 512)
                    nc.sync.dma_start(out[t * P:(t + 1) * P, cols_], xn[:, t, cols_]).then_inc(out_done, 16)
            sp.wait_ge(out_done, 16 * 2 * NT)

        @block.gpsimd
        def _(pool):
            merges = [0]
            pool.wait_ge(rpb_copied, 16)
            for h in range(8):
                for half in range(2):
                    src = bass.AP(tensor=rpb_copies.tensor, offset=h * GRID_W * RPB + (5 - half) * 31 + 15,
                                  ap=[[RPB - 1, GRID_W], [31, 6], [1, GRID_W]])
                    nc.gpsimd.dma_start(biasA[64 * half:64 * half + 64, h], src).then_inc(biasA_in, 16)
            wait_emptied(pool, "t5")
            nc.gpsimd.dma_start(t5_copies, tb_sb.unsqueeze(1).to_broadcast([8, P, REL])).then_inc(t5_stored, 16)
            pool.wait_ge(t5_stored, 16)
            src = bass.AP(tensor=t5_copies.tensor, offset=P - 1, ap=[[REL - 1, P], [P * REL, 8], [1, EXT]])
            nc.gpsimd.dma_start(biasB, src).then_inc(biasB_in, 16)
            for g, c in enumerate(chunks):
                if c[3] == "pool":
                    low_part(pool, nc.gpsimd.tensor_tensor, g)
            wait_filled(pool, "p2", 3, 1)
            for n, f in enumerate((AtP, frP)):
                nc.gpsimd.memset(f[64:128, 0], 0.0).then_inc(beside, 1)
                pool.wait_ge(beside, 2 * n + 1)
                nc.gpsimd.memset(f[0:64, 1], 0.0).then_inc(beside, 1)
                pool.wait_ge(beside, 2 * n + 2)
            for t in range(NT):
                for par in range(2):
                    hs = slice(4 * par, 4 * par + 4)
                    pool.wait_ge(at_copied, 2 * t + par + 1)
                    for dst, m in ((o16T, "m16T"), (o32T, "m32T")):
                        nc.gpsimd.tensor_tensor(dst[:, t, hs, :], o32T[:, t, hs, :], con(m).unsqueeze(1).to_broadcast([P, 4, P]),
                                                ALU.mult).then_inc(merge_ready, 1)
                        merges[0] += 1
                        pool.wait_ge(merge_ready, merges[0])
            wait_filled(pool, "wo2", 1, 1)
            nc.gpsimd.memset(dd, 0.0).then_inc(zeros, 1)
            pool.wait_ge(zeros, 1)
            nc.gpsimd.memset(GT, 0.0).then_inc(gt_ready, 1)
            wait_filled(pool, "logit", NT - 1)
            nc.gpsimd.dma_start(featT[:, 0:4, :].rearrange("p a b -> p (a b)"),
                                A["final_gain"].to_broadcast([P, D])).then_inc(gain_in, 16)
            pool.wait_ge(share_ready, 1)
            steps = [0]

            def link(ins):
                ins.then_inc(share_step, 1)
                steps[0] += 1
                pool.wait_ge(share_step, steps[0])

            ptt = nc.gpsimd.tensor_tensor
            link(ptt(w2, w1, e2, ALU.mult))
            pool.wait_ge(route_ready, 1)
            link(ptt(oh1, oh1, bc(w1, E), ALU.mult))
            link(ptt(oh2, oh2, bc(w2, E), ALU.mult))
            ptt(comb, oh1, oh2, ALU.add).then_inc(comb_ready, 1)

        @block.tensor
        def _(pe):
            at = [0]

            def begin(*key):
                n = index[key]
                assert n == at[0], (key, n, at[0])
                at[0] += 1
                if n >= 8:
                    wait_emptied(pe, *fills[n - 8][0])
                return psum[:, n % 8, :]

            def end(ins):
                ins.then_inc(filled, 1)

            mm, tr = nc.tensor.matmul, nc.tensor.transpose

            def mm_halves(o, lhs, rhs, start, stop):
                for r in (slice(0, 64), slice(64, 128)):
                    ins = mm(o[r], lhs[:, r], rhs, start=start, stop=stop, skip_group_check=True)
                return ins

            def transposes(key, sources, ready):
                b = begin(*key).rearrange("p (k q) -> p k q", q=P)
                ready()
                for k, s in enumerate(sources):
                    ins = tr(b[:, k, :], s, ident)
                end(ins)

            def norm_T():
                for t in range(NT):
                    for h in range(2):
                        transposes(("nt", 0, t, h), [xn[:, t, (4 * h + k) * P:(4 * h + k + 1) * P] for k in range(4)],
                                   lambda: pe.wait_ge(xn_ready, t + 1))

            def resid_T(n, j, *written):
                def ready():
                    for key in written:
                        wait_emptied(pe, *key)
                transposes(("nt", n, j), [x[:, t, (2 * j + k) * P:(2 * j + k + 1) * P] for k in range(2) for t in range(NT)],
                           ready)

            def spread(n):
                b = begin("rb", n)
                pe.wait_ge(diag_ready, n)
                end(mm(b[:, 0:T], con("ones"), diag.rearrange("p t q -> p (t q)"), start=True, stop=True))

            def mm3(o, lhs, rhs, start, stop):
                mm(o, lhs[0], rhs[0], start=start, stop=False, skip_group_check=True)
                mm(o, lhs[0], rhs[1], start=False, stop=False, skip_group_check=True)
                return mm(o, lhs[1], rhs[0], start=False, stop=stop, skip_group_check=True)

            def project_tile(b, g, t, ks=range(DK), first=False):
                for k in ks:
                    if first and k % 4 == 0:
                        pe.wait_ge(feat_lo, 2 * t + k // 4 + 1)
                    ins = mm3(b[:, t, :], [f[:, k, t * P:(t + 1) * P] for f in (featR, featLR)],
                              [part(g, k, 0, 256) for part in (hi_cols, lo_cols)], k == 0, k == DK - 1)
                return ins

            def project(key, name, c, first=False):
                b = begin(*key).rearrange("p (t n) -> p t n", t=NT)
                g = chunk_of[name, c]
                wait_split(pe, g)
                for t in range(NT):
                    ins = project_tile(b, g, t, first=first)
                end(ins)

            def features(key, name, c, feats, lows=None):
                b = begin(*key).rearrange("p (f t) -> p f t", f=2)
                g = chunk_of[name, c]
                wait_split(pe, g)
                for f in range(2):
                    for k in range(DK):
                        if lows is not None and f == 0 and k % 2 == 0:
                            pe.wait_ge(feat_lo, lows + k // 2 + 1)
                        ins = mm3(b[:, f, :], [part(g, k, P * f, P) for part in (hi_cols, lo_cols)],
                                  [r[:, k, :] for r in feats], k == 0, k == DK - 1)
                end(ins)

            pe.wait_ge(ident_in, 32)
            norm_T()
            offs = {"qa": 0, "ka": 512, "qb": 1536}
            def turn_qk(*names):
                for name in names:
                    s = ("qa", "ka", "qb", "kb").index(name)
                    for t in range(NT):
                        if name == "kb":
                            src = [kdup[:, t, kv, :] for kv in range(2)]
                        else:
                            src = [nat[:, t, offs[name] + P * k:offs[name] + P * (k + 1)] for k in range(4)]
                        transposes(("qkT", name, t), src, lambda: pe.wait_ge(qk_ready, 2 * s + t + 1))

            for u in range(5):
                if u == 4:
                    turn_qk("qa", "ka")
                for c in range(1 if u == 4 else 2):
                    project(("p1", u, c), ("p1", u), c, first=u + c == 0)
                if u == 2:
                    b = begin("t5")
                    pe.wait_ge(params_in, PARAMS_IN)
                    pe.wait_ge(t5_in, 32)
                    end(mm(b[0:8, 0:REL], t5b[:], onehot, start=True, stop=True))
            def turn_out(br, t):
                transposes(("oT", br, t), [xn[:, t, 512 * br + P * k:512 * br + P * (k + 1)] for k in range(4)],
                           lambda: wait_emptied(pe, "PV", 4 * br + 2 * t + 1))

            def scores(i):
                br, t, g = i // 4, i // 2 % 2, i % 2
                banks = [begin("S", i, par).rearrange("p (a k) -> p a k", a=2) for par in range(2)]
                for name in ("qa", "ka") if br == 0 else ("qb", "kb"):
                    wait_emptied(pe, "qkT", name, 1)
                for pair in range(2):
                    for par in range(2):
                        rows_ = slice(64 * par, 64 * par + 64)
                        q = (qbT if br else qaT)[rows_, 2 * g + pair, t * P:(t + 1) * P]
                        k = kbT[rows_, g, :] if br else kaT[rows_, 2 * g + pair, :]
                        ins = mm(banks[par][:, pair, :], q, k, start=True, stop=True)
                        if pair == 1:
                            end(ins)

            def turned(i):
                for par in range(2):
                    b = begin("PT", i, par).rearrange("p (a k q) -> p a k q", a=2, k=2)
                    pe.wait_ge(exp_ready, 2 * i + par + 1)
                    for pair in range(2):
                        for kt in range(NT):
                            ins = tr(b[:, pair, kt, :], prob[:, i % 2, par, pair, kt * P:(kt + 1) * P], ident)
                    end(ins)

            def weighted(i):
                br, t, g = i // 4, i // 2 % 2, i % 2
                b = begin("PV", i)
                for par in range(2):
                    wait_emptied(pe, "PT", i, par)
                for h in range(4):
                    for kt in range(NT):
                        v0 = 2176 + 64 * g if br else 1024 + 64 * (4 * g + h)
                        ins = mm_halves(b[:, 64 * h:64 * h + 64], probT[:, 2 * (i % 2) + h % 2, h // 2, kt, :],
                                        nat[:, kt, v0:v0 + 64], kt == 0, kt == NT - 1)
                end(ins)

            for i in range(9):
                if i < 8:
                    scores(i)
                if i >= 1:
                    turned(i - 1)
                if i == 0:
                    turn_qk("qb", "kb")
                if i < 8:
                    u, c = 5 + i // 2, i % 2
                    project(("p1", u, c), ("p1", u), c)
                if i == 8:
                    for key in ((0, 0), (0, 1), (1, 0)):
                        turn_out(*key)
                if i >= 1:
                    weighted(i - 1)
            for br in range(2):
                if br == 1:
                    turn_out(1, 1)
                for n in range(2):
                    g = chunk_of[("br", br), n]
                    wait_split(pe, g)
                    for t in range(NT):
                        b = begin("br", br, n, t)
                        wait_emptied(pe, "oT", br, t)
                        for k in range(4):
                            ins = mm3(b, [f[:, 4 * br + k, t * P:(t + 1) * P] for f in (featR, featLR)],
                                      [part(g, k, 0, 512) for part in (hi_cols, lo_cols)], k == 0, k == 3)
                        end(ins)
            for h in range(2):
                for t in range(NT):
                    transposes(("yT", t, h), [sig[:, t, (4 * h + k) * P:(4 * h + k + 1) * P] for k in range(4)],
                               lambda: pe.wait_ge(y_ready, 2 * h + t + 1))
            wait_emptied(pe, "yT", 1, 1)
            for j in range(4):
                project(("wo", j // 2, j % 2), ("wo", j // 2), j % 2)
                if j:
                    resid_T(1, j - 1, ("wo", (j - 1) // 2, (j - 1) % 2))
            resid_T(1, 3, ("wo", 1, 1))
            for u in range(FFK // 2):
                for c, name in enumerate(("gate", "up")):
                    features((name, u), ("ffn", u), c, ffn_parts, 4 if u + c == 0 else None)
                    if u == 0 and c == 0:
                        spread(1)
            banks = {(t, n): begin("down", t, n) for n in range(2) for t in range(NT)}
            for u in range(FFK // 2):
                g = chunk_of[("down", u // 2), u % 2]
                wait_split(pe, g)
                pe.wait_ge(hT_lo, u + 1)
                for n in range(2):
                    for t in range(NT):
                        for k in range(2):
                            ins = mm3(banks[t, n], [h[:, 2 * u + k, t * P:(t + 1) * P] for h in hT_parts],
                                      [part(g, k, 512 * n, 512) for part in (hi_cols, lo_cols)],
                                      u == 0 and k == 0, u == FFK // 2 - 1 and k == 1)
                        if u == FFK // 2 - 1:
                            end(ins)
                if u < FFK // 2 - 1:
                    ins.then_inc(down_read, 1)

            for j in range(4):
                resid_T(2, j, ("down", 1, j // 2))
            def lora_up(name, lo, sem_, src):
                for h in range(2):
                    b = begin(name, h).rearrange("p (f t) -> p f t", f=2)
                    pe.wait_ge(sem_, 1)
                    for f in range(2):
                        c = 2 * h + f
                        ins = mm(b[:, f, :], lora[lo:lo + 64, P * c:P * c + P], src, start=True, stop=True)
                    end(ins)

            for c in RW_ORDER:
                features(("rw", c), ("rw", c // 2), c % 2, (featR, featLR), 8 if c == RW_ORDER[0] else None)
                if c == 6:
                    spread(2)
                if c == 3:
                    lora_up("z", 0, lora_act, tanh_w[:])
                    lora_up("za", 64, lerp_ready, fT[64:128, 12, 1:257])
                if c == 0:
                    for h in range(2):
                        b = begin("ss", h)
                        pe.wait_ge(kk2_ready, 1)
                        end(mm(b, con("same"), kk2[:, 2 * h:2 * h + 2, :].rearrange("p a b -> p (a b)"), start=True, stop=True))
            for u in range(3):
                for c in range(2):
                    project(("p2", u, c), ("p2", u), c)
            for s, name in enumerate(("q", "k")):
                for t in range(NT):
                    transposes(("rT", name, t), [retn[:, t, 512 * s + P * k:512 * s + P * (k + 1)] for k in range(4)],
                               lambda: pe.wait_ge(rot_ready, t + 1))
            for j in range(3):
                b = begin("rs", j)
                for name in ("q", "k"):
                    wait_emptied(pe, "rT", name, 1)
                if j < 2:
                    for a in range(2):
                        ins = mm(b[:, T * a:T * a + T], rkT[:, 2 * j + a, 0:P], rqT[:, 2 * j + a, :], start=True, stop=True)
                else:
                    for a in range(4):
                        ins = mm(b[:, P * a:P * a + P], rkT[:, a, P:T], rqT[:, a, P:T], start=True, stop=True)
                end(ins)
            project(("p2", 3, 0), ("p2", 3), 0)
            for t in range(NT):
                b = begin("ro", t)
                wait_emptied(pe, "rs", 2 * t if t else 1)
                for a in range(4):
                    for kt in range(t + 1):
                        lhs = rsc[0][:, a, t * P:(t + 1) * P] if kt == 0 else rsc[1][:, a, :]
                        ins = mm(b[:, P * a:P * a + P], lhs, retn[:, kt, 1024 + P * a:1024 + P * (a + 1)],
                                 start=kt == 0, stop=kt == t)
                end(ins)
            project(("p2", 3, 1), ("p2", 3), 1)
            src = {"A": At, "B": BhT, "K": KhT, "V": f_v}
            for w in "ABKV":
                for t in range(NT):
                    transposes(("natl", w, t), [src[w][:, k, t * P:(t + 1) * P] for k in range(4)],
                               lambda: pe.wait_ge(rw_ready, 1))
            b = begin("bonus")
            for t in range(NT):
                for k in range(4):
                    ins = mm_halves(b[:, 8 * t + 2 * k:8 * t + 2 * k + 2], rk[:, k, t * P:(t + 1) * P], con("sel"), True, True)
            end(ins)

            sides = {"AT": (Bt, AtP), "A": (AtP, Bt), "Aak": (f_k, AtP), "Arb": (Bt, frP), "Ark": (f_k, frP)}

            def mat(name):
                lhs, rhs = sides[name]
                for t in range(NT):
                    for par in range(2):
                        b = begin("mat", name, t, par).rearrange("p (i q) -> p i q", i=4)
                        side_r = name in ("Arb", "Ark")
                        pe.wait_ge(padded[side_r], 2)
                        pe.wait_ge(beside, 4 if side_r else 2)
                        for i in range(4):
                            side = lambda m: m[:, par, i, t * P:(t + 1) * P] if m is AtP or m is frP else m[:, i, t * P:(t + 1) * P]
                            ins = mm(b[:, i, :], side(lhs), side(rhs), start=True, stop=True)
                        end(ins)

            mat("AT")
            mat("A")
            steps = {
                "P2": (AdT, Ad, ("mat A",)), "P2T": (Ad, AdT, ()),
                "X1": (P2T, X, ("P2T", "X0")), "P4": (P2T, P2, ("P2",)), "P4T": (P2, P2T, ()),
                "X2": (P4T, X, ("P4T", "X1")), "P8T": (P4, P4T, ("P4",)), "X3": (P8T, X, ("P8T", "X2")),
                "T16T": (X, None, ("X3",)), "Z1": (o16T, X, ("merge",)), "X4": (TT, Z, ("Z1", "T16T")),
                "T32T": (X, None, ("X4",)), "Z2": (o32T, X, ("merge",)), "X5": (TT, Z, ("Z2", "T32T")),
                "TT": (X, None, ("X5",)),
            }
            for name, _ in INVERSE:
                lhs, rhs, needs = steps[name]
                for t in range(NT):
                    for par in range(2):
                        b = begin("inv", name, t, par).rearrange("p (i q) -> p i q", i=4)
                        for need in needs:
                            if need == "mat A":
                                wait_emptied(pe, "mat", "A", t, par)
                            elif need == "merge":
                                pe.wait_ge(merge_ready, 2 * (2 * t + par + 1))
                            elif need == "X0":
                                pe.wait_ge(x0_ready, 2 * t + par + 1)
                            else:
                                wait_emptied(pe, "inv", need, t, par)
                        for i in range(4):
                            h = 4 * par + i
                            if rhs is None:
                                ins = tr(b[:, i, :], lhs[:, t, h, :], ident)
                            else:
                                ins = mm(b[:, i, :], lhs[:, t, h, :], rhs[:, t, h, :], start=True, stop=True)
                        end(ins)
                for extra in INV_EXTRA.get(name, ()):
                    mat(extra)
                if name == "Z2":
                    for t in range(NT):
                        b = begin("Q", t)
                        for par in range(2):
                            wait_emptied(pe, "mat", "Aak", t, par)
                        wait_emptied(pe, "natl", "V", t)
                        for h in range(8):
                            ins = mm_halves(b[:, 64 * h:64 * h + 64], AakT[:, t, 4 * (h % 2) + h // 2, :],
                                            natl["V"][:, t, 64 * h:64 * h + 64], True, True)
                        end(ins)
                    for t in range(NT):
                        b = begin("gn", t)
                        pe.wait_ge(lora_act, 2)
                        end(mm(b, sig_g[:, t * P:(t + 1) * P], gup[:], start=True, stop=True))
            for t in range(NT):
                b = begin("WT", t).rearrange("p (i q) -> p i q", i=4)
                for par in range(2):
                    wait_emptied(pe, "inv", "TT", t, par)
                for h in range(8):
                    ins = mm(b[64 * (h % 2):64 * (h % 2) + 64, h // 2, :], natl["A"][:, t, 64 * h:64 * h + 64],
                             TT[:, t, 4 * (h % 2) + h // 2, :], start=True, stop=True, skip_group_check=True)
                end(ins)
            def state_add(b, c, side, right):
                t, r = c // 2, slice(64 * (c % 2), 64 * (c % 2) + 64)
                for h in range(8):
                    par, i = h % 2, h // 2
                    ins = mm(b[64 * par:64 * par + 64, i, :], natl[side][r, t, 64 * h:64 * h + 64], right(r, t, par, i),
                             start=side == "K" and i == 0, stop=side == "B", skip_group_check=True)
                return ins

            def outputs(t, par):
                b = begin("Y", t, par)
                for p2 in range(2):
                    wait_emptied(pe, "U", 2 * t + 1, p2)
                    wait_emptied(pe, "mat", "Ark", t, p2)
                for i in range(4):
                    h = 2 * i + par
                    mm_halves(b[:, 64 * i:64 * i + 64], ArbT[:, t, 4 * par + i, :], Un[:, t, par, 64 * i:64 * i + 64],
                              True, False)
                    ins = mm_halves(b[:, 64 * i:64 * i + 64], ArkT[:, t, 4 * par + i, :], natl["V"][:, t, 64 * h:64 * h + 64],
                                    False, False)
                    for cc in (2 * t, 2 * t + 1):
                        if cc > 0:
                            ins = mm(b[64 * (cc % 2):64 * (cc % 2) + 64, 64 * i:64 * i + 64],
                                     frP[:, par, i, CH * cc:CH * cc + CH], S[:, cc, i, :],
                                     start=False, stop=cc % 2 == 1, skip_group_check=True)
                end(ins)

            for c in range(NCH):
                t, ro = c // 2, 64 * (c % 2)
                tok = slice(CH * c, CH * c + CH)
                banks = [begin("U", c, par) for par in range(2)]
                state = None
                if c < NCH - 1 and c not in Y_AFTER:
                    state = begin("St", c).rearrange("p (i v) -> p i v", v=64)
                    state_add(state, c, "K", lambda r, t, par, i: natl["V"][r, t, 64 * (2 * i + par):64 * (2 * i + par) + 64])
                wait_emptied(pe, "Q", t)
                wait_emptied(pe, "WT", t)
                for with_state in range(2 if c else 1):
                    if with_state:
                        wait_emptied(pe, "St", c - 1)
                    for par in range(2):
                        r = slice(64 * par, 64 * par + 64)
                        for i in range(4):
                            h = 2 * i + par
                            o = banks[par][ro:ro + 64, 64 * i:64 * i + 64]
                            if with_state:
                                ins = mm(o, WT[r, i, tok], S[r, c, i, :], start=False, stop=True, skip_group_check=True)
                            else:
                                ins = mm(o, TT[:, t, 4 * par + i, ro:ro + 64], Qn[:, t, 64 * h:64 * h + 64],
                                         start=i == 0, stop=c == 0, skip_group_check=True)
                        if with_state or c == 0:
                            end(ins)
                for y in Y_AFTER.get(c, ()):
                    outputs(*y)
                if c < NCH - 1:
                    if state is None:
                        state = begin("St", c).rearrange("p (i v) -> p i v", v=64)
                        state_add(state, c, "K", lambda r, t, par, i: natl["V"][r, t, 64 * (2 * i + par):64 * (2 * i + par) + 64])
                    for par in range(2):
                        wait_emptied(pe, "U", c, par)
                    end(state_add(state, c, "B", lambda r, t, par, i: Un[r, t, par, 64 * i:64 * i + 64]))
            def mixed_rows(t, h):
                return [xn[:, t, (4 * h + k) * P:(4 * h + k + 1) * P] for k in range(4)]

            transposes(("mT", 0, 0), mixed_rows(0, 0), lambda: pe.wait_ge(mixed_ready, 1))
            transposes(("mT", 0, 1), mixed_rows(0, 1), lambda: pe.wait_ge(mixed_ready, NT + 1))
            transposes(("mT", 1, 0), mixed_rows(1, 0), lambda: pe.wait_ge(mixed_ready, NT))
            last_T = begin("mT", 1, 1).rearrange("p (k q) -> p k q", q=P)
            ahead = [begin("wo2", 0, c).rearrange("p (t n) -> p t n", t=NT) for c in range(2)]
            wait_emptied(pe, "mT", 0, 1)
            for c in range(2):
                wait_split(pe, chunk_of[("wo2", 0), c])
                project_tile(ahead[c], chunk_of[("wo2", 0), c], 0)
            pe.wait_ge(mixed_ready, NT + 2)
            for k, rows_ in enumerate(mixed_rows(1, 1)):
                ins = tr(last_T[:, k, :], rows_, ident)
            end(ins)
            wait_emptied(pe, "mT", 1, 0)
            for c in range(2):
                project_tile(ahead[c], chunk_of[("wo2", 0), c], 1, range(DK // 2))
            wait_emptied(pe, "mT", 1, 1)
            for j in range(4):
                if j < 2:
                    end(project_tile(ahead[j], chunk_of[("wo2", 0), j], 1, range(DK // 2, DK)))
                else:
                    project(("wo2", 1, j % 2), ("wo2", 1), j % 2)
                if j:
                    resid_T(3, j - 1, ("wo2", (j - 1) // 2, (j - 1) % 2))
            resid_T(3, 3, ("wo2", 1, 1))
            logits = [begin("logit", t) for t in range(NT)]
            for j in range(4):
                wait_emptied(pe, "nt", 3, j)
                for t in range(NT):
                    for k in range(2 * j, 2 * j + 2):
                        ins = mm_halves(logits[t][:, 0:36], router_in[:, k, t * P:(t + 1) * P], wr[:, k, :], k == 0, k == DK - 1)
                    if j == 3:
                        end(ins)
            ybank = {(t, n): psum[:, MB[2 * t + n], :] for t in range(NT) for n in range(2)}
            wait_emptied(pe, "logit", 1)

            def busy(n):
                for _ in range(n):
                    mm(psum[:, MB[4], 0:P], ident, ident, start=True, stop=True)

            busy(4)
            pe.wait_ge(gt_ready, 1)
            for t in range(NT):
                for n in range(2):
                    ins = mm(ybank[t, n], GT[:, t, :], dd[:, n, :], start=True, stop=False, skip_group_check=True)
                    ins.then_inc(scattered, 1)
            b = begin("count")
            pe.wait_ge(route_ready, 1)
            for t in range(NT):
                ins = mm_halves(b[:, 0:E], con("ones"), selr[:, t, :], t == 0, t == NT - 1)
            end(ins)
            for t in range(NT):
                b = begin("rank", t)
                if t:
                    mm_halves(b[:, 0:E], con("ones"), selr[:, 0, :], True, False)
                end(mm_halves(b[:, 0:E], con("before"), selr[:, t, :], t == 0, True))

            busy(6)
            wait_emptied(pe, "rank", NT - 1)

            def moe_group(r, pair, gp):
                n = r * NG + pair * 2 + gp
                base = r * (4 * ALLQ) + pair * 48 + gp * 24

                def piece_ready(q, k):
                    pe.wait_ge(quad_in[quad_slot(q)][k], r * (12 * 16) + pair * (3 * 16) + (q // NQ + 1) * 16)
                    return quad[quad_slot(q)][:, k]

                pe.wait_ge(onehot_ready, n + 1)
                for kb in range(2):
                    b = psum[:, MB[6 + kb], :].rearrange("p (k s) -> p k s", k=4)
                    for k in range(4):
                        for t in range(NT):
                            ins = mm(b[:, k, :], xn[:, t, (4 * kb + k) * P:(4 * kb + k + 1) * P],
                                     G[:, t].rearrange("p e s -> p (e s)"), start=t == 0, stop=t == NT - 1)
                    ins.then_inc(gathered, 1)
                for m in range(2):
                    for half in range(2):
                        pe.wait_ge(xg_ready, 2 * n + half + 1)
                        for k in range(4):
                            w = piece_ready(6 * gp + 2 * m + half, k)
                            for j in range(EG):
                                ins = mm(psum[32 * j:32 * j + 32, MB[4 + m], :], xg[:, 4 * half + k, 32 * j:32 * j + 32],
                                         w[:, j, :], start=half == 0 and k == 0, stop=half == 1 and k == 3,
                                         skip_group_check=True)
                            ins.then_inc(pieces_read, 1)
                pe.wait_ge(shares_ready, n + 1)
                b = psum[:, MB[6], 0:2 * P].rearrange("p (t q) -> p t q", t=NT)
                for t in range(NT):
                    ins = tr(b[:, t, :], Gw[:, t].rearrange("p e s -> p (e s)"), ident)
                ins.then_inc(gt_filled, 1)
                pe.wait_ge(h_ready, n + 1)
                b = psum[:, MB[7], :].rearrange("p (k s) -> p k s", k=4)
                for k in range(4):
                    ins = tr(b[:, k, :], hh[:, k * P:(k + 1) * P], ident)
                ins.then_inc(hT_filled, 1)
                pe.wait_ge(hT_ready, n + 1)
                for half in range(2):
                    for k in range(4):
                        w = piece_ready(6 * gp + 4 + half, k)
                        for j in range(EG):
                            ins = mm(psum[32 * j:32 * j + 32, MB[4 + half], :], hhT[:, k, 32 * j:32 * j + 32], w[:, j, :],
                                     start=k == 0, stop=k == 3, skip_group_check=True)
                        ins.then_inc(pieces_read, 1)
                    if half:
                        pe.wait_ge(d1_ready, n + 1)
                    else:
                        pe.wait_ge(gt_ready, n + 2)
                        pe.wait_ge(d0_ready, n + 1)
                    for t in range(NT):
                        ins = mm(ybank[t, half], GT[:, t, :], dd[:, half, :], start=False, stop=False, skip_group_check=True)
                        ins.then_inc(scattered, 1)

            def moe_round(r):
                with pe.Fori(0, NG // 2) as pair:
                    for gp in range(2):
                        moe_group(r, pair, gp)

            pe.wait_ge(xn_ready, 2 * NT)
            moe_round(0)
            pe.wait_ge(count_ready, 1)
            most = pe.value_load(cnt[0:1, 0:1], min_val=0, max_val=T)
            with pe.If(most > CAP):
                with pe.Fori(1, ROUNDS) as r:
                    with pe.If(most > r * CAP):
                        moe_round(r)

        @block.scalar
        def _(act):
            a = Steps(act, act_step)
            fn = nc.scalar.activation
            empty = lambda ins, *key: a.empty("act", ins, *key)

            def squares(n, ready):
                fn(warm[:], eps_col[:, 0:1], ACT.Sqrt)
                for t in range(NT):
                    ready(t)
                    s = st[:, 2 * n + t:2 * n + t + 1]
                    a.link(fn(xn[:, t, :], x[:, t, :], ACT.Square, accum_out=s))
                    fn(s, s, ACT.Sqrt, scale=1.0 / D, bias=eps_col[:, 0:1]).then_inc(rms_ready, 1)

            n_roots = [0]

            def root(lo, n, d, k):
                n_roots[0] += 1
                act.wait_ge(var_ready, n_roots[0])
                s = st[:, lo:lo + n]
                fn(s, s, ACT.Sqrt, scale=1.0 / d, bias=eps_col[:, k:k + 1]).then_inc(root_ready, 1)

            def high_part(g, *also):
                name = chunks[g][0]
                if g == 0:
                    act.wait_ge(first_in, 16)
                else:
                    act.wait_ge(slot_in[uname[name] % NSLOT], unit_level[uname[name]])
                if before[g] is not None:
                    wait_chunk_read(act, before[g])
                for key in also:
                    wait_filled(act, *key)
                high, view, _ = hi_view(g)
                fn(high, view, ACT.Copy).then_inc(hi_ready, 1)

            def high_resid(n, j):
                wait_emptied(act, "nt", n, j)
                low, high = (ffn_v, ffn_parts[0]) if n == 1 else (featL, featR)
                fn(high[:, 2 * j:2 * j + 2, :], low[:, 2 * j:2 * j + 2, :], ACT.Copy).then_inc(feat_hi, 1)

            def spread(n):
                wait_filled(act, "rb", n)
                empty(fn(inv_rows, bank("rb", n)[:, 0:T], ACT.Copy), "rb", n)

            def high_features():
                for t in range(NT):
                    for h in range(2):
                        wait_emptied(act, "nt", 0, t, h)
                        fn(featR[:, 4 * h:4 * h + 4, t * P:(t + 1) * P],
                           featL[:, 4 * h:4 * h + 4, t * P:(t + 1) * P], ACT.Copy).then_inc(feat_hi, 1)

            ident_lo, ident_hi = CST["ident"]
            nc.scalar.dma_start(cst[:, ident_lo:ident_hi], A["cst"][:, ident_lo:ident_hi]).then_inc(ident_in, 16)
            nc.scalar.dma_start(cols[:], A["cols"]).then_inc(ident_in, 16)
            act.wait_ge(eps_ready, 3)
            squares(0, lambda t: act.wait_ge(x_in[t], 16))
            high_part(0)
            high_features()
            high_part(1)
            nc.scalar.dma_start(t5b[:], A["t5"]).then_inc(t5_in, 16)
            nc.scalar.dma_start(onehot, A["onehot"]).then_inc(t5_in, 16)
            nc.scalar.dma_start(cst[:, ident_hi:], A["cst"][:, ident_hi:]).then_inc(params_in, 16)
            nc.scalar.dma_start(rows[:], A["rows"].to_broadcast([P, ROWS["end"]])).then_inc(params_in, 16)
            nc.scalar.dma_start(rpb_copies, rpb.unsqueeze(1).to_broadcast([8, GRID_W, RPB])).then_inc(rpb_copied, 16)
            nc.scalar.dma_start(lora[:], A["lora"]).then_inc(params_in, 16)
            nc.scalar.dma_start(gup[:], A["gup"]).then_inc(params_in, 16)
            nc.scalar.dma_start(wr[:], A["wr"].rearrange("(k p) n -> p k n", p=P)).then_inc(params_in, 16)
            high_part(2)
            high_part(3)
            dsts = {"qa": qaT, "ka": kaT, "qb": qbT, "kb": kbT}

            def qk_moved(*names):
                for name in names:
                    nk = 2 if name == "kb" else 4
                    for t in range(NT):
                        wait_filled(act, "qkT", name, t)
                        empty(fn(dsts[name][:, :, t * P:(t + 1) * P],
                                 bank("qkT", name, t)[:, 0:nk * P].rearrange("p (k q) -> p k q", k=nk),
                                 ACT.Copy, scale=colp(name)), "qkT", name, t)

            act.wait_ge(ident_in, 32)
            for n in range(9):
                u, c = n // 2, n % 2
                if n == 8:
                    qk_moved("qa", "ka")
                wait_filled(act, "p1", u, c)
                if n + 4 < 9:
                    high_part(n + 4)
                elif n == 8:
                    high_part(9)
                lo = 512 * u + 256 * c
                empty(fn(nat[:, :, lo:lo + 256], bank("p1", u, c).rearrange("p (t n) -> p t n", t=NT), ACT.Copy), "p1", u, c)
                if n == 5:
                    wait_filled(act, "t5")
                    empty(fn(tb_sb, bank("t5")[0:8, 0:REL], ACT.Copy), "t5")
                if n == 5:
                    root(*QK_SUMS[0], HD, 0)
            def high_moved(*key):
                h, t = key[1:] if key[0] == "oT" else (key[2], key[1])
                wait_filled(act, *key)
                fn(featR[:, 4 * h:4 * h + 4, t * P:(t + 1) * P],
                   bank(*key).rearrange("p (k q) -> p k q", k=4), ACT.Copy).then_inc(feat_hi, 1)

            def gates(br):
                g = sig[:, :, 1024 * br:1024 * br + 1024]
                fn(g, g, ACT.Sigmoid).then_inc(gates_ready, 1)

            first = {n: chunk_of[n, 0] for n in (("p1", 5), ("br", 0), ("wo", 0), ("ffn", 0), ("down", 0), ("rw", 3), ("p2", 0),
                                              ("wo2", 0))}
            root(*QK_SUMS[1], HD, 0)
            for i in range(9):
                if i >= 1:
                    wait_filled(act, "PT", i - 1, 0)
                    empty(fn(probT[:, 2 * ((i - 1) % 2)].rearrange("p a k q -> p (a k q)"), bank("PT", i - 1, 0), ACT.Copy),
                          "PT", i - 1, 0)
                if i == 0:
                    qk_moved("qb", "kb")
                if i < 8:
                    for par in range(2):
                        act.wait_ge(max_ready, 2 * i + par + 1)
                        for pair in range(2):
                            k = 4 * i + 2 * par + pair
                            pr = prob[:, i % 2, par, pair, :]
                            ins = fn(pr, pr, ACT.Exp, bias=negmax[:, k:k + 1], accum_out=sums[:, k:k + 1])
                            if i >= 4 or pair == 0:
                                a.link(ins)
                        if i >= 4:
                            k = 4 * i + 2 * par
                            ins = fn(esink[:, k:k + 2], esink[:, k:k + 2], ACT.Exp)
                        ins.then_inc(exp_ready, 1)
                    u, c = 5 + i // 2, i % 2
                    if i == 0:
                        high_part(first["p1", 5] + 1)
                    wait_filled(act, "p1", u, c)
                    ins = fn(sig[:, :, 256 * i:256 * i + 256], bank("p1", u, c).rearrange("p (t n) -> p t n", t=NT), ACT.Copy)
                    empty(ins, "p1", u, c)
                    high_part(first["p1", 5] + i + 2)
            for key in ((0, 0), (0, 1), (1, 0)):
                high_moved("oT", *key)
            gates(0)
            high_part(first["br", 0] + 2, ("S", 7, 1))
            high_part(first["br", 0] + 3, ("PT", 7, 1))
            high_moved("oT", 1, 1)
            gates(1)
            for n in range(3):
                high_part(first["wo", 0] + n)
            for h in range(2):
                for t in range(NT):
                    high_moved("yT", t, h)
            high_part(first["wo", 0] + 3)
            high_resid(1, 0)
            high_part(first["ffn", 0])
            high_resid(1, 1)
            high_part(first["ffn", 0] + 1)
            for j in range(2, 4):
                high_resid(1, j)
            squares(1, lambda t: wait_emptied(act, "wo", 1, 1))
            for n in range(2, 4):
                high_part(first["ffn", 0] + n)
            spread(1)
            for u in range(FFK // 2):
                high_part(first["ffn", 0] + 2 * u + 4)
                wait_emptied(act, "gate", u)
                fn(silu_t[:, u % 2, :], silu_t[:, u % 2, :], ACT.Silu).then_inc(silu_done, 1)
                high_part(first["ffn", 0] + 2 * u + 5)
                act.wait_ge(h_scaled, u + 1)
                fn(hT_parts[0][:, 2 * u:2 * u + 2, :], hTl[:, 2 * u:2 * u + 2, :], ACT.Copy).then_inc(hT_hi, 1)
            for g in range(first["down", 0] + 4, first["rw", 3] + 1):
                high_part(g)

            for j in range(4):
                high_resid(2, j)
            high_part(first["rw", 3] + 1)
            squares(2, lambda t: wait_emptied(act, "down", t, 1))
            high_part(first["rw", 3] + 2)
            for n, c in enumerate(RW_ORDER):
                high_part(first["rw", 3] + n + 3)
                if c == 6:
                    spread(2)
                if c == 2:
                    act.wait_ge(lerp_ready, 1)
                    fn(tanh_w[:], fT[0:64, 12, 1:257], ACT.Tanh).then_inc(lora_act, 1)
                    fn(sig_g[:], fT[:, 13, 1:257], ACT.Sigmoid).then_inc(lora_act, 1)
                if c == 3:
                    for name, dst, bias in (("z", sw, "w0"), ("za", sa, "a0")):
                        for h in range(2):
                            wait_filled(act, name, h)
                            b = bank(name, h).rearrange("p (f t) -> p f t", f=2)
                            a.link(fn(dst[:, 2 * h, :], b[:, 0, :], ACT.Sigmoid, bias=colp(bias, 2 * h)))
                            empty(fn(dst[:, 2 * h + 1, :], b[:, 1, :], ACT.Sigmoid, bias=colp(bias, 2 * h + 1)), name, h)
                    act.wait_ge(kk_ready, 1)
                    fn(kk2, kk, ACT.Square).then_inc(kk2_ready, 1)
                if c == 0:
                    for h in range(2):
                        wait_filled(act, "ss", h)
                        empty(fn(kk2[:, 2 * h:2 * h + 2, :].rearrange("p a b -> p (a b)"), bank("ss", h), ACT.Sqrt), "ss", h)
                if c == 1:
                    act.wait_ge(scan_ready, 1)
                    a.link(fn(Einv, Ls, ACT.Exp, scale=DECAY))
                    a.link(fn(Ein, Ls, ACT.Exp, scale=-DECAY))
                    fn(Eex, Le, ACT.Exp, scale=-DECAY).then_inc(decay_ready, 1)

            def ret_move(u, c):
                wait_filled(act, "p2", u, c)
                if 2 * u + c + 3 < 8:
                    high_part(first["p2", 0] + 2 * u + c + 3)
                lo = 512 * u + 256 * c
                b = bank("p2", u, c).rearrange("p (t n) -> p t n", t=NT)
                for t in range(NT):
                    ins = fn(retn[:, t, lo:lo + 256], b[:, t, :], ACT.Silu if u == 3 else ACT.Copy, scale=st[:, 4 + t:5 + t])
                    if t == 0:
                        a.link(ins)
                empty(ins, "p2", u, c)

            for u in range(3):
                for c in range(2):
                    ret_move(u, c)
            for name, dst in (("q", rqT), ("k", rkT)):
                for t in range(NT):
                    wait_filled(act, "rT", name, t)
                    empty(fn(dst[:, :, t * P:(t + 1) * P], bank("rT", name, t).rearrange("p (k q) -> p k q", k=4), ACT.Copy),
                          "rT", name, t)
            ret_move(3, 0)
            for t in range(NT):
                root(48, RET_H, RET_D, 1)
            ret_move(3, 1)
            for w in "ABKV":
                for t in range(NT):
                    wait_filled(act, "natl", w, t)
                    empty(fn(natl[w][:, t, :], bank("natl", w, t), ACT.Copy), "natl", w, t)
            for par in range(2):
                r = slice(64 * par, 64 * par + 64)
                fn(frP[r, par], f_r[r], ACT.Copy).then_inc(padded[1], 1)
            for t in range(NT):
                for par in range(2):
                    wait_filled(act, "mat", "AT", t, par)
                    fn(o32T[:, t, 4 * par:4 * par + 4, :].rearrange("p i q -> p (i q)"), bank("mat", "AT", t, par), ACT.Copy)\
                        .then_inc(at_copied, 1)
            dst = {"P2": P2, "P4": P4, "P8T": P8T, "T16T": TT, "T32T": TT, "TT": TT, "Z1": Z, "Z2": Z}
            for name, who in INVERSE:
                if who == "act":
                    for t in range(NT):
                        for par in range(2):
                            key = ("inv", name, t, par)
                            wait_filled(act, *key)
                            empty(fn(dst[name][:, t, 4 * par:4 * par + 4, :].rearrange("p i q -> p (i q)"), bank(*key),
                                     ACT.Copy), *key)
                if name == "P4":
                    for n in range(2):
                        high_part(first["wo2", 0] + n, ("p2", 3, 1))
                if name == "Z2":
                    for t in range(NT):
                        wait_filled(act, "Q", t)
                        empty(fn(Qn[:, t, :], bank("Q", t), ACT.Copy), "Q", t)
                    for t in range(NT):
                        wait_filled(act, "gn", t)
                        empty(fn(gnat[:, t, :], bank("gn", t), ACT.Copy), "gn", t)
            for t in range(NT):
                wait_filled(act, "WT", t)
                empty(fn(WT[:, :, t * P:(t + 1) * P], bank("WT", t).rearrange("p (i q) -> p i q", i=4), ACT.Copy), "WT", t)
            for c in range(NCH):
                r = slice(64 * (c % 2), 64 * (c % 2) + 64)
                wait_filled(act, "U", c, 1)
                empty(fn(Un[r, c // 2, 1, :], bank("U", c, 1)[r, 0:256], ACT.Copy), "U", c, 1)
                for t, par in Y_AFTER.get(c, ()):
                    wait_filled(act, "Y", t, par)
                    yv = ynat[:, t, :].rearrange("p (i a v) -> p i a v", i=4, a=2)[:, :, par, :]
                    empty(fn(yv, bank("Y", t, par)[:, 0:256].rearrange("p (i v) -> p i v", i=4), ACT.Copy), "Y", t, par)
                    if t and par:
                        high_moved("mT", 0, 0)
                        high_moved("mT", 0, 1)
                        high_moved("mT", 1, 0)
                    if par == 1:
                        root(48, RW_H, 64, 2)
            high_part(first["wo2", 0] + 2, ("Y", 1, 1))
            high_moved("mT", 1, 1)
            high_part(first["wo2", 0] + 3)
            squares(3, lambda t: wait_emptied(act, "wo2", 1, 1))
            for t in range(NT):
                wait_emptied(act, "logit", t)
                fn(xn[:, t, :], x[:, t, :], ACT.Copy, scale=st[:, 6 + t:7 + t]).then_inc(xn_ready, 1)
            act.wait_ge(group_ready, 1)
            for t in range(NT):
                fn(e4[:, t, :], e4[:, t, :], ACT.Exp, accum_out=gp[:, t:t + 1]).then_inc(exp_ready, 1)
            act.wait_ge(e2_ready, 1)
            fn(e2, e2, ACT.Exp).then_inc(exp_ready, 1)

            def moe_group(r, pair, gp):
                n = r * NG + pair * 2 + gp
                base = r * (4 * ALLQ) + pair * 48 + gp * 24
                act.wait_ge(pieces_read, base + 8)
                fn(sg, psum[:, MB[4], :], ACT.Silu).then_inc(silu_ready, 1)
                act.wait_ge(hT_filled, n + 1)
                fn(hhT.rearrange("p k s -> p (k s)"), psum[:, MB[7], :], ACT.Copy).then_inc(hT_ready, 1)
                act.wait_ge(pieces_read, base + 20)
                fn(dd[:, 0, :], psum[:, MB[4], :], ACT.Copy).then_inc(d0_ready, 1)

            def moe_round(r):
                with act.Fori(0, NG // 2) as pair:
                    for gp in range(2):
                        moe_group(r, pair, gp)

            act.wait_ge(count_ready, 1)
            moe_round(0)
            most = act.value_load(cnt[0:1, 0:1], min_val=0, max_val=T)
            with act.If(most > CAP):
                with act.Fori(1, ROUNDS) as r:
                    with act.If(most > r * CAP):
                        moe_round(r)
            squares(4, lambda t: act.wait_ge(resid_done[t], 2))

        @block.vector
        def _(dve):
            v = Steps(dve, dve_step)
            link = v.link
            empty = lambda ins, *key: v.empty("dve", ins, *key)
            tt, ts, stt = nc.vector.tensor_tensor, nc.vector.tensor_scalar, nc.vector.scalar_tensor_tensor
            red = nc.vector.tensor_reduce

            roots = [0]

            def root(ins, ap, meanwhile=None):
                ins.then_inc(var_ready, 1)
                roots[0] += 1
                if meanwhile:
                    meanwhile()
                dve.wait_ge(root_ready, roots[0])
                link(nc.vector.reciprocal(ap, ap))

            def inverse(n, t):
                dve.wait_ge(rms_ready, NT * n + t + 1)
                s = st[:, 2 * n + t:2 * n + t + 1]
                link(nc.vector.reciprocal(s, s))
                return s

            def norm():
                for t in range(NT):
                    ts(xn[:, t, :], x[:, t, :], inverse(0, t), None, ALU.mult).then_inc(xn_ready, 1)

            def diagonals(n):
                for t in range(NT):
                    ins = ts(diag[:, t, :], ident, inverse(n, t), None, ALU.mult)
                    if t == 0:
                        link(ins)
                ins.then_inc(diag_ready, 1)

            def resid_gain(n, j):
                wait_filled(dve, "nt", n, j)
                v_ = (None, ffn_v, featL, router_in)[n][:, 2 * j:2 * j + 2, :]
                empty(tt(v_, bank("nt", n, j).rearrange("p (k q) -> p k q", k=2), bc(colp(f"norm{n}")[:, 2 * j:2 * j + 2], T),
                         ALU.mult), "nt", n, j)

            def resid_low(n, j):
                highs[0] += 1
                dve.wait_ge(feat_hi, highs[0])
                v_, high, low = (ffn_v, *ffn_parts) if n == 1 else (featL, featR, featLR)
                cols_ = slice(2 * j, 2 * j + 2)
                tt(low[:, cols_, :], v_[:, cols_, :], high[:, cols_, :].bitcast(F32), ALU.subtract).then_inc(feat_lo, 1)

            highs = [0]

            def norm_T(*weights):
                places = [(t, h) for t in range(NT) for h in range(2)]
                view = lambda f, t, h: f[:, 4 * h:4 * h + 4, t * P:(t + 1) * P]
                for t, h in places:
                    wait_filled(dve, "nt", 0, t, h)
                    gain = bc(colp("norm0")[:, 4 * h:4 * h + 4], P)
                    empty(tt(view(featL, t, h), bank("nt", 0, t, h).rearrange("p (k q) -> p k q", k=4), gain, ALU.mult),
                          "nt", 0, t, h)
                for g in weights:
                    low_part(dve, tt, g)
                for t, h in places:
                    highs[0] += 1
                    dve.wait_ge(feat_hi, highs[0])
                    tt(view(featLR, t, h), view(featL, t, h), view(featR, t, h).bitcast(F32), ALU.subtract).then_inc(feat_lo, 1)

            def low_moved(*key):
                h, t = key[1:] if key[0] == "oT" else (key[2], key[1])
                highs[0] += 1
                dve.wait_ge(feat_hi, highs[0])
                empty(tt(featLR[:, 4 * h:4 * h + 4, t * P:(t + 1) * P], bank(*key).rearrange("p (k q) -> p k q", k=4),
                         featR[:, 4 * h:4 * h + 4, t * P:(t + 1) * P].bitcast(F32), ALU.subtract), *key)

            for k, e in enumerate((EPS, 1e-5, 64e-5)):
                nc.vector.memset(eps_col[:, k:k + 1], e).then_inc(eps_ready, 1)
            dve.wait_ge(ident_in, 32)
            norm()
            norm_T(0)
            for g in range(1, 6):
                low_part(dve, tt, g)
            tmp = area(L1, "prob", 4, 512)[:, 0:2, :]
            for units_, (s_lo, s_n), lows in zip((((0, 0, 8), (1, 512, 8)), ((3, 1536, 8), (4, 2048, 2))), QK_SUMS, ((6, 7), ())):
                at = s_lo
                sums_of = []
                for u, lo, H in units_:
                    wait_emptied(dve, "p1", u, 0 if u == 4 else 1)
                    q = nat[:, :, lo:lo + 64 * H]
                    link(tt(tmp[:, :, 0:64 * H], q, q, ALU.mult))
                    s = st[:, at:at + 2 * H].rearrange("p (t h) -> p t h", t=NT)
                    at += 2 * H
                    sums_of.append(s)
                    ins = red(s, tmp[:, :, 0:64 * H].rearrange("p t (h d) -> p t h d", h=H), AX, ALU.add)
                    if at < s_lo + s_n:
                        link(ins)
                        for g in lows:
                            low_part(dve, tt, g)
                root(ins, st[:, s_lo:s_lo + s_n])
                for u, lo, H in units_:
                    s_both = sums_of.pop(0)
                    for t in range(NT):
                        s = s_both[:, t]
                        q3 = nat[:, t, lo:lo + 64 * H].rearrange("p (h d) -> p h d", h=H)
                        if u == 4:
                            dst = kdup[:, t].rearrange("p v (c d) -> p v c d", c=2)
                            tt(dst, q3.unsqueeze(2).to_broadcast([P, 2, 2, 64]), bc(bc(s, 2), 64), ALU.mult)                                .then_inc(qk_ready, 1)
                        else:
                            tt(q3, q3, bc(s, 64), ALU.mult).then_inc(qk_ready, 1)
                if lows:
                    low_part(dve, tt, 8)
                    dve.wait_ge(params_in, PARAMS_IN)
                    dve.wait_ge(biasA_in, 16 * 16)
                    flat = biasA.rearrange("p h j k -> p (h j) k")
                    link(tt(flat, flat, con("winm").unsqueeze(1).to_broadcast([P, 48, 64]), ALU.mult))
                    link(tt(flat, flat, con("wina").unsqueeze(1).to_broadcast([P, 48, 64]), ALU.add))
            low_part(dve, tt, chunk_of[("p1", 5), 0])

            def softmax_in(i):
                br, t, g = i // 4, i // 2 % 2, i % 2
                for par in range(2):
                    wait_filled(dve, "S", i, par)
                    if i >= 2:
                        wait_filled(dve, "PT", i - 2, par)
                    if br:
                        b = biasB[:, 4 * g + par:4 * g + par + 3:2, P - P * t:P - P * t + T]
                    else:
                        b = biasA[:, 4 * g + par:4 * g + par + 3:2, 2 - 2 * t:6 - 2 * t, :].rearrange("p h j k -> p h (j k)")
                    pr = prob[:, i % 2, par]
                    empty(stt(pr, bank("S", i, par).rearrange("p (a k) -> p a k", a=2), HD ** -0.5, b, ALU.mult, ALU.add),
                          "S", i, par)
                    k = 4 * i + 2 * par
                    m = negmax[:, k:k + 2]
                    link(red(m, pr, AX, ALU.max))
                    if br:
                        sk = row("sink")[:, 4 * g + par:4 * g + par + 3:2]
                        link(tt(m, m, sk, ALU.max))
                        link(tt(esink[:, k:k + 2], sk, m, ALU.subtract))
                    ts(m, m, -1.0, None, ALU.mult).then_inc(max_ready, 1)

            def weighted(i):
                br, t, g = i // 4, i // 2 % 2, i % 2
                wait_filled(dve, "PT", i, 1)
                empty(nc.vector.tensor_copy(probT[:, 2 * (i % 2) + 1].rearrange("p a k q -> p (a k q)"), bank("PT", i, 1)),
                      "PT", i, 1)
                if i == 7:
                    for key in ((0, 0), (0, 1), (1, 0)):
                        low_moved("oT", *key)
                s = sums[:, 4 * i:4 * i + 4]
                dve.wait_ge(exp_ready, 2 * i + 2)
                if br:
                    link(tt(s, s, esink[:, 4 * i:4 * i + 4], ALU.add))
                link(nc.vector.reciprocal(s, s))
                wait_filled(dve, "PV", i)
                dst = xn[:, t, 512 * br + 256 * g:512 * br + 256 * g + 256].rearrange("p (a b d) -> p a b d", a=2, b=2)
                empty(tt(dst, bank("PV", i)[:, 0:256].rearrange("p (a b d) -> p a b d", a=2, b=2),
                         bc(s.rearrange("p (b a) -> p a b", b=2), 64), ALU.mult), "PV", i)

            for i in range(9):
                if i == 4:
                    dve.wait_ge(biasB_in, 16)
                if i < 8:
                    softmax_in(i)
                if i == 0:
                    low_part(dve, tt, chunk_of[("p1", 5), 1])
                if i >= 1:
                    weighted(i - 1)
            for br in range(2):
                if br == 1:
                    low_moved("oT", 1, 1)
                for n in range(2):
                    for t in range(NT):
                        wait_filled(dve, "br", br, n, t)
                        dve.wait_ge(gates_ready, br + 1)
                        g = sig[:, t, 1024 * br + 512 * n:1024 * br + 512 * n + 512]
                        empty(tt(g, g, bank("br", br, n, t), ALU.mult), "br", br, n, t)
                        if br:
                            ya = sig[:, t, 512 * n:512 * n + 512]
                            tt(ya, ya, g, ALU.add).then_inc(y_ready, 1)
            for h in range(2):
                for t in range(NT):
                    low_moved("yT", t, h)

            first = {n: chunk_of[n, 0] for n in (("ffn", 0), ("down", 0), ("rw", 3))}
            for n in range(4):
                wait_filled(dve, "wo", n // 2, n % 2)
                xs = x[:, :, 256 * n:256 * n + 256]
                empty(tt(xs, xs, bank("wo", n // 2, n % 2).rearrange("p (t n) -> p t n", t=NT), ALU.add), "wo", n // 2, n % 2)
                if n >= 2:
                    resid_low(1, n - 2)
                if n:
                    resid_gain(1, n - 1)
            resid_gain(1, 3)
            for j in range(2, 4):
                resid_low(1, j)
            diagonals(1)
            rows2 = inv_rows.unsqueeze(1).to_broadcast([P, 2, T])
            wait_emptied(dve, "rb", 1)
            for u in range(FFK // 2):
                wait_filled(dve, "gate", u)
                empty(tt(silu_t[:, u % 2, :].rearrange("p (f t) -> p f t", f=2), bank("gate", u).rearrange("p (f t) -> p f t", f=2),
                         rows2, ALU.mult), "gate", u)
                low_part(dve, tt, first["ffn", 0] + 2 * u + 4)
                wait_filled(dve, "up", u)
                dve.wait_ge(silu_done, u + 1)
                h = hTl[:, 2 * u:2 * u + 2, :]
                empty(tt(h.rearrange("p f t -> p (f t)"), silu_t[:, u % 2, :], bank("up", u), ALU.mult), "up", u)
                tt(h, h, rows2, ALU.mult).then_inc(h_scaled, 1)
                low_part(dve, tt, first["ffn", 0] + 2 * u + 5)
                dve.wait_ge(hT_hi, u + 1)
                tt(hT_parts[1][:, 2 * u:2 * u + 2, :], h, hT_parts[0][:, 2 * u:2 * u + 2, :].bitcast(F32), ALU.subtract).then_inc(hT_lo, 1)
            for g in range(first["down", 0] + 4, first["rw", 3] + 1):
                low_part(dve, tt, g)
            for n in range(2):
                for t in range(NT):
                    wait_filled(dve, "down", t, n)
                    xs = x[:, t, 512 * n:512 * n + 512]
                    empty(tt(xs, xs, bank("down", t, n), ALU.add), "down", t, n)

            for j in range(4):
                resid_gain(2, j)
            for j in range(4):
                resid_low(2, j)
            low_part(dve, tt, first["rw", 3] + 1)
            link(nc.vector.memset(fT[:, :, 0:1], 0.0))
            diagonals(2)
            wait_emptied(dve, "rb", 2)

            def rw_move(c):
                wait_filled(dve, "rw", c)
                empty(tt(fT[:, 2 * c:2 * c + 2, 1:257], bank("rw", c).rearrange("p (f t) -> p f t", f=2), rows2, ALU.mult), "rw", c)

            def lerp(c0, n, diff=dtmp):
                cur = fT[:, c0:c0 + n, 1:257]
                link(tt(diff[:, 0:n, :], fT[:, c0:c0 + n, 0:256], cur, ALU.subtract))
                for c in range(n):
                    link(stt(fT[:, c0 + c, 1:257], diff[:, c, :], colp("mu", c0 + c), fT[:, c0 + c, 1:257],
                             ALU.mult, ALU.add))

            def percol(name):
                return bc(colp(name), T)

            rw_move(6)
            lerp(12, 2)
            dve.sem_inc(lerp_ready, 1)
            rw_move(2)
            rw_move(3)
            lerp(4, 4)
            tt(kk, f_k, percol("k_k"), ALU.mult).then_inc(kk_ready, 1)
            wait_emptied(dve, "z", 1)
            for c in range(4):
                link(nc.vector.tensor_tensor_scan(Ls[:, c, :], con("reset"), sw[:, c, :], 0.0, ALU.mult, ALU.add))
            tt(Le, Ls, sw, ALU.subtract).then_inc(scan_ready, 1)
            rw_move(0)
            wait_emptied(dve, "za", 1)
            for c in range(4):
                link(ts(dtmp[:, c, :], sa[:, c, :], 1.0, colp("k_a", c), ALU.subtract, ALU.mult))
            wait_emptied(dve, "ss", 1)
            link(ts(kk2, kk2, 1e-12, None, ALU.max))
            link(nc.vector.reciprocal(kk2, kk2))
            link(tt(kk, kk, kk2, ALU.mult))
            link(stt(kp, dtmp, 1.0, f_k, ALU.add, ALU.mult))
            link(tt(sa, kk, sa, ALU.mult))
            rw_move(1)
            lerp(0, 4)
            link(tt(rk, f_r, kp, ALU.mult))
            link(tt(rk, rk, percol("r_k"), ALU.mult))
            dve.wait_ge(decay_ready, 1)
            link(nc.vector.tensor_copy(PC[:], Ein.rearrange("p f (c s) -> p f c s", c=NCH)[:, :, :, CH - 1]))
            link(stt(At, kk, -1.0, Eex, ALU.mult, ALU.mult))
            link(tt(Bt, sa, Einv, ALU.mult))
            link(tt(f_k, kp, Einv, ALU.mult))
            link(tt(f_r, f_r, Ein, ALU.mult))
            for dst, src in ((BhT, Bt), (KhT, f_k)):
                for c in range(4):
                    ins = tt(dst[:, c, :].rearrange("p (c s) -> p c s", c=NCH), src[:, c, :].rearrange("p (c s) -> p c s", c=NCH),
                             bc(PC[:, c, :], CH), ALU.mult)
                    link(ins)
            rw_move(4)
            rw_move(5)
            lerp(8, 4, kk)
            dve.sem_inc(rw_ready, 1)
            for t in range(NT):
                wait_emptied(dve, "p2", 1, 1)
                xy = retn[:, t, 0:1024].rearrange("p (h c d) -> p h c d", h=8, c=2)
                x1, x2 = xy[:, :, 0, :], xy[:, :, 1, :]
                w4 = xn[:].rearrange("p t (a h d) -> p (t a) h d", a=2, h=8)
                cos = con("cos")[:, 64 * t:64 * t + 64].unsqueeze(1).to_broadcast([P, 8, 64])
                sin = con("sin")[:, 64 * t:64 * t + 64].unsqueeze(1).to_broadcast([P, 8, 64])
                link(tt(w4[:, 0], x1, cos, ALU.mult))
                link(tt(w4[:, 1], x2, sin, ALU.mult))
                link(tt(w4[:, 2], x1, sin, ALU.mult))
                link(tt(w4[:, 3], x2, cos, ALU.mult))
                link(tt(x1, w4[:, 0], w4[:, 1], ALU.subtract))
                tt(x2, w4[:, 2], w4[:, 3], ALU.add).then_inc(rot_ready, 1)
            for j in range(3):
                wait_filled(dve, "rs", j)
                dst = (rsc[0][:, 2 * j:2 * j + 2, :] if j < 2 else rsc[1]).rearrange("p a b -> p (a b)")
                lo = CST["dec"][0] + 512 * j
                empty(tt(dst, bank("rs", j), cst[:, lo:lo + 512], ALU.mult), "rs", j)

            def head_norm(y, work, H, src, emptied_key, after_mean=None, at_root=None):
                d = 512 // H
                per = lambda ap: ap.rearrange("p (h d) -> p h d", h=H)
                s = st[:, 32:32 + H]
                q = st[:, 48:48 + H]
                link(red(s, per(src), AX, ALU.add))
                link(ts(s, s, 1.0 / d, None, ALU.mult))
                if after_mean:
                    after_mean()
                ins = tt(per(y), per(src), bc(s, d), ALU.subtract)
                if emptied_key:
                    empty(ins, *emptied_key)
                else:
                    link(ins)
                link(tt(work, y, y, ALU.mult))
                root(red(q, per(work), AX, ALU.add), q, at_root)
                link(tt(per(y), per(y), bc(q, d), ALU.mult))

            dve.wait_ge(rot_ready, NT)
            for t in range(NT):
                wait_filled(dve, "ro", t)
                y = xn[:, t, 0:512]
                head_norm(y, xn[:, t, 512:1024], RET_H, bank("ro", t), ("ro", t))
                link(tt(y, y, row("ret_gn"), ALU.mult))
            wait_filled(dve, "p2", 3, 1)
            for par in range(2):
                r = slice(64 * par, 64 * par + 64)
                nc.vector.tensor_copy(AtP[r, par], At[r]).then_inc(padded[0], 1)
            wait_emptied(dve, "p2", 3, 1)
            for t in range(NT):
                y = xn[:, t, 0:512]
                tt(y, y, retn[:, t, 1536:2048], ALU.mult).then_inc(mixed_ready, 1)
            wait_filled(dve, "bonus")
            empty(nc.vector.tensor_copy(bonus, bank("bonus")[:, 0:16]), "bonus")

            def masked(dst, name, m, t, par, last):
                mask = con(m).unsqueeze(1).to_broadcast([P, 4, P])
                ins = tt(dst[:, t, 4 * par:4 * par + 4, :], bank("mat", name, t, par).rearrange("p (i q) -> p i q", i=4),
                         mask, ALU.mult)
                if last:
                    empty(ins, "mat", name, t, par)

            def mat(name, *outs):
                for t in range(NT):
                    for par in range(2):
                        wait_filled(dve, "mat", name, t, par)
                        for n, (dst, m) in enumerate(outs):
                            masked(dst, name, m, t, par, n == len(outs) - 1)

            dve.wait_ge(mixed_ready, NT)
            for t in range(NT):
                for par in range(2):
                    dve.wait_ge(at_copied, 2 * t + par + 1)
                    masked(AdT, "AT", "mAdT", t, par, True)
            for t in range(NT):
                for par in range(2):
                    wait_filled(dve, "mat", "A", t, par)
                    masked(Ad, "A", "mAd", t, par, True)
                    hs = slice(4 * par, 4 * par + 4)
                    tt(X[:, t, hs, :], Ad[:, t, hs, :], ident.unsqueeze(1).to_broadcast([P, 4, P]), ALU.add)\
                        .then_inc(x0_ready, 1)
            dst = {"P2T": P2T, "P4T": P4T}
            extra = {"Aak": (AakT, "mlt"), "Arb": (ArbT, "mle"), "Ark": (ArkT, "mle")}
            for name, who in INVERSE:
                if who == "dve":
                    for t in range(NT):
                        for par in range(2):
                            key = ("inv", name, t, par)
                            wait_filled(dve, *key)
                            hs = slice(4 * par, 4 * par + 4)
                            flat = lambda m: m[:, t, hs, :].rearrange("p i q -> p (i q)")
                            if name in dst:
                                empty(nc.vector.tensor_copy(flat(dst[name]), bank(*key)), *key)
                            else:
                                dve.wait_ge(x0_ready, 2 * t + par + 1)
                                empty(tt(flat(X), flat(X), bank(*key), ALU.add), *key)
                if name == "X2":
                    for n in range(2):
                        low_part(dve, tt, chunk_of[("wo2", 0), n])
                for e in INV_EXTRA.get(name, ()):
                    mat(e, extra[e])
            for c in range(NCH):
                r = slice(64 * (c % 2), 64 * (c % 2) + 64)
                if c in (1, 2):
                    t, g = c - 1, gnat[:, c - 1, :]
                    per = lambda ap: ap.rearrange("p (h d) -> p h d", h=RW_H)
                    wait_emptied(dve, "gn", t)
                    link(tt(per(bonus_v[:, t, :]), per(natl["V"][:, t, :]), bc(bonus[:, 8 * t:8 * t + 8], 64), ALU.mult))
                    link(tt(bonus_v[:, t, :], bonus_v[:, t, :], g, ALU.mult))
                    link(tt(g, g, row("rw_gn"), ALU.mult))
                wait_filled(dve, "U", c, 0)
                empty(nc.vector.tensor_copy(Un[r, c // 2, 0, :], bank("U", c, 0)[r, 0:256]), "U", c, 0)
                if c < NCH - 1:
                    if c:
                        link(tt(S[:, c + 1], S[:, c], bc(PC[:, :, c], 64), ALU.mult))
                    wait_filled(dve, "St", c)
                    b = bank("St", c)[:, 0:256].rearrange("p (i v) -> p i v", v=64)
                    if c == 0:
                        empty(nc.vector.tensor_copy(S[:, 1], b), "St", 0)
                    else:
                        empty(tt(S[:, c + 1], S[:, c + 1], b, ALU.add), "St", c)
            def first_lows():
                low_moved("mT", 0, 0)
                low_moved("mT", 0, 1)

            for t in range(NT):
                for par in range(2):
                    wait_emptied(dve, "Y", t, par)
                y, w = ynat[:, t, :], ytmp[:, t, :]
                head_norm(y, w, RW_H, y, None, *((first_lows, lambda: low_moved("mT", 1, 0)) if t else ()))
                link(tt(y, y, gnat[:, t, :], ALU.mult))
                tt(xn[:, t, 512:1024], y, bonus_v[:, t, :], ALU.add).then_inc(mixed_ready, 1)
            low_moved("mT", 1, 1)
            low_part(dve, tt, chunk_of[("wo2", 1), 0])
            for n in range(4):
                wait_filled(dve, "wo2", n // 2, n % 2)
                xs = x[:, :, 256 * n:256 * n + 256]
                empty(tt(xs, xs, bank("wo2", n // 2, n % 2).rearrange("p (t n) -> p t n", t=NT), ALU.add), "wo2", n // 2, n % 2)
                if n:
                    resid_gain(3, n - 1)
                if n == 0:
                    low_part(dve, tt, chunk_of[("wo2", 1), 1])
            resid_gain(3, 3)
            flat5 = lambda m: m.rearrange("p t g e -> p (t g) e")
            link(nc.vector.memset(lg[:, :, 0, 0:4], NEG))
            for t in range(NT):
                s = inverse(3, t)
                wait_filled(dve, "logit", t)
                o = lg[:, t].rearrange("p g e -> p (g e)")[:, 4:40]
                empty(stt(o, bank("logit", t)[:, 0:36], s, row("brt"), ALU.mult, ALU.add), "logit", t)

            def first_max(dst, mx, then=None):
                link(red(mx, flat5(lg), AX, ALU.max))
                link(tt(flat5(dst), flat5(lg), bc(mx, 8), ALU.is_equal))
                if then:
                    then()
                link(tt(flat5(dst), flat5(dst), con("desc").unsqueeze(1).to_broadcast([P, NT * 5, 8]), ALU.mult))
                link(red(cm, flat5(dst), AX, ALU.max))
                link(tt(flat5(dst), flat5(dst), bc(cm, 8), ALU.is_equal))

            by5 = lambda m: m.rearrange("p (t g) -> p t g", t=NT)
            by_group = lambda m: m.rearrange("p t (g e) -> p t g e", g=4)
            first_max(one1, m1, lambda: tt(e4, lg[:, :, 0, 4:8], by5(m1)[:, :, 0:1].to_broadcast([P, NT, 4]), ALU.subtract)
                      .then_inc(group_ready, 1))
            chosen = one1[:, :, 0, 4:8]
            link(stt(flat5(lg), flat5(one1), 3 * NEG, flat5(lg), ALU.mult, ALU.add))
            first_max(one2, m2, lambda: tt(by_group(oh1), one1[:, :, 1:5], bc(chosen, 8), ALU.mult).then_inc(oh1_ready, 1))
            link(tt(by_group(oh2), one2[:, :, 1:5], bc(chosen, 8), ALU.mult))
            dve.wait_ge(oh1_ready, 1)
            tt(selr, oh1, oh2, ALU.add).then_inc(route_ready, 1)
            link(tt(m2, m2, m1, ALU.subtract))
            m2g = by5(m2)[:, :, 1:5]
            link(tt(m2g, m2g, chosen, ALU.mult))
            red(e2, m2g, AX, ALU.add).then_inc(e2_ready, 1)
            wait_filled(dve, "count")
            empty(red(rt[:, 606:607], bank("count")[:, 0:E], AX, ALU.max), "count")
            dve.wait_ge(exp_ready, 16 + NT + 1)
            link(stt(w1, e2, 1.0, gp, ALU.add, ALU.mult))
            nc.vector.reciprocal(w1, w1).then_inc(share_ready, 1)
            for t in range(NT):
                wait_filled(dve, "rank", t)
                if t == 0:
                    dve.wait_ge(route_ready, 1)
                empty(stt(rank[:, t, :], bank("rank", t)[:, 0:E], CHOSEN, selr[:, t, :], ALU.add, ALU.mult), "rank", t)
            nc.vector.tensor_copy(cnt[:, 0:1], rt[:, 606:607]).then_inc(count_ready, 1)

            def moe_group(r, pair, gp_):
                n = r * NG + pair * 2 + gp_
                base = r * (4 * ALLQ) + pair * 48 + gp_ * 24
                e0 = pair * (2 * EG) + gp_ * EG
                es = slice(e0, e0 + EG) if isinstance(e0, int) else bass.ds(e0, EG)
                slots = con("slot").unsqueeze(1).unsqueeze(1).to_broadcast([P, NT, EG, CAP])
                tt(G, slots, rank[:, :, es].unsqueeze(3).to_broadcast([P, NT, EG, CAP]), ALU.is_equal).then_inc(onehot_ready, 1)
                for kb in range(2):
                    dve.wait_ge(gathered, 2 * n + kb + 1)
                    gain = bc(colp("norm3")[:, 4 * kb:4 * kb + 4], P)
                    tt(xg[:, 4 * kb:4 * kb + 4, :], psum[:, MB[6 + kb], :].rearrange("p (k s) -> p k s", k=4), gain, ALU.mult)\
                        .then_inc(xg_ready, 1)
                dve.wait_ge(onehot_ready, n + 1)
                dve.wait_ge(comb_ready, 1)
                tt(Gw, G, comb[:, :, es].unsqueeze(3).to_broadcast([P, NT, EG, CAP]), ALU.mult).then_inc(shares_ready, 1)
                dve.wait_ge(pieces_read, base + 16)
                dve.wait_ge(silu_ready, n + 1)
                tt(hh, sg, psum[:, MB[5], :], ALU.mult).then_inc(h_ready, 1)
                dve.wait_ge(gt_filled, n + 1)
                dve.wait_ge(scattered, 4 * (n + 1))
                nc.vector.tensor_copy(GT.rearrange("p t q -> p (t q)"), psum[:, MB[6], 0:2 * P]).then_inc(gt_ready, 1)
                dve.wait_ge(pieces_read, base + 24)
                nc.vector.tensor_copy(dd[:, 1, :], psum[:, MB[5], :]).then_inc(d1_ready, 1)

            def moe_round(r):
                with dve.Fori(0, NG // 2) as pair:
                    for g in range(2):
                        moe_group(r, pair, g)

            dve.wait_ge(gt_ready, 1)
            moe_round(0)
            dve.wait_ge(count_ready, 1)
            most = dve.value_load(cnt[0:1, 0:1], min_val=0, max_val=T)
            with dve.If(most > CAP):
                with dve.Fori(1, ROUNDS) as r:
                    with dve.If(most > r * CAP):
                        ts(rank, rank, -float(CAP), None, ALU.add).then_inc(shifted, 1)
                        dve.wait_ge(shifted, r)
                        nc.vector.memset(rt[:, 607:608], 0.0)
                        moe_round(r)
                        dve.wait_ge(scattered, r * (4 * NG) + (4 + 4 * NG))
                        nc.vector.memset(rt[:, 608:609], 0.0)
            for n in range(2):
                for t in range(NT):
                    dve.wait_ge(scattered, 4 * NG + (2 * n + t + 1))
                    xs = x[:, t, 512 * n:512 * n + 512]
                    tt(xs, xs, psum[:, MB[2 * t + n], :], ALU.add).then_inc(resid_done[t], 1)
            dve.wait_ge(gain_in, 16)
            for t in range(NT):
                dve.wait_ge(rms_ready, NT * 4 + t + 1)
                s = st[:, 8 + t:9 + t]
                nc.vector.reciprocal(s, s).then_inc(factor_ready, 1)
                dve.wait_ge(factor_ready, t + 1)
                gain = featT[:, 0:4, :].rearrange("p a b -> p (a b)")
                for n in range(2):
                    cols_ = slice(512 * n, 512 * n + 512)
                    stt(xn[:, t, cols_], x[:, t, cols_], s, gain[:, cols_], ALU.mult, ALU.mult).then_inc(out_ready, 1)


def kernel(**inputs):
    import concourse.bacc as _bacc
    from concourse.bass_utils import run_bass_kernel_spmd as _run

    g = {k: np.asarray(v) for k, v in inputs.items()}
    pk = lambda a: np.ascontiguousarray(a.reshape(-1, P).T)
    two = lambda a: np.concatenate([a[0], a[0]])[:, None]
    arrays = {
        "x": g["x"][0],
        "cst": constants(),
        "onehot": t5_one_hot(),
        "cols": np.concatenate([
            pk(g["norm_mix"][0]), pk(g["norm_ffn"][0]), pk(g["norm1_gain_2"][0]), pk(g["norm2_gain_2"][0]),
            two(g["q_norm_a"]), two(g["k_norm_a"]), two(g["q_norm_b"]), two(g["k_norm_b"]),
            pk(g["rwkv_mu_2"][0]), pk(g["rwkv_w0_2"][0]), pk(g["rwkv_a0_2"][0]), pk(g["rwkv_k_k_2"][0]),
            pk(g["rwkv_k_a_2"][0]), pk(g["rwkv_r_k_2"][0].reshape(-1))], 1),
        "rows": np.concatenate([g["sink_b"][0], g["b_route_group_2"][0], g["b_route_expert_2"][0],
                                g["ret_gn_gain_2"][0], g["rwkv_gn_gain_2"][0]])[None, :],
        "final_gain": g["final_norm_gain_2"][None, :],
        "rpb": g["rpb_a"][0].transpose(2, 0, 1).reshape(8, -1),
        "t5": np.concatenate([g["t5_table"], np.ones((1, 8), np.float32)]),
        "lora": np.concatenate([g["rwkv_w_up_2"][0], g["rwkv_a_up_2"][0]]),
        "gup": g["rwkv_g_up_2"][0],
        "wr": np.concatenate([g["w_route_group_2"][0], g["w_route_expert_2"][0]], 1),
    }
    for name in ("w_in", "w_branch_a", "w_branch_b", "w_out", "w_gate", "w_up", "w_down", "w_in_2", "w_out_2",
                 "w_gate_2", "w_up_2", "w_down_2"):
        arrays[name] = g[name][0]
    arrays = {k: np.ascontiguousarray(a) for k, a in arrays.items()}
    nc = _bacc.Bacc("TRN2", target_bir_lowering=False, num_devices=1)
    A = {k: nc.dram_tensor(f"in_{k}", a.shape, F32, kind="ExternalInput").ap() for k, a in arrays.items()}
    out = nc.dram_tensor("out", (T, D), F32, kind="ExternalOutput").ap()
    build(nc, A, out)
    r = _run(nc, [{f"in_{k}": a for k, a in arrays.items()}], core_ids=[0])
    return r.results[0]["out"].reshape(1, T, D)
```
